# Optimizing a Trainium2 kernel written in Bass

```python
import math
import jax, jax.numpy as jnp
from jax import lax
import numpy as np
import jax
import jax.numpy as jnp

D_MODEL = 1024
BATCH = 1
SEQ = 256
DEPTH = 2

D_MIX = D_MODEL
HEAD_DIM = 64
DIFF_HEADS = D_MIX // 256
DIFF_QK_DIM = HEAD_DIM
DIFF_V_DIM = 2 * HEAD_DIM
DSA_HEADS = D_MIX // 256
DSA_DIM = HEAD_DIM
IDX_HEADS = D_MIX // 128
IDX_DIM = HEAD_DIM
FOX_HEADS = D_MIX // 256
FOX_DIM = HEAD_DIM
DIFF_WIDTH = DIFF_HEADS * DIFF_V_DIM
DSA_WIDTH = DSA_HEADS * DSA_DIM
FOX_WIDTH = FOX_HEADS * FOX_DIM
DSA_TOPK_MAX = 256
Q_BLOCK = 128
ROPE_THETA = 10000.0
LN_EPS = 1e-5
SUBLN_EPS = 1e-5
NEG_INF = -1e30
DEEPNORM_ALPHA = (2 * DEPTH) ** 0.25
DEEPNORM_BETA = (8 * DEPTH) ** -0.25
IDX_WEIGHT_SCALE = (IDX_HEADS * IDX_DIM) ** -0.5

IN_SPLITS = (
    ('diff_q', DIFF_HEADS * 2 * DIFF_QK_DIM),
    ('diff_k', DIFF_HEADS * 2 * DIFF_QK_DIM),
    ('diff_v', DIFF_HEADS * DIFF_V_DIM),
    ('dsa_q', DSA_HEADS * DSA_DIM),
    ('dsa_k', DSA_DIM),
    ('dsa_v', DSA_DIM),
    ('idx_q', IDX_HEADS * IDX_DIM),
    ('idx_k', IDX_DIM),
    ('idx_w', IDX_HEADS),
    ('fox_q', FOX_HEADS * FOX_DIM),
    ('fox_k', FOX_HEADS * FOX_DIM),
    ('fox_v', FOX_HEADS * FOX_DIM),
    ('fox_f', FOX_HEADS),
    ('gate', D_MIX),
)
VALUE_COLS = ('diff_v', 'dsa_v', 'fox_v')
IN_WIDTH = sum(n for _, n in IN_SPLITS)


def split_columns(h):
    out, off = [], 0
    for _, n in IN_SPLITS:
        out.append(h[..., off:off + n])
        off += n
    return out

def rope(x, pos):
    d = x.shape[-1]
    inv = ROPE_THETA ** (-jnp.arange(0, d, 2, dtype=jnp.float32) / d)
    ang = pos.astype(jnp.float32)[:, None] * inv[None, :]
    shp = (x.shape[1],) + (1,) * (x.ndim - 3) + (d // 2,)
    cos = jnp.cos(ang).reshape(shp).astype(x.dtype)
    sin = jnp.sin(ang).reshape(shp).astype(x.dtype)
    x1, x2 = x[..., : d // 2], x[..., d // 2:]
    return jnp.concatenate([x1 * cos - x2 * sin, x2 * cos + x1 * sin], axis=-1)

def to_blocks(a):
    B, S = a.shape[:2]
    return jnp.moveaxis(a.reshape((B, S // Q_BLOCK, Q_BLOCK) + a.shape[2:]), 1, 0)

def from_blocks(a):
    nb, B, qb = a.shape[:3]
    return jnp.moveaxis(a, 0, 1).reshape((B, nb * qb) + a.shape[3:])

def layer_norm(x, g, b):
    xf = x.astype(jnp.float32)
    mu = jnp.mean(xf, axis=-1, keepdims=True)
    var = jnp.mean(jnp.square(xf - mu), axis=-1, keepdims=True)
    y = (xf - mu) * lax.rsqrt(var + LN_EPS) * g.astype(jnp.float32) + b.astype(jnp.float32)
    return y.astype(x.dtype)

def diff_attention(q, k, v, lam, pos):
    scale = DIFF_QK_DIM ** -0.5
    S = q.shape[1]

    def block(args):
        qb, t = args
        s = jnp.einsum('bqhmd,bkhmd->bhmqk', qb, k).astype(jnp.float32) * scale
        causal = t[:, None] >= pos[None, :]
        p = jax.nn.softmax(jnp.where(causal, s, NEG_INF), axis=-1)
        p = p[:, :, 0] - lam * p[:, :, 1]
        return jnp.einsum('bhqk,bkhe->bqhe', p, v)

    out = lax.map(block, (to_blocks(q), pos.reshape(S // Q_BLOCK, Q_BLOCK)))
    return from_blocks(out)

def dsa_attention(q, k, v, qi, ki, wi, pos, topk):
    scale = DSA_DIM ** -0.5
    S = q.shape[1]

    def block(args):
        qb, qib, wib, t = args
        sc = jnp.einsum('bqhd,bsd->bqhs', qib, ki).astype(jnp.float32)
        idx_score = jnp.einsum('bqhs,bqh->bqs', jax.nn.relu(sc), wib.astype(jnp.float32))
        causal = t[:, None] >= pos[None, :]
        idx_score = jnp.where(causal[None], idx_score, -jnp.inf)
        _, idx = lax.top_k(idx_score, topk)
        kg = jax.vmap(lambda kk, ii: kk[ii])(k, idx)
        vg = jax.vmap(lambda vv, ii: vv[ii])(v, idx)
        s = jnp.einsum('bqhd,bqkd->bhqk', qb, kg).astype(jnp.float32) * scale
        valid = idx <= t[None, :, None]
        p = jax.nn.softmax(jnp.where(valid[:, None], s, NEG_INF), axis=-1)
        return jnp.einsum('bhqk,bqkd->bqhd', p, vg)

    out = lax.map(block, (to_blocks(q), to_blocks(qi), to_blocks(wi),
                          pos.reshape(S // Q_BLOCK, Q_BLOCK)))
    return from_blocks(out)

def forgetting_attention(q, k, v, logf, pos):
    scale = FOX_DIM ** -0.5
    S = q.shape[1]
    c = jnp.cumsum(logf, axis=1)
    c_keys = jnp.transpose(c, (0, 2, 1))

    def block(args):
        qb, cb, t = args
        s = jnp.einsum('bqhd,bkhd->bhqk', qb, k).astype(jnp.float32) * scale
        s = s + jnp.transpose(cb, (0, 2, 1))[..., None] - c_keys[:, :, None, :]
        causal = t[:, None] >= pos[None, :]
        p = jax.nn.softmax(jnp.where(causal, s, NEG_INF), axis=-1)
        return jnp.einsum('bhqk,bkhd->bqhd', p, v)

    out = lax.map(block, (to_blocks(q), to_blocks(c), pos.reshape(S // Q_BLOCK, Q_BLOCK)))
    return from_blocks(out)

def hybrid_layer(x, w_in, b_f, lam_q1, lam_k1, lam_q2, lam_k2, g_subln, w_out, ln_g, ln_b, layer_idx):
    B, S, _ = x.shape
    pos = jnp.arange(S, dtype=jnp.int32)
    h = jnp.einsum('bsd,de->bse', x, w_in)
    (dq, dk, dv, sq, sk, sv, iq, ik, iw, fq, fk, fv, ff, gate) = split_columns(h)

    dq = rope(dq.reshape(B, S, DIFF_HEADS * 2, DIFF_QK_DIM), pos).reshape(B, S, DIFF_HEADS, 2, DIFF_QK_DIM)
    dk = rope(dk.reshape(B, S, DIFF_HEADS * 2, DIFF_QK_DIM), pos).reshape(B, S, DIFF_HEADS, 2, DIFF_QK_DIM)
    dv = dv.reshape(B, S, DIFF_HEADS, DIFF_V_DIM)
    lambda_init = 0.8 - 0.6 * math.exp(-0.3 * layer_idx)
    lam = (jnp.exp(jnp.sum(lam_q1.astype(jnp.float32) * lam_k1.astype(jnp.float32)))
           - jnp.exp(jnp.sum(lam_q2.astype(jnp.float32) * lam_k2.astype(jnp.float32))) + lambda_init)
    a = diff_attention(dq, dk, dv, lam, pos)
    a = a * lax.rsqrt(jnp.mean(a * a, axis=-1, keepdims=True) + SUBLN_EPS) * g_subln.astype(jnp.float32) * (1.0 - lambda_init)
    a = a.reshape(B, S, DIFF_WIDTH)

    sq = rope(sq.reshape(B, S, DSA_HEADS, DSA_DIM), pos)
    sk = rope(sk, pos)
    iq = rope(iq.reshape(B, S, IDX_HEADS, IDX_DIM), pos)
    ik = rope(ik, pos)
    topk = min(DSA_TOPK_MAX, S // 4)
    bo = dsa_attention(sq, sk, sv, iq, ik, iw * IDX_WEIGHT_SCALE, pos, topk).reshape(B, S, DSA_WIDTH)

    logf = jax.nn.log_sigmoid(ff.astype(jnp.float32) + b_f.astype(jnp.float32))
    co = forgetting_attention(fq.reshape(B, S, FOX_HEADS, FOX_DIM), fk.reshape(B, S, FOX_HEADS, FOX_DIM),
                              fv.reshape(B, S, FOX_HEADS, FOX_DIM), logf, pos).reshape(B, S, FOX_WIDTH)

    mixed = jnp.concatenate([a, bo, co], axis=-1) * jax.nn.silu(gate.astype(jnp.float32))
    out = jnp.einsum('bse,ed->bsd', mixed.astype(x.dtype), w_out)
    return layer_norm(DEEPNORM_ALPHA * x + out, ln_g, ln_b)

def first_inputs(seed: int = 0) -> dict:
    key = jax.random.key(seed)
    ks = jax.random.split(key, 12)
    x = jax.random.normal(ks[0], (BATCH, SEQ, D_MODEL), jnp.float32)
    col_scale = np.concatenate([
        np.full((n,), DEEPNORM_BETA if name in VALUE_COLS else 1.0, np.float32) for name, n in IN_SPLITS
    ]) * np.float32(D_MODEL ** -0.5)
    w_in = jax.random.normal(ks[1], (DEPTH, D_MODEL, IN_WIDTH), jnp.float32) * jnp.asarray(col_scale)
    b_f = 1.0 + 0.1 * jax.random.normal(ks[2], (DEPTH, FOX_HEADS), jnp.float32)
    lam_q1 = 0.1 * jax.random.normal(ks[3], (DEPTH, DIFF_QK_DIM), jnp.float32)
    lam_k1 = 0.1 * jax.random.normal(ks[4], (DEPTH, DIFF_QK_DIM), jnp.float32)
    lam_q2 = 0.1 * jax.random.normal(ks[5], (DEPTH, DIFF_QK_DIM), jnp.float32)
    lam_k2 = 0.1 * jax.random.normal(ks[6], (DEPTH, DIFF_QK_DIM), jnp.float32)
    g_subln = 1.0 + 0.02 * jax.random.normal(ks[7], (DEPTH, DIFF_V_DIM), jnp.float32)
    w_out = jax.random.normal(ks[8], (DEPTH, D_MIX, D_MODEL), jnp.float32) * (D_MIX ** -0.5) * DEEPNORM_BETA
    ln_g = 1.0 + 0.02 * jax.random.normal(ks[9], (DEPTH, D_MODEL), jnp.float32)
    ln_b = 0.02 * jax.random.normal(ks[10], (DEPTH, D_MODEL), jnp.float32)
    return {'x': x, 'w_in': w_in, 'b_f': b_f, 'lam_q1': lam_q1, 'lam_k1': lam_k1,
            'lam_q2': lam_q2, 'lam_k2': lam_k2, 'g_subln': g_subln, 'w_out': w_out,
            'ln_g': ln_g, 'ln_b': ln_b}

def first_block(x, w_in, b_f, lam_q1, lam_k1, lam_q2, lam_k2, g_subln, w_out, ln_g, ln_b):
    for l in range(DEPTH):
        x = hybrid_layer(x, w_in[l], b_f[l], lam_q1[l], lam_k1[l], lam_q2[l], lam_k2[l],
                         g_subln[l], w_out[l], ln_g[l], ln_b[l], l)
    return x


CTX_LEN = 256
GRID_W = 64
EPS = 1e-6

D_CONV = 512
CONV_WIDTH = 31
GLA_HEADS = 4
GLA_DK = 64
GLA_DV = 128
GLA_QK = GLA_HEADS * GLA_DK
GLA_V = GLA_HEADS * GLA_DV
GLA_RANK = 16
GLA_GATE_NORM = 16.0
GLA_CHUNK = 64
ATT_HEADS = 8
ATT_KV_HEADS = 2
ATT_GROUP = ATT_HEADS // ATT_KV_HEADS
ATT_HD = 64
ATT_Q = ATT_HEADS * ATT_HD
ATT_KV = ATT_KV_HEADS * ATT_HD
ATT_BLOCK = 128
ROPE_AXIS_DIM = ATT_HD // 2

IN_SPLITS_2 = (D_CONV, D_CONV, D_CONV,
             GLA_QK, GLA_QK, GLA_V, GLA_V, GLA_RANK, GLA_RANK,
             ATT_Q, ATT_KV, ATT_KV, ATT_Q,
             D_MODEL, D_MODEL, D_MODEL)
N_IN = sum(IN_SPLITS_2)


def rms_norm(x, g):
    xf = x.astype(jnp.float32)
    y = xf * lax.rsqrt(jnp.mean(xf * xf, axis=-1, keepdims=True) + EPS)
    return (y * g.astype(jnp.float32)).astype(x.dtype)

def layer_norm_2(x, g, b):
    xf = x.astype(jnp.float32)
    mu = jnp.mean(xf, axis=-1, keepdims=True)
    var = jnp.mean(jnp.square(xf - mu), axis=-1, keepdims=True)
    y = (xf - mu) * lax.rsqrt(var + EPS)
    return (y * g.astype(jnp.float32) + b.astype(jnp.float32)).astype(x.dtype)

def split_cols(p):
    idx = np.cumsum(np.array(IN_SPLITS_2))[:-1].tolist()
    return jnp.split(p, idx, axis=-1)

def conv_module(val, glu, gate, dw_w, dw_b, ln_g, ln_b, w_o):
    u = val * jax.nn.sigmoid(glu)
    pad = CONV_WIDTH // 2
    u = lax.conv_general_dilated(u, dw_w[:, None, :], window_strides=(1,),
                                 padding=[(pad, pad)],
                                 dimension_numbers=('NWC', 'WIO', 'NWC'),
                                 feature_group_count=D_CONV) + dw_b
    u = jax.nn.silu(layer_norm_2(u, ln_g, ln_b)) * jax.nn.silu(gate)
    return u @ w_o

def gla_scan(q, k, v, log_a, s0):
    b_, t_, h_, _ = q.shape
    dv = v.shape[-1]
    n = t_ // GLA_CHUNK

    def chunks(z):
        return z.astype(jnp.float32).reshape(b_, n, GLA_CHUNK, h_, z.shape[-1])

    q, k, v, log_a = chunks(q), chunks(k), chunks(v), chunks(log_a)
    cum = jnp.cumsum(log_a, axis=2)
    last = cum[:, :, -1]
    q_in = q * jnp.exp(cum)
    k_in = k * jnp.exp(-cum)
    mask = jnp.tril(jnp.ones((GLA_CHUNK, GLA_CHUNK), dtype=bool))
    att = jnp.where(mask, jnp.einsum('bnihd,bnjhd->bnhij', q_in, k_in), 0.0)
    o_intra = jnp.einsum('bnhij,bnjhe->bnihe', att, v)
    k_state = k * jnp.exp(last[:, :, None] - cum)
    contrib = jnp.einsum('bnjhd,bnjhe->bnhde', k_state, v)
    decay = jnp.exp(last)

    def step(s, inp):
        dec, con = inp
        return dec[..., None] * s + con, s

    s_fin, s_prev = lax.scan(step, s0, (jnp.swapaxes(decay, 0, 1), jnp.swapaxes(contrib, 0, 1)))
    o_inter = jnp.einsum('bnihd,bnhde->bnihe', q_in, jnp.swapaxes(s_prev, 0, 1))
    return (o_intra + o_inter).reshape(b_, t_, h_, dv), s_fin

def gla_heads(q, k, v):
    b_, t_, _ = q.shape
    return (q.reshape(b_, t_, GLA_HEADS, GLA_DK) * (GLA_DK ** -0.5),
            k.reshape(b_, t_, GLA_HEADS, GLA_DK),
            v.reshape(b_, t_, GLA_HEADS, GLA_DV))

def gla_log_gate(lr, w_up, b_up):
    b_, t_, _ = lr.shape
    z = (lr @ w_up + b_up).astype(jnp.float32)
    return (jax.nn.log_sigmoid(z) / GLA_GATE_NORM).reshape(b_, t_, GLA_HEADS, GLA_DK)

def gla_output(o, gate, norm_g, w_o):
    b_, t_ = o.shape[:2]
    o = rms_norm(o, norm_g).reshape(b_, t_, GLA_V).astype(gate.dtype)
    return (o * jax.nn.silu(gate)) @ w_o

def gla_branch(xp, cp, w_up, b_up, norm_g, w_o, need_ctx):
    xq, xk, xv, xg, xlf, xlb = xp
    cq, ck, cv, cg, clf, clb = cp
    xq, xk, xv = gla_heads(xq, xk, xv)
    cq, ck, cv = gla_heads(cq, ck, cv)
    s0 = jnp.zeros((xq.shape[0], GLA_HEADS, GLA_DK, GLA_DV), jnp.float32)

    def flip(z):
        return jnp.flip(z, axis=1)

    oc_f, sc_f = gla_scan(cq, ck, cv, gla_log_gate(clf, w_up[0], b_up[0]), s0)
    ox_f, _ = gla_scan(xq, xk, xv, gla_log_gate(xlf, w_up[0], b_up[0]), sc_f)
    oc_b, sc_b = gla_scan(flip(cq), flip(ck), flip(cv),
                          flip(gla_log_gate(clb, w_up[1], b_up[1])), s0)
    ox_b, _ = gla_scan(flip(xq), flip(xk), flip(xv),
                       flip(gla_log_gate(xlb, w_up[1], b_up[1])), sc_b)
    y_x = gla_output(ox_f + flip(ox_b), xg, norm_g, w_o)
    y_c = gla_output(oc_f + flip(oc_b), cg, norm_g, w_o) if need_ctx else None
    return y_x, y_c

def rope_tables(t_):
    n_rows = t_ // GRID_W
    row = jnp.repeat(jnp.arange(n_rows, dtype=jnp.float32), GRID_W)
    col = jnp.tile(jnp.arange(GRID_W, dtype=jnp.float32), n_rows)
    n_freq = ROPE_AXIS_DIM // 2
    freqs = ROPE_THETA ** (-jnp.arange(n_freq, dtype=jnp.float32) / n_freq)
    ang_r = row[:, None] * freqs
    ang_c = col[:, None] * freqs
    return jnp.cos(ang_r), jnp.sin(ang_r), jnp.cos(ang_c), jnp.sin(ang_c)

def rotate_half(x, cos, sin):
    x1, x2 = jnp.split(x, 2, axis=-1)
    cos = cos[:, None, :]
    sin = sin[:, None, :]
    return jnp.concatenate([x1 * cos - x2 * sin, x2 * cos + x1 * sin], axis=-1)

def rope_2d(x, tabs):
    cr, sr, cc, sc = tabs
    xr, xcol = jnp.split(x.astype(jnp.float32), 2, axis=-1)
    return jnp.concatenate([rotate_half(xr, cr, sr), rotate_half(xcol, cc, sc)], axis=-1).astype(x.dtype)

def attn_heads(q, k, v, qn_g, kn_g, tabs):
    b_, t_, _ = q.shape
    q = rms_norm(q.reshape(b_, t_, ATT_HEADS, ATT_HD), qn_g)
    k = rms_norm(k.reshape(b_, t_, ATT_KV_HEADS, ATT_HD), kn_g)
    if tabs is not None:
        q, k = rope_2d(q, tabs), rope_2d(k, tabs)
    return (q.reshape(b_, t_, ATT_KV_HEADS, ATT_GROUP, ATT_HD), k,
            v.reshape(b_, t_, ATT_KV_HEADS, ATT_HD))

def gqa_attend(q, k, v):
    s = jnp.einsum('bqkgd,bskd->bkgqs', q, k).astype(jnp.float32) * (ATT_HD ** -0.5)
    p = jax.nn.softmax(s, axis=-1).astype(v.dtype)
    return jnp.einsum('bkgqs,bskd->bqkgd', p, v)

def attn_branch(xp, cp, qn_g, kn_g, w_o, need_ctx):
    xq, xk, xv, xg = xp
    cq, ck, cv, cg = cp
    b_, t_, _ = xq.shape
    xq, xk, xv = attn_heads(xq, xk, xv, qn_g, kn_g, rope_tables(t_))
    cq, ck, cv = attn_heads(cq, ck, cv, qn_g, kn_g, None)
    k_all = jnp.concatenate([ck, xk], axis=1)
    v_all = jnp.concatenate([cv, xv], axis=1)
    n_blk = t_ // ATT_BLOCK
    q_blk = jnp.swapaxes(xq.reshape(b_, n_blk, ATT_BLOCK, ATT_KV_HEADS, ATT_GROUP, ATT_HD), 0, 1)
    o = lax.map(lambda qb: gqa_attend(qb, k_all, v_all), q_blk)
    o = jnp.swapaxes(o, 0, 1).reshape(b_, t_, ATT_Q)
    y_x = (o * jax.nn.silu(xg)) @ w_o
    y_c = None
    if need_ctx:
        oc = gqa_attend(cq, ck, cv).reshape(b_, cq.shape[1], ATT_Q)
        y_c = (oc * jax.nn.silu(cg)) @ w_o
    return y_x, y_c

def hybrid_layer_2(xs, cs, c, c_ctx, norm_g, w_mod, b_mod, w_in, b_in, dw_w, dw_b, ln_g, ln_b,
                 w_conv_out, gla_w_gate, gla_b_gate, gla_norm_g, w_gla_out, q_norm_g, k_norm_g,
                 w_attn_out, w_out, need_ctx):
    shift_x, scale_x, gate_x = jnp.split(jax.nn.silu(c) @ w_mod + b_mod, 3, axis=-1)
    shift_c, scale_c, gate_c = jnp.split(jax.nn.silu(c_ctx) @ w_mod + b_mod, 3, axis=-1)
    hx = rms_norm(xs, norm_g) * (1 + scale_x[:, None]) + shift_x[:, None]
    hc = rms_norm(cs, norm_g) * (1 + scale_c) + shift_c
    px = split_cols(hx @ w_in + b_in)
    pc = split_cols(hc @ w_in + b_in)

    ya_x = conv_module(*px[0:3], dw_w, dw_b, ln_g, ln_b, w_conv_out)
    yb_x, yb_c = gla_branch(px[3:9], pc[3:9], gla_w_gate, gla_b_gate, gla_norm_g, w_gla_out, need_ctx)
    yc_x, yc_c = attn_branch(px[9:13], pc[9:13], q_norm_g, k_norm_g, w_attn_out, need_ctx)

    def merge(p, ya, yb, yc):
        return (jax.nn.sigmoid(p[13]) * ya + jax.nn.sigmoid(p[14]) * yb
                + jax.nn.sigmoid(p[15]) * yc) @ w_out

    xs = xs + gate_x[:, None] * merge(px, ya_x, yb_x, yc_x)
    if need_ctx:
        ya_c = conv_module(*pc[0:3], dw_w, dw_b, ln_g, ln_b, w_conv_out)
        cs = cs + gate_c * merge(pc, ya_c, yb_c, yc_c)
    return xs, cs

def second_inputs(seed: int = 0) -> dict:
    key = jax.random.key(seed)
    ks = jax.random.split(key, 22)

    def nrm(k, shape, s):
        return jax.random.normal(k, shape, jnp.float32) * s

    return {
        'x': nrm(ks[0], (BATCH, SEQ, D_MODEL), 1.0),
        'c': nrm(ks[1], (BATCH, D_MODEL), 1.0),
        'ctx': nrm(ks[2], (BATCH, CTX_LEN, D_MODEL), 1.0),
        'c_ctx': nrm(ks[3], (D_MODEL,), 1.0),
        'norm_g': 1.0 + nrm(ks[4], (DEPTH, D_MODEL), 0.02),
        'w_mod': nrm(ks[5], (DEPTH, D_MODEL, 3 * D_MODEL), 0.5 * D_MODEL ** -0.5),
        'b_mod': nrm(ks[6], (DEPTH, 3 * D_MODEL), 0.01),
        'w_in': nrm(ks[7], (DEPTH, D_MODEL, N_IN), D_MODEL ** -0.5),
        'b_in': nrm(ks[8], (DEPTH, N_IN), 0.01),
        'conv_dw_w': nrm(ks[9], (DEPTH, CONV_WIDTH, D_CONV), CONV_WIDTH ** -0.5),
        'conv_dw_b': nrm(ks[10], (DEPTH, D_CONV), 0.01),
        'conv_ln_g': 1.0 + nrm(ks[11], (DEPTH, D_CONV), 0.02),
        'conv_ln_b': nrm(ks[12], (DEPTH, D_CONV), 0.01),
        'w_conv_out': nrm(ks[13], (DEPTH, D_CONV, D_MODEL), D_CONV ** -0.5),
        'gla_w_gate': nrm(ks[14], (DEPTH, 2, GLA_RANK, GLA_QK), GLA_RANK ** -0.5),
        'gla_b_gate': nrm(ks[15], (DEPTH, 2, GLA_QK), 0.1),
        'gla_norm_g': 1.0 + nrm(ks[16], (DEPTH, GLA_DV), 0.02),
        'w_gla_out': nrm(ks[17], (DEPTH, GLA_V, D_MODEL), GLA_V ** -0.5),
        'q_norm_g': 1.0 + nrm(ks[18], (DEPTH, ATT_HD), 0.02),
        'k_norm_g': 1.0 + nrm(ks[19], (DEPTH, ATT_HD), 0.02),
        'w_attn_out': nrm(ks[20], (DEPTH, ATT_Q, D_MODEL), ATT_Q ** -0.5),
        'w_out': nrm(ks[21], (DEPTH, D_MODEL, D_MODEL), D_MODEL ** -0.5),
    }

def second_block(x, c, ctx, c_ctx, norm_g, w_mod, b_mod, w_in, b_in, conv_dw_w, conv_dw_b,
              conv_ln_g, conv_ln_b, w_conv_out, gla_w_gate, gla_b_gate, gla_norm_g, w_gla_out,
              q_norm_g, k_norm_g, w_attn_out, w_out):
    xs, cs = x, ctx
    for l in range(DEPTH):
        xs, cs = hybrid_layer_2(xs, cs, c, c_ctx, norm_g[l], w_mod[l], b_mod[l], w_in[l], b_in[l],
                              conv_dw_w[l], conv_dw_b[l], conv_ln_g[l], conv_ln_b[l], w_conv_out[l],
                              gla_w_gate[l], gla_b_gate[l], gla_norm_g[l], w_gla_out[l],
                              q_norm_g[l], k_norm_g[l], w_attn_out[l], w_out[l],
                              need_ctx=(l < DEPTH - 1))
    return xs


def setup_inputs(seed=0):
    out = dict(first_inputs(seed))
    for name, value in second_inputs(seed + 1).items():
        if name != "x":
            out[name + "_2"] = value
    return out


def reference(
    x, w_in, b_f, lam_q1, lam_k1, lam_q2, lam_k2, g_subln, w_out, ln_g, ln_b, c_2, ctx_2,
    c_ctx_2, norm_g_2, w_mod_2, b_mod_2, w_in_2, b_in_2, conv_dw_w_2, conv_dw_b_2, conv_ln_g_2,
    conv_ln_b_2, w_conv_out_2, gla_w_gate_2, gla_b_gate_2, gla_norm_g_2, w_gla_out_2,
    q_norm_g_2, k_norm_g_2, w_attn_out_2, w_out_2,
):
    x = first_block(
        x, w_in, b_f, lam_q1, lam_k1, lam_q2, lam_k2, g_subln, w_out, ln_g, ln_b,
    )
    return second_block(
        x, c_2, ctx_2, c_ctx_2, norm_g_2, w_mod_2, b_mod_2, w_in_2, b_in_2, conv_dw_w_2,
        conv_dw_b_2, conv_ln_g_2, conv_ln_b_2, w_conv_out_2, gla_w_gate_2, gla_b_gate_2,
        gla_norm_g_2, w_gla_out_2, q_norm_g_2, k_norm_g_2, w_attn_out_2, w_out_2,
    )


_drawn_inputs = setup_inputs


def setup_inputs(seed=0):
    import zlib

    import numpy as np

    out = dict(_drawn_inputs(seed))
    spreads = {}
    factors = {'b_f': 64.0,
     'lam_q1': 4.398,
     'lam_k1': 4.757,
     'lam_q2': 5.287,
     'g_subln': 8.0,
     'norm_g_2': 8.0,
     'b_mod_2': 6.679,
     'b_in_2': 8.0,
     'conv_dw_b_2': 8.0,
     'conv_ln_g_2': 8.0,
     'conv_ln_b_2': 8.0,
     'gla_b_gate_2': 8.0,
     'gla_norm_g_2': 8.0,
     'q_norm_g_2': 8.0,
     'k_norm_g_2': 8.0}
    for name, (base, spread) in spreads.items():
        noise = np.random.default_rng([zlib.crc32(name.encode()), seed]).standard_normal(out[name].shape)
        drawn = base * np.exp(spread * noise) if base else spread * noise
        out[name] = jnp.asarray(drawn.astype(out[name].dtype))
    for name, factor in factors.items():
        out[name] = (out[name] * factor).astype(out[name].dtype)
    return out
```

```python
import numpy as np
import concourse.bass as bass
import concourse.mybir as mybir
from concourse.alu_op_type import AluOpType as ALU

F32, F32R, BF16 = mybir.dt.float32, mybir.dt.float32r, mybir.dt.bfloat16
ACT = mybir.ActivationFunctionType
AXX = mybir.AxisListType.X

P = 128
D = 1024
S = 256
NT = S // P
KD = D // P
HD = 64
LAYERS = 2
NEG = -1e30
FILL = -3e38
TOPK = 64
ALPHA = (2 * LAYERS) ** 0.25
EPS1 = 1e-5
EPS2 = 1e-6
WC = 512
KP = 2

SPLIT1 = [("diff_q", 512), ("diff_k", 512), ("diff_v", 512), ("dsa_q", 256), ("dsa_k", 64),
          ("dsa_v", 64), ("idx_q", 512), ("idx_k", 64), ("idx_w", 8), ("fox_q", 256),
          ("fox_k", 256), ("fox_v", 256), ("fox_f", 4), ("gate", 1024)]
CHUNKS1 = [[("idx_q", 0, 512)],
           [("idx_k", 0, 64), ("dsa_k", 0, 64), ("dsa_q", 0, 256), ("dsa_v", 0, 64),
            ("idx_w", 0, 8), ("fox_f", 0, 4)],
           [("diff_q", 0, 512)], [("diff_k", 0, 512)], [("diff_v", 0, 512)],
           [("fox_q", 0, 256), ("fox_k", 0, 256)],
           [("fox_v", 0, 256), ("gate", 768, 256)],
           [("gate", 0, 512)], [("gate", 512, 256)]]
IQ, DSA, DQ, DK, DV, FQK, FV, GA, GB = range(len(CHUNKS1))
WIDTH1 = [sum(n for _, _, n in c) for c in CHUNKS1]


def offsets(widths, rows):
    out = [0]
    for w in widths:
        out.append(out[-1] + rows * w)
    return out


OFF1 = offsets(WIDTH1, D)
OFFO = offsets([WC, WC], D)


class Engine:

    def __init__(self, engine, sem):
        self.engine, self.sem, self.count, self.seen = engine, sem, 0, {}

    def after(self, *tokens):
        for token in tokens:
            if token is None:
                continue
            sem, value = token
            if self.seen.get(id(sem), 0) < value:
                self.engine.wait_ge(sem, value)
                self.seen[id(sem)] = value
        return self.engine

    def mark(self, instruction):
        self.count += 1
        instruction.then_inc(self.sem, 1)
        return (self.sem, self.count)

    def restart(self):
        self.count, self.seen = 0, {}


class Loads:

    def __init__(self, queue, sems):
        self.queue, self.sems, self.counts = queue, sems, [0] * len(sems)

    def start(self, k, out, in_, *tokens):
        self.queue.after(*tokens).dma_start(out, in_).then_inc(self.sems[k], 16)
        self.counts[k] += 16
        return (self.sems[k], self.counts[k])

    def restart(self):
        self.counts = [0] * len(self.sems)


class Ring:

    def __init__(self, buffers):
        self.buffers, self.tokens, self.at = buffers, [()] * len(buffers), -1

    def take(self):
        self.at = (self.at + 1) % len(self.buffers)
        return self.buffers[self.at], self.tokens[self.at], self.at

    def free(self, slot, *tokens):
        self.tokens[slot] = tokens

    def restart(self):
        self.tokens, self.at = [()] * len(self.buffers), -1


def spread(ap, shape):
    return ap.unsqueeze(1).to_broadcast(shape)


def pipeline(items, stages):
    for step in range(len(items) + len(stages) - 1):
        for s in reversed(range(len(stages))):
            if 0 <= step - s < len(items):
                stages[s](items[step - s])
                yield


class Core:

    SLOTS = 6

    def __init__(self, nc, ctx):
        self.nc, self.ctx = nc, ctx
        sem = lambda name: ctx.enter_context(nc.semaphore(name))
        self.pe = Engine(nc.tensor, sem("pe_done"))
        self.act = Engine(nc.scalar, sem("act_done"))
        self.dve = Engine(nc.vector, sem("dve_done"))
        self.pool = Engine(nc.gpsimd, sem("pool_done"))
        self.sp = Engine(nc.sync, sem("sp_unused"))
        self.weights = Loads(self.sp, [sem(f"weights_in{i}") for i in range(self.SLOTS)])
        self.small = Loads(self.sp, [sem(f"small_in{i}") for i in range(16)])
        self.bank = [ctx.enter_context(nc.psum_tensor(f"bank{i}", [P, 512], F32)) for i in range(8)]
        self.proj = Ring(self.bank[0:4])
        self.aux = Ring(self.bank[4:7])
        self.sum_bank = Ring(self.bank[7:8])
        self.rings = [self.proj, self.aux, self.sum_bank]
        self.pieces, self.cut, self.done = [], [], []

    def sb(self, name, shape, dtype=F32):
        return self.ctx.enter_context(self.nc.sbuf_tensor(name, shape, dtype))

    def ring(self, name, n, shape, dtype=F32):
        whole = self.sb(name, [shape[0], n] + shape[1:], dtype)
        ring = Ring([whole[:, i] for i in range(n)])
        self.rings.append(ring)
        return ring

    def piece_slots(self, name, raw, cut):
        self.RAW, self.CUT = raw, cut
        self.raw = self.sb("w_raw" + name, [P, raw, KP * WC])
        self.hi = self.sb("w_hi" + name, [P, cut, KP * WC], F32R)
        self.lo = self.sb("w_lo" + name, [P, cut, KP * WC], F32R)

    def stream(self, pieces):
        self.pieces += pieces

    def load_piece(self):
        n = len(self.loaded)
        dram, width = self.pieces[n]
        slot = n % self.RAW
        before = self.cut[n - self.RAW] if n >= self.RAW else ()
        self.loaded.append(self.weights.start(slot, self.raw[:, slot, 0:KP * width], dram, *before))

    def cut_piece(self):
        n = len(self.cut)
        _, width = self.pieces[n]
        raw = self.raw[:, n % self.RAW, 0:KP * width]
        hi = self.hi[:, n % self.CUT, 0:KP * width]
        lo = self.lo[:, n % self.CUT, 0:KP * width]
        free = self.done[n - self.CUT] if n >= self.CUT else None
        rounded = self.act.mark(self.act.after(self.loaded[n], free).activation(hi, raw, ACT.Copy))
        rest = self.dve.mark(self.dve.after(self.loaded[n], rounded).tensor_tensor(
            lo, raw, hi.bitcast(F32), ALU.subtract))
        self.cut.append((rounded, rest))

    def next_piece(self):
        n = len(self.done)
        while len(self.loaded) < min(n + self.RAW, len(self.pieces)):
            if len(self.loaded) >= self.RAW and len(self.cut) <= len(self.loaded) - self.RAW:
                break
            self.load_piece()
        while len(self.cut) < min(n + self.CUT, len(self.pieces)):
            self.cut_piece()
            if len(self.loaded) < len(self.pieces):
                self.load_piece()
        width = self.pieces[n][1]
        shape = lambda t: t[:, n % self.CUT, 0:KP * width].rearrange("p (k n) -> p k n", k=KP)
        return shape(self.hi), shape(self.lo), self.cut[n]

    def piece_used(self, token):
        self.done.append(token)

    def project(self, xs, n_k, tiles, width, evacuate, bias=None, width_of=None):
        (xh, xl, ready) = xs
        banks = []
        for t in tiles:
            ps, free, slot = self.proj.take()
            banks.append((ps, free, slot))
        pairs = n_k // KP
        for kp in range(pairs):
            hi, lo, cut = self.next_piece()
            for i, t in enumerate(tiles):
                ps, free, slot = banks[i]
                col = slice(t * P, (t + 1) * P)
                w = width_of(t) if width_of else width
                self.pe.after(*cut, *ready(t), *(free if kp == 0 else ()))
                for kk in range(KP):
                    k = kp * KP + kk
                    first, last = kp == 0 and kk == 0, kp == pairs - 1 and kk == KP - 1
                    mm = self.nc.tensor.matmul
                    if first and bias is not None:
                        bias(ps[:, 0:w], w)
                        first = False
                    mm(ps[:, 0:w], xh[:, k, col], hi[:, kk, 0:w], start=first, stop=False)
                    mm(ps[:, 0:w], xh[:, k, col], lo[:, kk, 0:w], start=False, stop=False)
                    ins = mm(ps[:, 0:w], xl[:, k, col], hi[:, kk, 0:w], start=False, stop=last)
                token = self.pe.mark(ins)
                if kp == pairs - 1:
                    self.proj.free(slot, *evacuate(t, ps, token))
                if i == len(tiles) - 1:
                    self.piece_used(token)
                yield

    def project_t(self, xs, n_k, n_tok, evacuate):
        (xh, xl, ready) = xs
        banks = [self.proj.take() for _ in range(WC // P)]
        for kp in range(n_k // KP):
            hi, lo, cut = self.next_piece()
            for j, (ps, free, slot) in enumerate(banks):
                self.pe.after(*cut, *ready, *(free if kp == 0 else ()))
                for kk in range(KP):
                    k = kp * KP + kk
                    first, last = k == 0, k == n_k - 1
                    mm, cols, out = self.nc.tensor.matmul, slice(j * P, (j + 1) * P), ps[:, 0:n_tok]
                    mm(out, hi[:, kk, cols], xh[:, k, 0:n_tok], start=first, stop=False)
                    mm(out, lo[:, kk, cols], xh[:, k, 0:n_tok], start=False, stop=False)
                    ins = mm(out, hi[:, kk, cols], xl[:, k, 0:n_tok], start=False, stop=last)
                token = self.pe.mark(ins)
                if k == n_k - 1:
                    self.proj.free(slot, *evacuate(j, ps, token))
                if j == len(banks) - 1:
                    self.piece_used(token)
                yield

    def transpose(self, blocks, ready, width=P):
        ps, free, slot = self.aux.take()
        self.pe.after(*ready, *free)
        for i, block in enumerate(blocks):
            ins = self.nc.tensor.transpose(ps[0:width, i * P:(i + 1) * P], block, self.ident[:, :])
        return ps, self.pe.mark(ins), slot

    def transpose_cut(self, src, cols, dst_hi, dst_lo, ready, free=()):
        tokens = []
        for b in range(0, cols // P, 4):
            ps, token, slot = self.transpose([src[:, (b + i) * P:(b + i + 1) * P] for i in range(4)],
                                             ready)
            view = ps[:, :].rearrange("p (k t) -> p k t", k=4)
            hi, lo = dst_hi[:, b:b + 4, :], dst_lo[:, b:b + 4, :]
            rounded = self.act.mark(self.act.after(token, *free).activation(hi, view, ACT.Copy))
            rest = self.dve.mark(self.dve.after(token, rounded).tensor_tensor(
                lo, view, hi.bitcast(F32), ALU.subtract))
            self.aux.free(slot, rest, rounded)
            tokens += [rounded, rest]
            yield
        self.last = tokens

    def fence(self):
        return [(e.sem, e.count) for e in (self.pe, self.act, self.dve, self.pool) if e.count]

    def restart(self):
        nc = self.nc
        nc.all_engine_barrier()
        for e in (self.pe, self.act, self.dve, self.pool, self.sp):
            nc.sync.sem_clear(e.sem)
        for s in self.weights.sems + self.small.sems:
            nc.sync.sem_clear(s)
        nc.all_engine_barrier()
        for x in [self.pe, self.act, self.dve, self.pool, self.sp, self.weights, self.small] + self.rings:
            x.restart()
        self.pieces, self.loaded, self.cut, self.done = [], [], [], []


def weave(main, side, ratio):
    owed = 0.0
    for condition in main:
        while condition is not None and not condition():
            next(side)
        owed += ratio
        while owed >= 1 and side is not None:
            owed -= 1
            if next(side, "end") == "end":
                side = None
    for _ in (side or ()):
        pass


def first_layer(core, layer, io, m):
    nc, pe, act, dve, pool, sp = core.nc, core.pe, core.act, core.dve, core.pool, core.sp
    small = core.small
    piece = lambda array, at, width: (array[layer, at:at + P * KP * width]
                                      .rearrange("(p n) -> p n", p=P), width)
    for c, width in enumerate(WIDTH1):
        core.stream([piece(io["w1"], OFF1[c] + kp * P * KP * width, width) for kp in range(KD // KP)])
    for c in range(2):
        core.stream([piece(io["wo1"], OFFO[c] + kp * P * KP * WC, WC) for kp in range(KD // KP)])

    row = io["small1"][layer, :].partition_broadcast(P)
    params = small.start(0, m.par[:, :], row)
    bf, lams, gsub = m.par[:, 0:4], m.par[:, 4:260], m.par[:, 260:388]
    ln_g, ln_b = m.par[:, 388:388 + D], m.par[:, 388 + D:388 + 2 * D]

    lp = lams.rearrange("p (a b d) -> p a b d", a=2, b=2)
    prod = dve.mark(dve.after(params).tensor_tensor(m.lprod[:, :, :], lp[:, :, 0, :], lp[:, :, 1, :], ALU.mult))
    dots = dve.mark(dve.after(prod).tensor_reduce(m.lam[:, 0:2], m.lprod[:, :, :], AXX, ALU.add))
    li = act.mark(act.after().activation(m.linit[:, 2:4], m.lconst[:, bass.ds(layer * 2, 2)], ACT.Copy))
    exps = act.mark(act.after(dots, li).activation(m.lam[:, 2:4], m.lam[:, 0:2], ACT.Exp))
    diff = dve.mark(dve.after(exps).tensor_tensor(m.lam[:, 4:5], m.lam[:, 2:3], m.lam[:, 3:4], ALU.subtract))
    lam = dve.mark(dve.after(diff).tensor_tensor(m.lam[:, 5:6], m.lam[:, 4:5], m.linit[:, 2:3], ALU.add))
    gsc = dve.mark(dve.after(li, params).tensor_scalar(m.gs[:, :], gsub, m.linit[:, 3:4], None, ALU.mult))

    x_ready = {}
    for t in range(NT):
        cols = slice(t * P, (t + 1) * P)
        for _ in core.transpose_cut(m.x[:, t, :], D, m.xh[:, :, cols], m.xl[:, :, cols], ()):
            pass
        x_ready[t] = core.last
    xs = (m.xh, m.xl, lambda t: x_ready[t])

    got = {}

    def rope(ps, heads, t, out, token):
        v = ps[:, 0:heads * HD].rearrange("p (h d) -> p h d", d=HD)
        (tmp, free, slot) = m.rope.take()
        a = tmp[:, 0, 0:heads * HD].rearrange("p (h d) -> p h d", d=HD)
        b = tmp[:, 1, 0:heads * HD].rearrange("p (h d) -> p h d", d=HD)
        h = HD // 2
        one = dve.mark(dve.after(token, *free).tensor_tensor(
            a, v, spread(m.cos[:, t, :], [P, heads, HD]), ALU.mult))
        dve.mark(dve.after().tensor_tensor(
            b[:, :, 0:h], v[:, :, h:HD], spread(m.sin[:, t, 0:h], [P, heads, h]), ALU.mult))
        two = dve.mark(dve.after().tensor_tensor(
            b[:, :, h:HD], v[:, :, 0:h], spread(m.sin[:, t, h:HD], [P, heads, h]), ALU.mult))
        end = pool.mark(pool.after(two).tensor_tensor(out, a, b, ALU.add))
        m.rope.free(slot, end)
        return two, end

    def evacuate(chunk):
        def run(t, ps, token):
            if chunk in (IQ, DQ, DK):
                dst = {IQ: m.iq, DQ: m.dq, DK: m.dk}[chunk]
                read, end = rope(ps, 8, t, dst[:, t, :].rearrange("p (h d) -> p h d", d=HD), token)
                got[chunk, t] = [end]
                return [read]
            if chunk == DSA:
                read, end = rope(ps, 6, t, m.sx[:, t, :].rearrange("p (h d) -> p h d", d=HD), token)
                end2 = dve.mark(dve.after().tensor_copy(m.sv[:, t, :], ps[:, 384:460]))
                got[chunk, t] = [end, end2]
                return [end2]
            if chunk == FQK:
                v = ps[:, :].rearrange("p (h d) -> p h d", d=HD)
                end = act.mark(act.after(token).activation(m.fqk[:, t, :, 0:HD], v, ACT.Copy))
            elif chunk == FV:
                dve_end = dve.mark(dve.after(token).tensor_copy(m.fv[:, t, :], ps[:, 0:256]))
                end = act.mark(act.after(dve_end).activation(m.gate[:, t, 768:1024], ps[:, 256:512], ACT.Copy))
                got[chunk, t] = [dve_end, end]
                return [dve_end, end]
            elif chunk == DV:
                end = act.mark(act.after(token).activation(m.dv[:, t, :], ps[:, :], ACT.Copy))
            elif chunk == GA:
                end = act.mark(act.after(token).activation(m.gate[:, t, 0:512], ps[:, :], ACT.Copy))
            else:
                end = act.mark(act.after(token).activation(m.gate[:, t, 512:768], ps[:, 0:256], ACT.Copy))
            got[chunk, t] = [end]
            return [end]
        return run

    def need(*chunks):
        while not all((c, t) in got for c in chunks for t in range(NT)):
            yield

    def tokens(*chunks):
        return [x for c in chunks for t in range(NT) for x in got[c, t]]

    def head_transposes(src, heads, dst, rows, scale, ready, free=()):
        out = []
        for h in range(0, heads, 2):
            n = min(2, heads - h)
            ps, free_ps, slot = core.aux.take()
            pe.after(*ready, *free_ps)
            for i in range(n):
                for t in range(NT):
                    ins = nc.tensor.transpose(ps[0:rows, (i * NT + t) * P:(i * NT + t + 1) * P],
                                              src(h + i, t), m.ident[:, :])
            token = pe.mark(ins)
            view = ps[0:rows, 0:n * S].rearrange("p (h t) -> p h t", h=n)
            if (h // 2) % 2 == 0:
                end = act.mark(act.after(token, *free).activation(dst[0:rows, h:h + n, :], view, ACT.Copy, scale=scale))
            else:
                end = dve.mark(dve.after(token, *free).tensor_scalar(dst[0:rows, h:h + n, :], view, scale, None, ALU.mult))
            core.aux.free(slot, end)
            out.append(end)
            yield
        core.last = out

    mixed = {}

    def sparse_index():
        yield from need(IQ, DSA)
        ready = tokens(IQ, DSA)
        yield from head_transposes(lambda h, t: m.iq[:, t, h * HD:(h + 1) * HD], 8, m.qa, HD, 1.0, ready)
        q_t = core.last
        yield from head_transposes(lambda h, t: m.sx[:, t, h * HD:(h + 1) * HD], 2, m.sk_t, HD, 1.0, ready)
        k_t = core.last
        yield from head_transposes(lambda h, t: m.sx[:, t, (2 + h) * HD:(3 + h) * HD], 4, m.sq_t, HD, HD ** -0.5, ready)
        got["dsa_t"] = k_t + core.last
        w_end = dve.mark(dve.after(*ready).tensor_scalar(m.iw[:, :, :], m.sv[:, :, 64:72], (8 * HD) ** -0.5, None, ALU.mult))
        for qt in range(NT):
            keys = (qt + 1) * P
            acc = None
            items = list(range(0, 8, 2))
            state = {}

            def scores(h):
                ps, free, slot = core.aux.take()
                pe.after(*q_t, *k_t, *free)
                for i in range(2):
                    ins = nc.tensor.matmul(ps[:, i * keys:(i + 1) * keys], m.qa[0:HD, h + i, qt * P:(qt + 1) * P],
                                           m.sk_t[0:HD, 0, 0:keys], start=True, stop=True)
                state[h] = (ps, slot, pe.mark(ins))

            def weigh(h):
                ps, slot, token = state[h]
                r, free, rslot = m.relu.take()
                end = act.mark(act.after(token, *free).activation(r[:, 0:2 * keys], ps[:, 0:2 * keys], ACT.Relu))
                core.aux.free(slot, end)
                for i in range(2):
                    w = m.iw[:, qt, h + i:h + i + 1]
                    part = r[:, i * keys:(i + 1) * keys]
                    if h + i == 0:
                        state["acc"] = dve.mark(dve.after(end, w_end, *state.get("acc_free", ())).tensor_scalar(
                            m.score[:, qt, 0:keys], part, w, None, ALU.mult))
                    else:
                        state["acc"] = dve.mark(dve.after(end, state["acc"]).scalar_tensor_tensor(
                            m.score[:, qt, 0:keys], part, w, m.score[:, qt, 0:keys], ALU.mult, ALU.add))
                m.relu.free(rslot, state["acc"])
            yield from pipeline(items, [scores, weigh])
            diag = m.score[:, qt, qt * P:keys]
            last = dve.mark(dve.after(state["acc"]).tensor_tensor(diag, diag, m.mask[:, :], ALU.add))
            for _ in range(TOPK // 8):
                top = dve.mark(dve.after(last).max(m.top8[:, :], m.score[:, qt, 0:keys]))
                last = dve.mark(dve.after(top).match_replace(m.score[:, qt, 0:keys], m.top8[:, :], m.score[:, qt, 0:keys], FILL))
                yield
            got["sel", qt] = dve.mark(dve.after(last, *m.sel_free).tensor_scalar(
                m.sel[:, qt, 0:keys], m.score[:, qt, 0:keys], 0.5 * FILL, NEG, ALU.is_gt, ALU.mult))
        m.idx_done = [q for q in q_t] + [(pe.sem, pe.count)]

    def attend(name, heads, q_of, k_of, rows, v_of, v_width, out, bias_sel, ready, gates):
        for qt in range(NT):
            keys = (qt + 1) * P
            nb = qt + 1
            diff_kind = name == "diff"
            n_out = 1 if diff_kind else 2
            osum, ofree, oslot = core.sum_bank.take()
            stat, sfree, sslot = m.stat.take()
            n_maps = 2 * heads
            top_of, sum_of, inv_of, sub_of = (stat[:, i * n_maps:(i + 1) * n_maps] for i in range(4))
            st = {}

            def scores(j):
                ps, free, slot = core.aux.take()
                pe.after(*ready, *free)
                for i in range(2):
                    part = ps[:, i * keys:(i + 1) * keys]
                    nc.tensor.matmul(part, q_of(2 * j + i)[0:rows, qt * P:(qt + 1) * P],
                                     k_of(2 * j + i)[0:rows, 0:keys], start=True, stop=False)
                    if bias_sel:
                        nc.tensor.matmul(part, m.identb[:, :], m.sel[:, qt, 0:keys], start=False, stop=False)
                    ins = nc.tensor.matmul(part[:, qt * P:keys], m.identb[:, :], m.maskb[:, :], start=False, stop=True)
                st[j] = [ps, slot, pe.mark(ins)]

            def soft(j):
                ps, slot, token = st[j]
                view = ps[:, 0:2 * keys].rearrange("p (a b) -> p a b", a=2)
                top = dve.mark(dve.after(token, *sfree).tensor_reduce(
                    top_of[:, 2 * j:2 * j + 2], view, AXX, ALU.max, negate=True))
                pm, free, pslot = m.prob.take()
                act.after(top, *free)
                for i in range(2):
                    n = 2 * j + i
                    end = act.mark(nc.scalar.activation(pm[:, i, 0:keys], ps[:, i * keys:(i + 1) * keys], ACT.Exp,
                                                        bias=top_of[:, n:n + 1], accum_out=sum_of[:, n:n + 1]))
                core.aux.free(slot, end)
                inv = dve.mark(dve.after(end).reciprocal(inv_of[:, 2 * j:2 * j + 2], sum_of[:, 2 * j:2 * j + 2]))
                if diff_kind:
                    lam_l1 = dve.mark(dve.after(inv).tensor_scalar(
                        sub_of[:, 2 * j:2 * j + 1], inv_of[:, 2 * j + 1:2 * j + 2], m.lam[:, 5:6], None, ALU.mult))
                    second = dve.mark(dve.after(lam_l1).tensor_scalar(
                        pm[:, 1, 0:keys], pm[:, 1, 0:keys], sub_of[:, 2 * j:2 * j + 1], None, ALU.mult))
                    end = dve.mark(dve.after(second).scalar_tensor_tensor(
                        pm[:, 0, 0:keys], pm[:, 0, 0:keys], inv_of[:, 2 * j:2 * j + 1], pm[:, 1, 0:keys],
                        ALU.mult, ALU.subtract))
                st[j] = [pm, pslot, end]
                st["inv"] = inv

            def flip(j):
                pm, pslot, end = st[j]
                ps, free, slot = core.aux.take()
                pe.after(end, *free)
                for i in range(n_out):
                    for b in range(nb):
                        ins = nc.tensor.transpose(ps[:, (i * nb + b) * P:(i * nb + b + 1) * P],
                                                  pm[:, i, b * P:(b + 1) * P], m.ident[:, :])
                token = pe.mark(ins)
                m.prob.free(pslot, token)
                pt, pfree, ptslot = m.prob_t.take()
                n = n_out * nb * P
                if j % 2 == 0:
                    end = act.mark(act.after(token, *pfree).activation(pt[:, 0:n], ps[:, 0:n], ACT.Copy))
                else:
                    end = dve.mark(dve.after(token, *pfree).tensor_copy(pt[:, 0:n], ps[:, 0:n]))
                core.aux.free(slot, end)
                st[j] = [pt, ptslot, end]

            def values(j):
                pt, ptslot, end = st[j]
                pe.after(end, *(ofree if j == 0 else ()))
                for i in range(n_out):
                    h = n_out * j + i
                    for b in range(nb):
                        ins = nc.tensor.matmul(osum[:, h * v_width:(h + 1) * v_width],
                                               pt[:, (i * nb + b) * P:(i * nb + b + 1) * P], v_of(h, b),
                                               start=b == 0, stop=b == nb - 1)
                st["sum"] = pe.mark(ins)
                m.prob_t.free(ptslot, st["sum"])
            yield from pipeline(list(range(heads)), [scores, soft, flip, values])
            n_cols = heads * n_out * v_width
            if diff_kind:
                end = act.mark(act.after(st["sum"]).activation(out[:, qt, :], osum[:, 0:n_cols], ACT.Copy))
            else:
                end = dve.mark(dve.after(st["sum"], st["inv"]).tensor_tensor(
                    out[:, qt, :].rearrange("p (h d) -> p h d", d=v_width),
                    osum[:, 0:n_cols].rearrange("p (h d) -> p h d", d=v_width),
                    inv_of.unsqueeze(2).to_broadcast([P, n_maps, v_width]), ALU.mult))
            m.stat.free(sslot, end)
            core.sum_bank.free(oslot, end)
            mixed[name, qt] = [end]
            yield

    def sub_norm(qt):
        a = m.mix[:, qt, 0:512]
        sq, free, slot = m.relu.take()
        s1 = pool.mark(pool.after(*mixed["diff", qt], *free).tensor_tensor(sq[:, 0:512], a, a, ALU.mult))
        s2 = dve.mark(dve.after(s1).tensor_reduce(m.ms[:, qt, :], sq[:, 0:512].rearrange("p (h d) -> p h d", h=4), AXX, ALU.add))
        m.relu.free(slot, s2)
        s3 = dve.mark(dve.after(s2).tensor_scalar(m.ms[:, qt, :], m.ms[:, qt, :], 1.0 / P, EPS1, ALU.mult, ALU.add))
        s4 = pool.mark(pool.after(s3).tensor_tensor(m.ms2[:, qt, :], m.ms[:, qt, :], m.half[:, 0:4], ALU.pow))
        av = a.rearrange("p (h d) -> p h d", h=4)
        gated = pool.mark(pool.after(gsc).tensor_tensor(av, av, spread(m.gs[:, :], [P, 4, P]), ALU.mult))
        for h in range(4):
            end = dve.mark(dve.after(s4, gated).tensor_scalar(av[:, h, :], av[:, h, :], m.ms2[:, qt, h:h + 1], None, ALU.mult))
        mixed["norm", qt] = [end]

    def side():
        yield from sparse_index()
        yield from attend("dsa", 2, lambda h: m.sq_t[:, h, :], lambda h: m.sk_t[:, 1, :], HD,
                          lambda h, b: m.sv[:, b, 0:64], HD, m.mix[:, :, 512:768], True,
                          got["dsa_t"] + [got["sel", 0], got["sel", 1]] + tokens(DSA), None)
        yield from need(DQ, DK)
        yield from head_transposes(lambda h, t: m.dq[:, t, h * HD:(h + 1) * HD], 8, m.qb, HD, HD ** -0.5, tokens(DQ))
        q_t = core.last
        yield from head_transposes(lambda h, t: m.dk[:, t, h * HD:(h + 1) * HD], 8, m.kb, HD, 1.0, tokens(DK))
        q_t = q_t + core.last
        yield from need(DV)
        yield from attend("diff", 4, lambda h: m.qb[:, h, :], lambda h: m.kb[:, h, :], HD,
                          lambda h, b: m.dv[:, b, h * P:(h + 1) * P], P, m.mix[:, :, 0:512], False,
                          q_t + [lam] + tokens(DV), None)
        for qt in range(NT):
            sub_norm(qt)
            yield
        yield from need(FQK)
        z = dve.mark(dve.after(*tokens(DSA), params).tensor_tensor(
            m.fz[:, :, :], m.sv[:, :, 72:76], spread(bf, [P, NT, 4]), ALU.add))
        az = dve.mark(dve.after(z).scalar_tensor_tensor(m.fa[:, :, :], m.fz[:, :, :], -1.0, m.fz[:, :, :], ALU.mult, ALU.max))
        ez = act.mark(act.after(az).activation(m.fe[:, :, :], m.fa[:, :, :], ACT.Exp, scale=-1.0))
        lz = act.mark(act.after(ez).activation(m.fl[:, :, :], m.fe[:, :, :], ACT.Ln, bias=1.0))
        lf = dve.mark(dve.after(lz).scalar_tensor_tensor(m.lf[:, :, :], m.fz[:, :, :], 0.0, m.fl[:, :, :], ALU.min, ALU.subtract))
        ps, free, slot = core.aux.take()
        pe.after(lf, *free)
        nc.tensor.matmul(ps[:, 0:4], m.tri[:, :], m.lf[:, 0, :], start=True, stop=True)
        nc.tensor.matmul(ps[:, 4:8], m.ones[:, :], m.lf[:, 0, :], start=True, stop=False)
        cs = pe.mark(nc.tensor.matmul(ps[:, 4:8], m.tri[:, :], m.lf[:, 1, :], start=False, stop=True))
        cv = ps[:, 0:8].rearrange("p (t h) -> p t h", t=NT)
        c1 = dve.mark(dve.after(cs).tensor_scalar(m.fqk[:, :, 0:4, 64], cv, HD ** 0.5, None, ALU.mult))
        c2 = dve.mark(dve.after(cs).tensor_scalar(m.fqk[:, :, 4:8, 65], cv, -HD ** 0.5, None, ALU.mult))
        core.aux.free(slot, c2)
        c3 = dve.mark(dve.after().memset(m.fqk[:, :, 0:4, 65], 1.0))
        c4 = dve.mark(dve.after().memset(m.fqk[:, :, 4:8, 64], 1.0))
        ready = tokens(FQK) + [c1, c2, c3, c4]
        yield
        yield from head_transposes(lambda h, t: m.fqk[:, t, h, :], 4, m.qa, 66, HD ** -0.5, ready, m.idx_done)
        f_t = core.last
        yield from head_transposes(lambda h, t: m.fqk[:, t, 4 + h, :], 4, m.ka, 66, 1.0, ready)
        f_t = f_t + core.last
        yield from need(FV)
        yield from attend("fox", 2, lambda h: m.qa[:, h, :], lambda h: m.ka[:, h, :], 66,
                          lambda h, b: m.fv[:, b, h * HD:(h + 1) * HD], HD, m.mix[:, :, 768:1024], False,
                          f_t + tokens(FV), None)

    def main():
        for c, width in enumerate(WIDTH1):
            yield from core.project(xs, KD, range(NT), width, evacuate(c))

    weave(main(), side(), io.get("ratio1", 2.0))

    proj_done = core.done[-1]
    ready = {}
    for t in range(NT):
        sg = act.mark(act.after(*tokens(GA, GB, FV)).activation(m.gate[:, t, :], m.gate[:, t, :], ACT.Silu))
        half = 512
        ends = []
        e1 = pool.mark(pool.after(sg, *mixed["norm", t]).tensor_tensor(
            m.mix[:, t, 0:half], m.mix[:, t, 0:half], m.gate[:, t, 0:half], ALU.mult))
        e2 = dve.mark(dve.after(sg, *mixed["dsa", t], *mixed["fox", t]).tensor_tensor(
            m.mix[:, t, half:D], m.mix[:, t, half:D], m.gate[:, t, half:D], ALU.mult))
        cols = slice(t * P, (t + 1) * P)
        for _ in core.transpose_cut(m.mix[:, t, :], D, m.xh[:, :, cols], m.xl[:, :, cols],
                                    (e1, e2), (proj_done,)):
            pass
        ready[t] = core.last

    sums = {}

    def add_residual(c):
        def run(t, ps, token):
            part = m.x[:, t, c * WC:(c + 1) * WC]
            end = dve.mark(dve.after(token).scalar_tensor_tensor(part, part, ALPHA, ps[:, :], ALU.mult, ALU.add))
            st = dve.mark(dve.after(end).bn_stats(m.bn[:, t, c * 6:(c + 1) * 6], part))
            sums[t] = (end, st)
            return [end]
        return run
    for c in range(2):
        for _ in core.project((m.xh, m.xl, lambda t: ready[t]), KD, range(NT), WC, add_residual(c)):
            pass
    for t in range(NT):
        ag = dve.mark(dve.after(*sums[t]).bn_aggr(m.mv[:, t, :], m.bn[:, t, :]))
        ve = dve.mark(dve.after(ag).tensor_scalar(m.mv[:, t, 1:2], m.mv[:, t, 1:2], EPS1, None, ALU.add))
        rs = pool.mark(pool.after(ve).tensor_tensor(m.rstd[:, t, :], m.mv[:, t, 1:2], m.half[:, 0:1], ALU.pow))
        xn = dve.mark(dve.after(rs).tensor_scalar(m.x[:, t, :], m.x[:, t, :], m.mv[:, t, 0:1], m.rstd[:, t, :],
                                                  ALU.subtract, ALU.mult))
        halves = ((dve, slice(0, 512)), (pool, slice(512, D)))
        for e, s in halves:
            g = e.mark(e.after(xn).tensor_tensor(m.x[:, t, s], m.x[:, t, s], ln_g[:, s], ALU.mult))
            e.mark(e.after(g).tensor_tensor(m.x[:, t, s], m.x[:, t, s], ln_b[:, s], ALU.add))


class Mem:
    pass


def first_block(core, io, shared):
    from contextlib import ExitStack
    nc = core.nc
    with ExitStack() as ctx:
        core.ctx, outer = ctx, core.ctx
        rings = list(core.rings)
        m = Mem()
        m.ident, m.ones, m.half, m.x = shared.ident, shared.ones, shared.half, shared.x
        core.piece_slots("1", 6, 4)
        m.xh, m.xl = core.sb("x_hi1", [P, KD, S], F32R), core.sb("x_lo1", [P, KD, S], F32R)
        m.par = core.sb("par1", [P, 388 + 2 * D])
        m.lprod, m.lam = core.sb("lam_prod", [P, 2, HD]), core.sb("lam", [P, 6])
        m.linit, m.gs = core.sb("lam_init", [P, 4]), core.sb("g_sub_scaled", [P, P])
        m.lconst = core.sb("lam_consts", [P, 2 * LAYERS])
        m.cos, m.sin = core.sb("cos1", [P, NT, HD]), core.sb("sin1", [P, NT, HD])
        m.mask, m.maskb = core.sb("causal_bias", [P, P]), core.sb("causal_bias_bf", [P, P], BF16)
        m.identb = core.sb("ident_bf", [P, P], BF16)
        m.tri = core.sb("tri", [P, P])
        m.rope = core.ring("rope_tmp", 1, [P, 2, 512])
        m.iq, m.sx, m.sv = core.sb("idx_q", [P, NT, 512]), core.sb("dsa_roped", [P, NT, 384]), core.sb("dsa_v_w_f", [P, NT, 76])
        m.dq, m.dk, m.dv = (core.sb(n, [P, NT, 512]) for n in ("diff_q", "diff_k", "diff_v"))
        m.fqk, m.fv = core.sb("fox_qk", [P, NT, 8, 66]), core.sb("fox_v", [P, NT, 256])
        m.gate, m.mix = core.sb("gate1", [P, NT, D]), core.sb("mix1", [P, NT, D])
        m.qa, m.ka = core.sb("q_t_a", [66, 8, S]), core.sb("k_t_a", [66, 4, S])
        m.qb, m.kb = core.sb("q_t_b", [HD, 8, S]), core.sb("k_t_b", [HD, 8, S])
        m.sk_t, m.sq_t = core.sb("dsa_k_t", [HD, 2, S]), core.sb("dsa_q_t", [HD, 4, S])
        m.iw, m.relu = core.sb("idx_w", [P, NT, 8]), core.ring("relu", 2, [P, 512])
        m.score, m.top8 = core.sb("idx_score", [P, NT, S]), core.sb("top8", [P, 8])
        m.sel = core.sb("sel_bias", [P, NT, S], BF16)
        m.sel_free = []
        m.out_free = []
        m.stat, m.prob, m.prob_t = core.ring("stat", 2, [P, 32]), core.ring("prob", 3, [P, 2, S]), core.ring("prob_t", 3, [P, 512])
        m.ms, m.ms2 = core.sb("ms", [P, NT, 4]), core.sb("ms_inv", [P, NT, 4])
        m.fz, m.fa, m.fe, m.fl, m.lf = (core.sb(n, [P, NT, 4]) for n in ("fox_z", "fox_abs", "fox_exp", "fox_ln", "fox_logf"))
        m.bn, m.mv, m.rstd = core.sb("bn1", [P, NT, 12]), core.sb("mean_var1", [P, NT, 2]), core.sb("rstd1", [P, NT, 1])
        got = core.small.start(1, m.cos[:, :, :], io["cos1"])
        core.small.start(1, m.sin[:, :, :], io["sin1"])
        core.small.start(1, m.mask[:, :], io["causal"])
        core.small.start(1, m.tri[:, :], io["tri"])
        got = core.small.start(1, m.lconst[:, :], io["lam_consts"])
        core.dve.mark(core.dve.after(got).tensor_copy(m.maskb[:, :], m.mask[:, :]))
        core.dve.mark(core.dve.after().tensor_copy(m.identb[:, :], m.ident[:, :]))
        core.restart()
        with nc.Fori(0, LAYERS) as layer:
            first_layer(core, layer, io, m)
            core.restart()
        core.ctx, core.rings = outer, rings


CONV, QK2, V2, RANK, HEADS2 = 512, 256, 512, 16, 4
SPLIT2 = [("val", CONV), ("glu", CONV), ("cgate", CONV), ("gla_q", QK2), ("gla_k", QK2),
          ("gla_v", V2), ("gla_g", V2), ("low_f", RANK), ("low_b", RANK), ("att_q", 512),
          ("att_k", P), ("att_v", P), ("att_g", 512), ("merge0", D), ("merge1", D), ("merge2", D)]
CHUNKS2 = [[("val", 0, 512)], [("glu", 0, 512)], [("cgate", 0, 512)],
           [("gla_k", 0, 256), ("att_k", 0, 128), ("att_v", 0, 128)],
           [("gla_v", 0, 512)],
           [("low_f", 0, 16), ("low_b", 0, 16), ("gla_q", 0, 256)],
           [("att_q", 0, 512)],
           [("merge0", 0, 512)], [("merge0", 512, 512)],
           [("gla_g", 0, 512)],
           [("merge1", 0, 512)], [("merge1", 512, 512)],
           [("att_g", 0, 512)],
           [("merge2", 0, 512)], [("merge2", 512, 512)]]
VAL, GLU, CGATE, KKV, GV, LRQ, AQ, M0A, M0B, GG, M1A, M1B, AG, M2A, M2B = range(len(CHUNKS2))
WIDTH2 = [sum(n for _, _, n in c) for c in CHUNKS2]
OFF2 = offsets(WIDTH2, D)
N_BIAS = len(CHUNKS2) - 3
OFFM = offsets([WC] * 6, D)
OFFY = offsets([WC] * 2, CONV)
TAPS, PAD = 31, 15
GC = 64
AH, AKV = 8, 2
X_TILES, C_TILES = (0, 1), (2, 3)
PAR_COLS = KD + 12 + 4 * TAPS + 4 + 4 + 4


def second_layer(core, layer, io, m):
    from contextlib import ExitStack
    nc, pe, act, dve, pool, sp, small = core.nc, core.pe, core.act, core.dve, core.pool, core.sp, core.small
    full = layer < LAYERS - 1
    tiles = X_TILES + C_TILES if full else X_TILES
    every = X_TILES + C_TILES
    n_tok = len(tiles) * P
    streams = [0, 1] if full else [0]

    def pieces(array, offs, c, width, n_k):
        at0 = offs[c]
        return [(array[layer, at0 + kp * P * KP * width:at0 + (kp + 1) * P * KP * width]
                 .rearrange("(p n) -> p n", p=P), width) for kp in range(n_k // KP)]
    for c in range(6):
        core.stream(pieces(io["wm2"], OFFM, c, WC, KD))
    order = [("in", c) for c in (VAL, GLU, CGATE, KKV, GV, LRQ)]
    order += [("in", M0A), ("conv", 0), ("in", M0B), ("conv", 1), ("in", GG)]
    order += [("in", AQ), ("in", M1A), ("gla", 0), ("in", M1B), ("gla", 1), ("in", AG)]
    order += [("in", M2A), ("att", 0), ("in", M2B), ("att", 1), ("out", 0), ("out", 1)]
    for kind, c in order:
        if kind == "in":
            core.stream(pieces(io["w2"], OFF2, c, WIDTH2[c], KD))
        elif kind == "out":
            core.stream(pieces(io["wo2"], OFFO, c, WC, KD))
        else:
            core.stream(pieces(io["wy_" + kind], OFFY, c, WC, CONV // P))

    par_in = small.start(4, m.par[:, :], io["par2"][layer])
    rows_in = small.start(4, m.rows[:, :], io["rows2"][layer, :].partition_broadcast(P))
    par_in = rows_in
    norm_g = m.par[:, 0:KD]
    b_conv = m.par[:, KD:KD + 12]
    taps = m.par[:, KD + 12:KD + 12 + 4 * TAPS].rearrange("p (c k) -> p c k", k=TAPS)
    o = KD + 12 + 4 * TAPS
    dw_b, cln_g, cln_b = (m.par[:, o + 4 * i:o + 4 * i + 4] for i in range(3))
    gla_g, qn_g, kn_g = m.rows[:, 0:P], m.rows[:, P:P + HD], m.rows[:, P + HD:P + 2 * HD]

    with ExitStack() as scope:
        core.ctx, outer = scope, core.ctx
        raw = core.sb(f"bias_raw{layer}", [96, WC])
        rest, part = core.sb(f"bias_rest{layer}", [96, WC]), core.sb(f"bias_part{layer}", [96, WC], BF16)
        z = dve.mark(dve.after(*core.fence()).memset(raw[:, :], 0.0))
        for i in range(3):
            bias_in = small.start(5, raw[32 * i:32 * i + N_BIAS, :], io["bias2"][layer], z)
        t0 = dve.mark(dve.after(bias_in).tensor_copy(part[:, :], raw[:, :]))
        b0 = dve.mark(dve.after(t0).tensor_copy(m.bias[0:32, :], part[0:32, :]))
        r1 = dve.mark(dve.after().tensor_tensor(rest[:, :], raw[:, :], part[:, :], ALU.subtract))
        t1 = dve.mark(dve.after(r1).tensor_copy(part[:, :], rest[:, :]))
        b1 = dve.mark(dve.after(t1).tensor_copy(m.bias[32:64, :], part[32:64, :]))
        r2 = dve.mark(dve.after().tensor_tensor(raw[:, :], rest[:, :], part[:, :], ALU.subtract))
        bias_ready = dve.mark(dve.after(r2).tensor_copy(m.bias[64:96, :], raw[64:96, :]))

        vec, cut_c = core.sb(f"mod_c{layer}", [P, KD, 2]), core.sb(f"mod_cut{layer}", [P, KD, P], F32R)
        modrow = core.sb(f"mod_rows{layer}", [5, 3 * D])
        c_in = small.start(6, vec[:, :, :], io["c2"], z)
        b_in = small.start(6, modrow[4:5, :], io["b_mod2"][layer:layer + 1, :], z)
        zc = pool.mark(pool.after(z).memset(cut_c[:, :, :].bitcast(F32), 0.0))
        sc = act.mark(act.after(c_in, b_in).activation(vec[:, :, :], vec[:, :, :], ACT.Silu))
        ch = dve.mark(dve.after(sc, zc).tensor_copy(cut_c[:, :, 0:2], vec[:, :, :]))
        cl = dve.mark(dve.after(ch).tensor_tensor(cut_c[:, :, 2:4], vec[:, :, :], cut_c[:, :, 0:2].bitcast(F32), ALU.subtract))
        for c in range(6):
            ps, free, slot = core.proj.take()
            for kp in range(KD // KP):
                hi, lo, cut = core.next_piece()
                pe.after(*cut, cl, *(free if kp == 0 else ()))
                for kk in range(KP):
                    k = kp * KP + kk
                    nc.tensor.matmul(ps[:, :], cut_c[:, k, :], hi[:, kk, :], start=k == 0, stop=False)
                    ins = nc.tensor.matmul(ps[:, :], cut_c[:, k, :], lo[:, kk, :], start=False, stop=k == KD - 1)
                token = pe.mark(ins)
                core.piece_used(token)
            mod_end = act.mark(act.after(token).activation(modrow[0:4, c * WC:(c + 1) * WC], ps[0:4, :], ACT.Copy))
            core.proj.free(slot, mod_end)
        ps, free, slot = core.aux.take()
        pe.after(mod_end, b_in, *free)
        for j in range(2 * KD):
            ins = nc.tensor.matmul(ps[:, 2 * j:2 * j + 2], modrow[0:5, j * P:(j + 1) * P], m.sel5[0:5, :, 0],
                                   start=True, stop=True)
        cols = pe.mark(ins)
        view = ps[:, 0:4 * KD].rearrange("p (a k s) -> p a k s", a=2, k=KD)
        sh = dve.mark(dve.after(cols).tensor_copy(m.shift[:, :, :], view[:, 0]))
        g2 = norm_g.unsqueeze(2).to_broadcast([P, KD, 2])
        s1 = dve.mark(dve.after(par_in).tensor_scalar(m.scale[:, :, :], view[:, 1], 1.0, None, ALU.add))
        core.aux.free(slot, s1)
        scale_ready = dve.mark(dve.after(s1).tensor_tensor(m.scale[:, :, :], m.scale[:, :, :], g2, ALU.mult))
        gate_row = act.mark(act.after(mod_end, b_in).activation(m.gate_row[:, :], modrow[:, 2 * D:3 * D], ACT.Copy))

        xn = core.ring(f"x_normed{layer}", 2, [P, D])
        mod = core.ring(f"x_mod{layer}", 2, [P, 4, P])
        ss = core.sb(f"sum_sq{layer}", [P, 8])
        hx = {}
        if layer == 0:
            ctx_in = small.start(7, m.acc[:, 2:4, :], io["ctx2"].rearrange("(t p) d -> p t d", p=P))
        else:
            ctx_in = None
        for t in every:
            src = m.x[:, t, :] if t < 2 else m.acc[:, t, :]
            s = t // 2
            buf, free, slot = xn.take()
            sq = act.mark(act.after(ctx_in, *free, *core.x_ready).activation(buf, src, ACT.Square, accum_out=ss[:, t:t + 1]))
            mean = dve.mark(dve.after(sq).tensor_scalar(ss[:, 4 + t:5 + t], ss[:, t:t + 1], 1.0 / D, EPS2, ALU.mult, ALU.add))
            rinv = pool.mark(pool.after(mean).tensor_tensor(ss[:, t:t + 1], ss[:, 4 + t:5 + t], m.half[:, 0:1], ALU.pow))
            norm = dve.mark(dve.after(rinv, sq).tensor_scalar(buf, src, ss[:, t:t + 1], None, ALU.mult))
            ends = []
            for b in range(0, KD, 4):
                ps, token, pslot = core.transpose([buf[:, (b + i) * P:(b + i + 1) * P] for i in range(4)], [norm])
                view = ps[:, :].rearrange("p (k t) -> p k t", k=4)
                tmp, tfree, tslot = mod.take()
                sc_b = m.scale[:, b:b + 4, s:s + 1].to_broadcast([P, 4, P])
                sh_b = m.shift[:, b:b + 4, s:s + 1].to_broadcast([P, 4, P])
                a1 = dve.mark(dve.after(token, scale_ready, *tfree).tensor_tensor(tmp, view, sc_b, ALU.mult))
                core.aux.free(pslot, a1)
                a2 = pool.mark(pool.after(a1, sh).tensor_tensor(tmp, tmp, sh_b, ALU.add))
                hi, lo = m.xh[:, b:b + 4, t * P:(t + 1) * P], m.xl[:, b:b + 4, t * P:(t + 1) * P]
                a3 = act.mark(act.after(a2).activation(hi, tmp, ACT.Copy))
                a4 = dve.mark(dve.after(a3).tensor_tensor(lo, tmp, hi.bitcast(F32), ALU.subtract))
                mod.free(tslot, a4)
                ends += [a3, a4]
            xn.free(slot, token)
            hx[t] = ends
        core.rings.remove(xn), core.rings.remove(mod)
        core.ctx = outer
    hx_all = [x for t in tiles for x in hx[t]]
    xs = (m.xh, m.xl, lambda t: hx[t])
    got = {}
    pre_fence = core.fence()

    def bias_of(c):
        def add(out, w):
            nc.tensor.matmul(out, m.sel[:, c - 3, :], m.bias[0:96, 0:w], start=True, stop=False)
        return add

    def need(*keys):
        while not all(k in got for k in keys):
            yield

    def toks(*keys):
        return [x for k in keys for x in got[k]]

    shape = {}

    def ev_val(j, ps, token):
        e = act.mark(act.after(token, *pre_fence).activation(m.cv[:, j, 0:n_tok], ps[:, 0:n_tok], ACT.Identity, bias=b_conv[:, j:j + 1]))
        got["val", j] = [e]
        return [e]

    def ev_glu(j, ps, token):
        e = act.mark(act.after(token, *pre_fence).activation(m.cg[:, j, 0:n_tok], ps[:, 0:n_tok], ACT.Sigmoid, bias=b_conv[:, 4 + j:5 + j]))
        u = m.u[:, j, 0:len(streams), PAD:PAD + S]
        w = lambda b: b[:, j, 0:n_tok].rearrange("p (s t) -> p s t", t=S)
        e2 = pool.mark(pool.after(e, *toks(("val", j)), got["u_zero"]).tensor_tensor(u, w(m.cv), w(m.cg), ALU.mult))
        got["u", j] = [e2]
        return [e]

    def ev_cgate(j, ps, token):
        e = act.mark(act.after(token, *toks(("u", j))).activation(m.cg[:, j, 0:n_tok], ps[:, 0:n_tok], ACT.Silu, bias=b_conv[:, 8 + j:9 + j]))
        got["cg", j] = [e]
        return [e]

    def ev_kkv(t, ps, token):
        e = act.mark(act.after(token).activation(m.kkv[:, t, :], ps[:, :], ACT.Copy))
        got[KKV, t] = [e]
        return [e]

    def ev_gv(t, ps, token):
        e = act.mark(act.after(token).activation(m.gv[:, t, :], ps[:, :], ACT.Copy))
        got[GV, t] = [e]
        return [e]

    def ev_lrq(t, ps, token):
        w = 288 if t in tiles else 32
        e = dve.mark(dve.after(token).tensor_copy(m.lrq[:, t, 0:w], ps[:, 0:w]))
        got[LRQ, t] = [e]
        return [e]

    def ev_aq(t, ps, token):
        e = act.mark(act.after(token, *toks("gla_gated"), got["go_read"]).activation(m.aq[:, t, :], ps[:, :], ACT.Copy))
        got[AQ, t] = [e]
        return [e]

    def ev_sigma(t, ps, token):
        e = act.mark(act.after(token, *got.get(("sigma_read", t), ())).activation(m.sigma[:, t, :], ps[:, :], ACT.Sigmoid))
        got["sigma", t] = [e]
        return [e]

    def ev_y(branch, c):
        def run(t, ps, token):
            out = m.acc[:, t, c * WC:(c + 1) * WC]
            if branch == 0:
                e = dve.mark(dve.after(token, *toks(("sigma", t)), *pre_fence).tensor_tensor(out, ps[:, :], m.sigma[:, t, :], ALU.mult))
                got["sigma_read", t] = [e]
                got["acc", t, c] = [e]
                return [e]
            e = dve.mark(dve.after(token, *toks(("sigma", t))).tensor_tensor(m.sigma[:, t, :], ps[:, :], m.sigma[:, t, :], ALU.mult))
            e2 = pool.mark(pool.after(e, *toks(("acc", t, c))).tensor_tensor(out, out, m.sigma[:, t, :], ALU.add))
            got["sigma_read", t] = [e2]
            got["acc", t, c] = [e2]
            return [e]
        return run

    def ev_gate(o_buf, key):
        def run(t, ps, token):
            g, free, slot = m.gtmp.take()
            e = act.mark(act.after(token, *free).activation(g, ps[:, :], ACT.Silu))
            e2 = pool.mark(pool.after(e, *toks((key, t))).tensor_tensor(o_buf()[:, t, :], o_buf()[:, t, :], g, ALU.mult))
            m.gtmp.free(slot, e2)
            cols = slice(t * P, (t + 1) * P)
            for _ in core.transpose_cut(o_buf()[:, t, :], 512, m.yh[:, :, cols], m.yl[:, :, cols], [e2], toks("y_read")):
                pass
            got["y", t] = core.last
            got["go_read"] = (pe.sem, pe.count)
            return [e]
        return run

    def main():
        for c, ev in ((VAL, ev_val), (GLU, ev_glu), (CGATE, ev_cgate)):
            yield from core.project_t((m.xh, m.xl, hx_all), KD, n_tok, ev)
        def inp(c, tt, ev, **kw):
            yield from core.project(xs, KD, tt, WIDTH2[c], ev, bias_of(c), **kw)
        def y_out(branch, c):
            yield from core.project((m.yh, m.yl, lambda t: got["y", t]), CONV // P, tiles, WC, ev_y(branch, c))
            got["y_read"] = [core.done[-1]]
        yield from inp(KKV, every, ev_kkv)
        yield from inp(GV, every, ev_gv)
        yield from inp(LRQ, every, ev_lrq, width_of=lambda t: 288 if t in tiles else 32)
        yield from inp(M0A, tiles, ev_sigma)
        yield lambda: ("conv_cut" in got)
        for t in tiles:
            got["y", t] = got["conv_cut"]
        yield from y_out(0, 0)
        yield from inp(M0B, tiles, ev_sigma)
        yield from y_out(0, 1)
        yield lambda: all(("gla_o", t) in got for t in tiles)
        yield from inp(GG, tiles, ev_gate(lambda: m.go, "gla_o"))
        got["gla_gated"] = toks(*[("y", t) for t in tiles])
        yield from inp(AQ, tiles, ev_aq)
        yield from inp(M1A, tiles, ev_sigma)
        yield from y_out(1, 0)
        yield from inp(M1B, tiles, ev_sigma)
        yield from y_out(1, 1)
        yield lambda: all(("att_o", t) in got for t in tiles)
        yield from inp(AG, tiles, ev_gate(lambda: m.ao, "att_o"))
        yield from inp(M2A, tiles, ev_sigma)
        yield from y_out(2, 0)
        yield from inp(M2B, tiles, ev_sigma)
        yield from y_out(2, 1)
        got["main_end"] = []

    n_st = len(streams)

    def conv():
        yield from need(*[("cg", j) for j in range(4)])
        end = {}
        for k in range(TAPS):
            for j in range(4):
                src = m.u[:, j, 0:n_st, k:k + S]
                out = m.cv[:, j, 0:n_tok].rearrange("p (s t) -> p s t", t=S)
                if k == 0:
                    end[j] = dve.mark(dve.after(*toks(("u", j)), par_in).tensor_scalar(
                        out, src, taps[:, j, k:k + 1], dw_b[:, j:j + 1], ALU.mult, ALU.add))
                else:
                    end[j] = dve.mark(dve.after(end[j]).scalar_tensor_tensor(
                        out, src, taps[:, j, k:k + 1], out, ALU.mult, ALU.add))
            yield
        ps, free, slot = core.aux.take()
        pe.after(*end.values(), *free)
        for j in range(4):
            ins = nc.tensor.matmul(ps[:, 0:n_tok], m.mean_w[:, :], m.cv[:, j, 0:n_tok], start=j == 0, stop=j == 3)
        mu = pe.mark(ins)
        stat = m.cstat
        c = act.mark(act.after(mu).activation(stat[:, 0, 0:n_tok], ps[:, 0:n_tok], ACT.Copy))
        core.aux.free(slot, c)
        yield
        sqs = []
        for j in range(4):
            d = dve.mark(dve.after(c).tensor_tensor(m.cv[:, j, 0:n_tok], m.cv[:, j, 0:n_tok], stat[:, 0, 0:n_tok], ALU.subtract))
            end[j] = d
            sqs.append(pool.mark(pool.after(d).tensor_tensor(m.u2[:, j, 0:n_tok], m.cv[:, j, 0:n_tok], m.cv[:, j, 0:n_tok], ALU.mult)))
            yield
        ps, free, slot = core.aux.take()
        pe.after(*sqs, *free)
        for j in range(4):
            ins = nc.tensor.matmul(ps[:, 0:n_tok], m.mean_w[:, :], m.u2[:, j, 0:n_tok], start=j == 0, stop=j == 3)
        var = pe.mark(ins)
        ve = dve.mark(dve.after(var).tensor_scalar(stat[:, 1, 0:n_tok], ps[:, 0:n_tok], EPS2, None, ALU.add))
        core.aux.free(slot, ve)
        sd = act.mark(act.after(ve).activation(stat[:, 1, 0:n_tok], stat[:, 1, 0:n_tok], ACT.Sqrt))
        rs = dve.mark(dve.after(sd).reciprocal(stat[:, 1, 0:n_tok], stat[:, 1, 0:n_tok]))
        yield
        cut = []
        for j in range(4):
            w = m.cv[:, j, 0:n_tok]
            n = dve.mark(dve.after(rs, end[j]).tensor_tensor(w, w, stat[:, 1, 0:n_tok], ALU.mult))
            a = act.mark(act.after(n).activation(w, w, ACT.Silu, scale=cln_g[:, j:j + 1], bias=cln_b[:, j:j + 1]))
            g = pool.mark(pool.after(a, *toks(("cg", j))).tensor_tensor(w, w, m.cg[:, j, 0:n_tok], ALU.mult))
            hi, lo = m.yh[:, j, 0:n_tok], m.yl[:, j, 0:n_tok]
            h = act.mark(act.after(g).activation(hi, w, ACT.Copy))
            l = dve.mark(dve.after(h).tensor_tensor(lo, w, hi.bitcast(F32), ALU.subtract))
            cut += [h, l]
            yield
        got["conv_cut"] = cut

    def gla():
        fence = core.fence()
        yield from need(*[(c, t) for c in (KKV, GV, LRQ) for t in every])
        zw = pool.mark(pool.after(*fence).memset(m.wup[:, :], 0.0))
        for d in range(2):
            small.start(8, m.wup[d * RANK:(d + 1) * RANK, d * QK2:(d + 1) * QK2], io["w_gate2"][layer, d], zw)
        wup_in = small.start(8, m.wup[2 * RANK:2 * RANK + 1, :], io["b_gate2"][layer:layer + 1, :], zw)
        one = dve.mark(dve.after(*fence).memset(m.lr_t[32:33, :], 1.0))
        za = pool.mark(pool.after(*fence).memset(m.att[:, :, :, :, :], 0.0))
        z0 = pool.mark(pool.after(*fence).memset(m.st[:, :, :, 0, :], 0.0))
        ps, free, slot = core.aux.take()
        pe.after(*toks(*[(LRQ, t) for t in every]), *free)
        for t in every:
            ins = nc.tensor.transpose(ps[0:32, t * P:(t + 1) * P], m.lrq[:, t, 0:32], m.ident[:, :])
        tr = pe.mark(ins)
        lr = act.mark(act.after(tr, *fence).activation(m.lr_t[0:32, :], ps[0:32, :], ACT.Copy))
        core.aux.free(slot, lr)
        yield
        state = {}
        last_state = None
        inter_read = []

        def gates(t):
            i = t % 2
            out = t in tiles
            ps, free, slot = core.aux.take()
            zt = pe.mark(pe.after(lr, one, wup_in, *free).matmul(ps[:, :], m.lr_t[0:33, t * P:(t + 1) * P], m.wup[0:33, :], start=True, stop=True))
            e = act.mark(act.after(zt, *fence, *state.get("tmp_read", ())).activation(m.e3[:, i, :], ps[:, :], ACT.Abs))
            e = act.mark(act.after(e).activation(m.e3[:, i, :], m.e3[:, i, :], ACT.Exp, scale=-1.0))
            e = act.mark(act.after(e).activation(m.e3[:, i, :], m.e3[:, i, :], ACT.Ln, bias=1.0))
            la = dve.mark(dve.after(e, *fence, *state.get("la_read", ())).scalar_tensor_tensor(
                m.la[:, :], ps[:, :], 0.0, m.e3[:, i, :], ALU.min, ALU.subtract))
            core.aux.free(slot, la)
            yield
            ps1, free1, slot1 = core.aux.take()
            pe.after(la, *free1)
            for d in range(2):
                ins = nc.tensor.matmul(ps1[:, d * QK2:(d + 1) * QK2], m.tri2[:, d, :], m.la[:, d * QK2:(d + 1) * QK2], start=True, stop=True)
            cum = pe.mark(ins)
            ps2, free2, slot2 = core.aux.take()
            pe.after(*free2)
            for d in range(2):
                ins = nc.tensor.matmul(ps2[:, d * QK2:(d + 1) * QK2], m.tri2[:, 2 + d, :], m.la[:, d * QK2:(d + 1) * QK2], start=True, stop=True)
            left = pe.mark(ins)
            ps3, free3, slot3 = core.aux.take()
            pe.after(*free3)
            for dp in range(4):
                ins = nc.tensor.matmul(ps3[:, 2 * dp:2 * dp + 2], m.la[:, dp * P:(dp + 1) * P], m.halves[:, :], start=True, stop=True)
            tot = pe.mark(ins)
            state["la_read"] = [tot]
            n = 1.0 / 16.0
            dec = act.mark(act.after(tot, *state.get("dec_read", ())).activation(
                m.dec[:, :, 2 * i:2 * i + 2], ps3[:, 0:8].rearrange("p (a b) -> p a b", b=2), ACT.Exp, scale=n))
            core.aux.free(slot3, dec)
            if out:
                e1 = act.mark(act.after(cum, *state.get("tmp_read", ())).activation(m.e1[:, :], ps1[:, :], ACT.Exp, scale=n))
                e2 = act.mark(act.after().activation(m.e2[:, :], ps1[:, :], ACT.Exp, scale=-n))
                core.aux.free(slot1, e2)
            else:
                core.aux.free(slot1, cum)
            e3 = act.mark(act.after(left, la).activation(m.e3[:, i, :], ps2[:, :], ACT.Exp, scale=n))
            core.aux.free(slot2, e3)
            v = lambda b: b.rearrange("p (d n) -> p d n", d=2)
            k_b = spread(m.kkv[:, t, 0:QK2], [P, 2, QK2])
            ks = pool.mark(pool.after(e3, *toks((KKV, t))).tensor_tensor(v(m.e3[:, i, :]), v(m.e3[:, i, :]), k_b, ALU.mult))
            state["ks", t] = ks
            yield
            if out:
                q_b = spread(m.lrq[:, t, 32:32 + QK2], [P, 2, QK2])
                qi = dve.mark(dve.after(e1, *toks((LRQ, t))).scalar_tensor_tensor(v(m.e1[:, :]), q_b, GC ** -0.5, v(m.e1[:, :]), ALU.mult, ALU.mult))
                ki = pool.mark(pool.after(e2).tensor_tensor(v(m.e2[:, :]), v(m.e2[:, :]), k_b, ALU.mult))
                ps, tok_q, slot = core.transpose([m.e1[:, dp * P:(dp + 1) * P] for dp in range(4)], [qi])
                view = ps[:, :].rearrange("p (a t) -> p a t", a=4)
                qt = act.mark(act.after(tok_q, *fence, *inter_read).activation(m.q_t[:, :, i, :], view, ACT.Copy))
                core.aux.free(slot, qt)
                ps, tok_k, slot = core.transpose([m.e2[:, dp * P:(dp + 1) * P] for dp in range(4)], [ki])
                kt = dve.mark(dve.after(tok_k, *fence, tot).tensor_copy(m.k_t[:, :], ps[:, :]))
                core.aux.free(slot, kt)
                state["tmp_read"] = [tok_q, tok_k]
                yield
                for par in range(2):
                    ps, free, slot = core.aux.take()
                    rows = slice(par * HD, (par + 1) * HD)
                    pe.after(qt, kt, *free)
                    for dp in range(4):
                        ins = nc.tensor.matmul(ps[:, dp * P:(dp + 1) * P], m.k_t[rows, dp * P:(dp + 1) * P],
                                               m.q_t[rows, dp, i, :], start=True, stop=True)
                    a = pe.mark(ins)
                    am = dve.mark(dve.after(a, za, *inter_read).copy_predicated(m.att[:, i, par, :, :], m.gmask[:, :, :],
                                                                     ps[:, :].rearrange("p (a t) -> p a t", a=4)))
                    core.aux.free(slot, am)
                    state["att", t, par] = am
                state["la_read"] = [a]
                yield

        for s in (1, 0):
            tl = C_TILES if s else X_TILES
            out = tl[0] in tiles
            for t in tl:
                yield from gates(t)
            upd = last_state or [z0]
            for step in range(4):
                psd = []
                for d in range(2):
                    c = step if d == 0 else 3 - step
                    i, half = c // 2, c % 2
                    rows = slice(half * GC, (half + 1) * GC)
                    ps, free, slot = core.aux.take()
                    pe.after(state["ks", tl[i]], *free, *toks((GV, tl[i])))
                    for h in range(HEADS2):
                        par, pair = h % 2, h // 2
                        ins = nc.tensor.matmul(ps[par * HD:(par + 1) * HD, pair * P:(pair + 1) * P],
                                               m.e3[rows, i, d * QK2 + h * HD:d * QK2 + (h + 1) * HD],
                                               m.gv[rows, tl[i], h * P:(h + 1) * P], start=True, stop=True)
                    con = pe.mark(ins)
                    ends = []
                    for pair in range(2):
                        ends.append(dve.mark(dve.after(con, *upd, *inter_read, dec_tok(state)).scalar_tensor_tensor(
                            m.st[:, d, pair, step + 1, :], m.st[:, d, pair, step, :],
                            m.dec[:, 2 * d + pair, c:c + 1], ps[:, pair * P:(pair + 1) * P], ALU.mult, ALU.add)))
                    core.aux.free(slot, ends[-1])
                    psd += ends
                upd = psd
                yield
            state["dec_read"] = upd
            state["tmp_read"] = state.get("tmp_read", []) + [con]
            if out:
                for t in tl:
                    i = t % 2
                    be, fe, se = core.aux.take()
                    bo, fo, so = core.sum_bank.take()
                    pe.after(*fe, *fo, *upd, state["att", t, 0], state["att", t, 1])
                    for h in range(HEADS2):
                        par, pair = h % 2, h // 2
                        bk = (be, bo)[par][:, pair * P:(pair + 1) * P]
                        rows = slice(par * HD, (par + 1) * HD)
                        v_h = m.gv[:, t, h * P:(h + 1) * P]
                        for d in range(2):
                            nc.tensor.matmul(bk, m.att[:, i, par, 2 * d + pair, :], v_h, start=d == 0, stop=False)
                        for d in range(2):
                            for half in range(2):
                                c = 2 * i + half
                                step = c if d == 0 else 3 - c
                                hs = slice(half * GC, (half + 1) * GC)
                                ins = nc.tensor.matmul(bk[hs, :], m.q_t[rows, 2 * d + pair, i, hs],
                                                       m.st[rows, d, pair, step, :], start=False, stop=d == 1)
                    token = pe.mark(ins)
                    inter_read = [token]
                    og = m.go[:, t, :].rearrange("p (a b n) -> p a b n", a=2, b=2)
                    bv = lambda b: b[:, 0:256].rearrange("p (a n) -> p a n", a=2)
                    o1 = act.mark(act.after(token, *fence).activation(og[:, :, 0, :], bv(be), ACT.Copy))
                    o2 = dve.mark(dve.after(token, *fence).tensor_copy(og[:, :, 1, :], bv(bo)))
                    core.aux.free(se, o1)
                    core.sum_bank.free(so, o2)
                    yield
                    g, gf, gs = m.gtmp.take()
                    sq = pool.mark(pool.after(o1, o2, *gf).tensor_tensor(g, m.go[:, t, :], m.go[:, t, :], ALU.mult))
                    sm = dve.mark(dve.after(sq).tensor_reduce(m.gms[:, t, 0:4], g.rearrange("p (h n) -> p h n", h=4), AXX, ALU.add))
                    m.gtmp.free(gs, sm)
                    me = dve.mark(dve.after(sm).tensor_scalar(m.gms[:, t, 4:8], m.gms[:, t, 0:4], 1.0 / P, EPS2, ALU.mult, ALU.add))
                    iv = pool.mark(pool.after(me).tensor_tensor(m.gms[:, t, 0:4], m.gms[:, t, 4:8], m.half[:, 0:4], ALU.pow))
                    ov = m.go[:, t, :].rearrange("p (h n) -> p h n", h=4)
                    n1 = pool.mark(pool.after(iv, rows_in).tensor_tensor(ov, ov, spread(gla_g, [P, 4, P]), ALU.mult))
                    n2 = dve.mark(dve.after(n1).tensor_tensor(ov, ov, m.gms[:, t, 0:4].unsqueeze(2).to_broadcast([P, 4, P]), ALU.mult))
                    got["gla_o", t] = [n2]
                    yield
            if s == 1:
                cp = pool.mark(pool.after(*upd, *inter_read).tensor_copy(m.st[:, :, :, 0, :], m.st[:, :, :, 4, :]))
                last_state = [cp] + upd
                inter_read = inter_read + [cp]

    def dec_tok(state):
        return (act.sem, act.count)

    def norm_rope(src, heads, g, t, ready, roped):
        v = src.rearrange("p (h d) -> p h d", d=HD)
        n = heads * HD
        tmp, free, slot = m.ropet.take()
        a, b = tmp[:, 0, 0:n], tmp[:, 1, 0:n]
        st = m.ams
        sq = pool.mark(pool.after(*ready, *free).tensor_tensor(a, src, src, ALU.mult))
        sm = dve.mark(dve.after(sq, *got.get("ams_read", ())).tensor_reduce(st[:, 0, 0:heads], a.rearrange("p (h d) -> p h d", d=HD), AXX, ALU.add))
        me = dve.mark(dve.after(sm).tensor_scalar(st[:, 1, 0:heads], st[:, 0, 0:heads], 1.0 / HD, EPS2, ALU.mult, ALU.add))
        iv = pool.mark(pool.after(me).tensor_tensor(st[:, 2, 0:heads], st[:, 1, 0:heads], m.half[:, 0:heads], ALU.pow))
        n1 = pool.mark(pool.after(rows_in).tensor_tensor(v, v, spread(g, [P, heads, HD]), ALU.mult))
        n2 = dve.mark(dve.after(iv, n1).tensor_tensor(v, v, st[:, 2, 0:heads].unsqueeze(2).to_broadcast([P, heads, HD]), ALU.mult))
        got["ams_read"] = [n2]
        if not roped:
            m.ropet.free(slot, n2)
            return n2
        q = HD // 4
        w = lambda x: x.rearrange("p (h a b i) -> p h a b i", a=2, b=2, i=q)
        av = a.rearrange("p (h d) -> p h d", d=HD)
        one = dve.mark(dve.after(n2, sm).tensor_tensor(av, v, spread(m.cos[:, t, :], [P, heads, HD]), ALU.mult))
        sn = m.sin[:, t, :].rearrange("p (a b i) -> p a b i", a=2, b=2)
        for x in range(2):
            for half in range(2):
                two = dve.mark(dve.after().tensor_tensor(
                    w(b)[:, :, x, half, :], w(src)[:, :, x, 1 - half, :], spread(sn[:, x, half, :], [P, heads, q]), ALU.mult))
        end = pool.mark(pool.after(two).tensor_tensor(src, a, b, ALU.add))
        m.ropet.free(slot, end)
        return end

    def att():
        fence = core.fence() + toks("gla_gated")
        for e in (act, dve, pool):
            e.after(*fence)
        yield from need(*[(AQ, t) for t in tiles])
        k_end, q_end = {}, {}
        for t in every:
            k_end[t] = norm_rope(m.kkv[:, t, QK2:QK2 + P], AKV, kn_g, t, toks((KKV, t)), t < 2)
            yield
        for t in tiles:
            q_end[t] = norm_rope(m.aq[:, t, :], AH, qn_g, t, toks((AQ, t)), t < 2)
            yield
        def flipped(src, heads, tl, dst, scale, ready):
            ends = []
            for h in range(heads):
                ps, free, slot = core.aux.take()
                pe.after(*ready, *free)
                for i, t in enumerate(tl):
                    ins = nc.tensor.transpose(ps[0:HD, i * P:(i + 1) * P], src(h, t), m.ident[:, :])
                token = pe.mark(ins)
                n = len(tl) * P
                if h % 2:
                    e = act.mark(act.after(token).activation(dst[:, h, 0:n], ps[0:HD, 0:n], ACT.Copy, scale=scale))
                else:
                    e = dve.mark(dve.after(token).tensor_scalar(dst[:, h, 0:n], ps[0:HD, 0:n], scale, None, ALU.mult))
                core.aux.free(slot, e)
                ends.append(e)
                yield
            core.last = ends
        yield from flipped(lambda h, t: m.kkv[:, t, QK2 + h * HD:QK2 + (h + 1) * HD], AKV, every, m.ak_t, 1.0, list(k_end.values()))
        kt = core.last
        yield from flipped(lambda h, t: m.aq[:, t, h * HD:(h + 1) * HD], AH, tiles, m.aq_t, HD ** -0.5, list(q_end.values()))
        ready = kt + core.last
        for qt in tiles:
            key_tiles = every if qt < 2 else C_TILES
            keys = len(key_tiles) * P
            k0 = key_tiles[0] * P
            n_maps = 512 // keys
            osum, ofree, oslot = core.sum_bank.take()
            stat, sfree, sslot = m.astat.take()
            top_of, sum_of, inv_of = (stat[:, i * AH:(i + 1) * AH] for i in range(3))
            st = {}

            def scores(j):
                ps, free, slot = core.aux.take()
                pe.after(*ready, *free)
                for i in range(n_maps):
                    h = j * n_maps + i
                    ins = nc.tensor.matmul(ps[:, i * keys:(i + 1) * keys], m.aq_t[:, h, qt * P:(qt + 1) * P],
                                           m.ak_t[:, h // (AH // AKV), k0:k0 + keys], start=True, stop=True)
                st[j] = [ps, slot, pe.mark(ins)]

            def soft(j):
                ps, slot, token = st[j]
                h = j * n_maps
                view = ps[:, :].rearrange("p (a b) -> p a b", a=n_maps)
                top = dve.mark(dve.after(token, *sfree).tensor_reduce(top_of[:, h:h + n_maps], view, AXX, ALU.max, negate=True))
                pm, free, pslot = m.aprob.take()
                act.after(top, *free)
                for i in range(n_maps):
                    end = act.mark(nc.scalar.activation(pm[:, i * keys:(i + 1) * keys], ps[:, i * keys:(i + 1) * keys], ACT.Exp,
                                                        bias=top_of[:, h + i:h + i + 1], accum_out=sum_of[:, h + i:h + i + 1]))
                core.aux.free(slot, end)
                st["inv"] = dve.mark(dve.after(end).reciprocal(inv_of[:, h:h + n_maps], sum_of[:, h:h + n_maps]))
                st[j] = [pm, pslot, end]

            def flip(j):
                pm, pslot, end = st[j]
                ps, token, slot = core.transpose([pm[:, b * P:(b + 1) * P] for b in range(4)], [end])
                m.aprob.free(pslot, token)
                pt, pfree, ptslot = m.aprob_t.take()
                if j % 2:
                    end = act.mark(act.after(token, *pfree).activation(pt, ps[:, :], ACT.Copy))
                else:
                    end = dve.mark(dve.after(token, *pfree).tensor_copy(pt, ps[:, :]))
                core.aux.free(slot, end)
                st[j] = [pt, ptslot, end]

            def values(j):
                pt, ptslot, end = st[j]
                pe.after(end, *(ofree if j == 0 else ()))
                nb = len(key_tiles)
                for i in range(n_maps):
                    h = j * n_maps + i
                    kh = h // (AH // AKV)
                    for b, t in enumerate(key_tiles):
                        ins = nc.tensor.matmul(osum[:, h * HD:(h + 1) * HD], pt[:, (i * nb + b) * P:(i * nb + b + 1) * P],
                                               m.kkv[:, t, QK2 + P + kh * HD:QK2 + P + (kh + 1) * HD],
                                               start=b == 0, stop=b == nb - 1)
                st["sum"] = pe.mark(ins)
                m.aprob_t.free(ptslot, st["sum"])
            yield from pipeline(list(range(AH // n_maps)), [scores, soft, flip, values])
            end = dve.mark(dve.after(st["sum"], st["inv"]).tensor_tensor(
                m.ao[:, qt, :].rearrange("p (h d) -> p h d", d=HD), osum[:, :].rearrange("p (h d) -> p h d", d=HD),
                inv_of.unsqueeze(2).to_broadcast([P, AH, HD]), ALU.mult))
            m.astat.free(sslot, end)
            core.sum_bank.free(oslot, end)
            got["att_o", qt] = [end]
            yield

    with ExitStack() as scope:
        core.ctx, outer = scope, core.ctx
        base_rings = list(core.rings)

        def open_conv(ctx):
            core.ctx = ctx
            m.u = core.sb(f"conv_u{layer}", [P, 4, 2, S + 2 * PAD])
            m.u2 = core.sb(f"conv_sq{layer}", [P, 4, 2 * S])
            m.cv, m.cg = core.sb(f"conv_v{layer}", [P, 4, 2 * S]), core.sb(f"conv_g{layer}", [P, 4, 2 * S])
            m.cstat = core.sb(f"conv_stat{layer}", [P, 2, 2 * S])
            core.ctx = outer

        def open_gla(ctx):
            core.ctx = ctx
            m.wup, m.lr_t = core.sb(f"w_up{layer}", [33, 512]), core.sb(f"low_t{layer}", [33, 512])
            m.att = core.sb(f"gla_att{layer}", [P, 2, 2, 4, P])
            m.st = core.sb(f"gla_state{layer}", [P, 2, 2, 5, P])
            m.la, m.e1, m.e2 = (core.sb(f"{n}{layer}", [P, 512]) for n in ("gla_la", "gla_e1", "gla_e2"))
            m.e3 = core.sb(f"gla_k_state{layer}", [P, 2, 512])
            m.q_t, m.k_t = core.sb(f"gla_q_t{layer}", [P, 4, 2, P]), m.la
            m.dec, m.gms = core.sb(f"gla_decay{layer}", [P, 4, 4]), core.sb(f"gla_ms{layer}", [P, 4, 8])
            m.go = m.aq
            core.ctx = outer

        def open_att(ctx):
            core.ctx = ctx
            m.aq_t, m.ak_t = core.sb(f"att_q_t{layer}", [HD, AH, 512]), core.sb(f"att_k_t{layer}", [HD, AKV, 512])
            m.aprob, m.aprob_t = core.ring(f"att_p{layer}", 3, [P, 512]), core.ring(f"att_pt{layer}", 2, [P, 512])
            m.astat, m.ams = core.ring(f"att_stat{layer}", 2, [P, 24]), core.sb(f"att_ms{layer}", [P, 3, 8])
            m.ropet = core.ring(f"att_rope{layer}", 1, [P, 2, 512])
            m.ao = m.aq
            core.ctx = outer

        conv_scope = ExitStack()
        open_conv(conv_scope)
        got["u_zero"] = pool.mark(pool.after(*pre_fence).memset(m.u[:, :, :, :], 0.0))

        def side():
            yield from conv()
            conv_scope.close()
            with ExitStack() as c:
                open_gla(c)
                yield from gla()
                yield from need("gla_gated")
            with ExitStack() as c:
                open_att(c)
                yield from att()
                yield from need("main_end")
        sd = side()
        weave(main(), sd, io.get("ratio2", 1.0) if False else RATIO2[layer])

    proj_done = core.done[-1]
    fence = core.fence()
    ready = {}
    for t in tiles:
        cols = slice(t * P, (t + 1) * P)
        for _ in core.transpose_cut(m.acc[:, t, :], D, m.xh[:, :, cols], m.xl[:, :, cols],
                                    toks(("acc", t, 0), ("acc", t, 1)), (proj_done,)):
            pass
        ready[t] = core.last
    flipped = core.fence()
    gates = []
    for s in streams:
        for c in range(2):
            ps, free, slot = core.aux.take()
            pe.after(gate_row, *free)
            token = pe.mark(nc.tensor.matmul(ps[:, :], m.sel5[0:5, s, :], m.gate_row[0:5, c * WC:(c + 1) * WC], start=True, stop=True))
            e = act.mark(act.after(token, *flipped).activation(m.acc[:, s, c * WC:(c + 1) * WC], ps[:, :], ACT.Copy))
            core.aux.free(slot, e)
            gates.append(e)
    if full:
        ctx_again = small.start(9, m.acc[:, 2:4, :], io["ctx2"].rearrange("(t p) d -> p t d", p=P), *flipped)
    else:
        ctx_again = None
    ends = []

    def add_gated(c):
        def run(t, ps, token):
            cs = slice(c * WC, (c + 1) * WC)
            g, free, slot = m.gtmp.take()
            dst = m.x[:, t, cs] if t < 2 else m.acc[:, t, cs]
            e = dve.mark(dve.after(token, *gates, *free).tensor_tensor(g, ps[:, :], m.acc[:, t // 2, cs], ALU.mult))
            e2 = pool.mark(pool.after(e, ctx_again).tensor_tensor(dst, dst, g, ALU.add))
            m.gtmp.free(slot, e2)
            ends.append(e2)
            if not full:
                small.start(10, io["y"].rearrange("(t p) d -> p t d", p=P)[:, t, cs], dst, e2)
            return [e]
        return run
    for c in range(2):
        for _ in core.project((m.xh, m.xl, lambda t: ready[t]), KD, tiles, WC, add_gated(c)):
            pass
    core.x_ready = ends


RATIO2 = [1.5, 2.5]


def second_block(core, io, shared):
    from contextlib import ExitStack
    nc, small = core.nc, core.small
    with ExitStack() as ctx:
        core.ctx, outer = ctx, core.ctx
        m = Mem()
        m.ident, m.ones, m.half, m.x = shared.ident, shared.ones, shared.half, shared.x
        core.piece_slots("2", 4, 3)
        m.xh, m.xl = core.sb("x_hi2", [P, KD, 2 * S], F32R), core.sb("x_lo2", [P, KD, 2 * S], F32R)
        m.acc, m.sigma = core.sb("merged", [P, 4, D]), core.sb("sigma", [P, 4, WC])
        m.yh, m.yl = core.sb("y_hi", [P, 4, 2 * S], F32R), core.sb("y_lo", [P, 4, 2 * S], F32R)
        m.kkv, m.gv = core.sb("gla_k_att_kv", [P, 4, 512]), core.sb("gla_v", [P, 4, 512])
        m.lrq, m.aq = core.sb("low_gla_q", [P, 4, 288]), core.sb("att_q", [P, 4, 512])
        m.par, m.rows = core.sb("par2", [P, PAR_COLS]), core.sb("rows2", [P, 2 * P])
        m.bias, m.sel = core.sb("bias_parts", [96, WC], BF16), core.sb("bias_sel", [96, N_BIAS, P], BF16)
        m.shift, m.scale = core.sb("shift", [P, KD, 2]), core.sb("scale", [P, KD, 2])
        m.gate_row, m.sel5 = core.sb("gate_row", [5, D]), core.sb("sel5", [5, 2, P])
        m.cos, m.sin = core.sb("cos2", [P, NT, HD]), core.sb("sin2", [P, NT, HD])
        m.tri2, m.halves = core.sb("tri2", [P, 4, P]), core.sb("halves", [P, 2])
        m.gmask = core.sb("gla_mask", [P, 4, P], mybir.dt.uint32)
        m.mean_w = core.sb("mean_w", [P, P])
        m.gtmp = core.ring("gate_tmp", 2, [P, 512])
        core.small.start(3, m.sel5[:, :, :], io["sel5"])
        core.small.start(3, m.cos[:, :, :], io["cos2"])
        core.small.start(3, m.sin[:, :, :], io["sin2"])
        core.small.start(3, m.tri2[:, :, :], io["tri2"])
        core.small.start(3, m.halves[:, :], io["halves"])
        core.small.start(3, m.gmask[:, :, :], io["gla_mask"])
        got = core.small.start(3, m.acc[0:96, 0:2, :].rearrange("p a b -> p (a b)")[:, 0:N_BIAS * P], io["bias_sel"])
        core.dve.mark(core.dve.after(got).tensor_copy(m.sel[:, :, :].rearrange("p a b -> p (a b)"),
                                                      m.acc[0:96, 0:2, :].rearrange("p a b -> p (a b)")[:, 0:N_BIAS * P]))
        core.dve.mark(core.dve.after().memset(m.mean_w[:, :], 1.0 / CONV))
        core.restart()
        core.x_ready = []
        for layer in range(LAYERS):
            second_layer(core, layer, io, m)
        core.sp.after((small.sems[10], small.counts[10]))
        core.ctx = outer


def shared_memory(core, io):
    m = Mem()
    m.ident, m.ones = core.sb("ident", [P, P]), core.sb("ones", [P, P])
    m.half = core.sb("minus_half", [P, 32])
    m.x = core.sb("x", [P, NT, D])
    core.ident = m.ident
    core.small.start(0, m.ident[:, :], io["ident"])
    got = core.small.start(0, m.x[:, :, :], io["x"].rearrange("(t p) d -> p t d", p=P))
    core.dve.mark(core.dve.after(got).memset(m.ones[:, :], 1.0))
    core.dve.mark(core.dve.after().memset(m.half[:, :], -0.5))
    return m


def program(nc, io):
    from contextlib import ExitStack
    with ExitStack() as ctx:
        core = Core(nc, ctx)
        core.loaded = []
        m = shared_memory(core, io)
        first_block(core, io, m)
        if "dbg_x1" not in io:
            core.x_ready = []
            second_block(core, io, m)
        else:
            t = core.small.start(2, io["dbg_x1"].rearrange("(t p) d -> p t d", p=P), m.x[:, :, :])
            core.sp.after(t)


def chunk_pieces(w, cols):
    k = w.shape[0] // P
    part = w[:, cols]
    n = part.shape[1]
    return part.reshape(k // KP, KP, P, n).transpose(0, 2, 1, 3).reshape(-1)


def columns(split, chunk):
    at, start = {}, 0
    for name, n in split:
        at[name] = start
        start += n
    return np.concatenate([np.arange(at[name] + first, at[name] + first + n) for name, first, n in chunk])


def rope_1():
    inv = np.float32(10000.0) ** (-np.arange(0, HD, 2, dtype=np.float32) / np.float32(HD))
    ang = np.arange(S, dtype=np.float32)[:, None] * inv[None, :]
    cos, sin = np.cos(ang), np.sin(ang)
    lay = lambda a: np.ascontiguousarray(a.reshape(NT, P, HD).transpose(1, 0, 2).astype(np.float32))
    return lay(np.concatenate([cos, cos], 1)), lay(np.concatenate([-sin, sin], 1))


def rope_2():
    rows, n_freq = S // 64, HD // 4
    pos_r = np.repeat(np.arange(rows, dtype=np.float32), 64)
    pos_c = np.tile(np.arange(64, dtype=np.float32), rows)
    freqs = np.float32(10000.0) ** (-np.arange(n_freq, dtype=np.float32) / np.float32(n_freq))
    ar, ac = pos_r[:, None] * freqs, pos_c[:, None] * freqs
    cos = np.concatenate([np.cos(ar), np.cos(ar), np.cos(ac), np.cos(ac)], 1)
    sin = np.concatenate([-np.sin(ar), np.sin(ar), -np.sin(ac), np.sin(ac)], 1)
    lay = lambda a: np.ascontiguousarray(a.reshape(NT, P, HD).transpose(1, 0, 2).astype(np.float32))
    return lay(cos), lay(sin)


def lay_out(inp):
    a = {}
    f = lambda n: np.asarray(inp[n])
    a["x"] = f("x").reshape(S, D)
    w, wo = f("w_in"), f("w_out")
    cols = [columns(SPLIT1, c) for c in CHUNKS1]
    a["w1"] = np.stack([np.concatenate([chunk_pieces(w[l], c) for c in cols]) for l in range(LAYERS)])
    a["wo1"] = np.stack([np.concatenate([chunk_pieces(wo[l], slice(c * WC, (c + 1) * WC)) for c in range(2)])
                         for l in range(LAYERS)])
    a["small1"] = np.concatenate([f("b_f"), f("lam_q1"), f("lam_k1"), f("lam_q2"), f("lam_k2"),
                                  f("g_subln"), f("ln_g"), f("ln_b")], axis=1)
    a["cos1"], a["sin1"] = rope_1()
    w, wm, bi = f("w_in_2"), f("w_mod_2"), f("b_in_2")
    cols = [columns(SPLIT2, c) for c in CHUNKS2]
    per = lambda fn: np.stack([fn(l) for l in range(LAYERS)])
    halves = lambda mat, n: np.concatenate([chunk_pieces(mat, slice(c * WC, (c + 1) * WC)) for c in range(n)])
    a["w2"] = per(lambda l: np.concatenate([chunk_pieces(w[l], c) for c in cols]))
    a["wm2"] = per(lambda l: halves(wm[l], 6))
    a["wo2"] = per(lambda l: halves(f("w_out_2")[l], 2))
    for n, key in (("conv", "w_conv_out_2"), ("gla", "w_gla_out_2"), ("att", "w_attn_out_2")):
        a["wy_" + n] = per(lambda l: halves(f(key)[l], 2))
    col = lambda v: v.reshape(-1, P).T
    dw = f("conv_dw_w_2")
    a["par2"] = per(lambda l: np.concatenate(
        [col(f("norm_g_2")[l]), col(bi[l][cols[0]]), col(bi[l][cols[1]]), col(bi[l][cols[2]]),
         dw[l].T.reshape(4, P, TAPS).transpose(1, 0, 2).reshape(P, 4 * TAPS),
         col(f("conv_dw_b_2")[l]), col(f("conv_ln_g_2")[l]), col(f("conv_ln_b_2")[l])], axis=1))
    a["rows2"] = np.concatenate([f("gla_norm_g_2"), f("q_norm_g_2"), f("k_norm_g_2")], axis=1)
    a["bias2"] = np.zeros((LAYERS, N_BIAS, WC), np.float32)
    for l in range(LAYERS):
        for c in range(N_BIAS):
            a["bias2"][l, c, :WIDTH2[c + 3]] = bi[l][cols[c + 3]]
    a["w_gate2"], a["b_gate2"] = f("gla_w_gate_2"), f("gla_b_gate_2").reshape(LAYERS, 2 * QK2)
    a["b_mod2"] = f("b_mod_2")
    a["c2"] = np.stack([f("c_2").reshape(KD, P).T, f("c_ctx_2").reshape(KD, P).T], axis=2)
    a["ctx2"] = f("ctx_2").reshape(S, D)
    a["cos2"], a["sin2"] = rope_2()
    i = np.arange(P)
    t_from, t_to = i[:, None], i[None, :]
    same = t_from // GC == t_to // GC
    a["tri2"] = np.stack([same & (t_from <= t_to), same & (t_from >= t_to),
                          same & (t_from > t_to), same & (t_from < t_to)], axis=1).astype(np.float32)
    a["halves"] = np.stack([i < GC, i >= GC], axis=1).astype(np.float32)
    a["gla_mask"] = np.stack([same & (t_from <= t_to)] * 2 + [same & (t_from >= t_to)] * 2, axis=1).astype(np.uint32)
    sel = np.zeros((96, N_BIAS, P), np.float32)
    for c in range(N_BIAS):
        sel[[c, 32 + c, 64 + c], c, :] = 1.0
    a["bias_sel"] = sel.reshape(96, N_BIAS * P)
    rows = np.array([[1, 0], [0, 1], [1, 0], [0, 1], [1, 1]], np.float32)
    a["sel5"] = np.repeat(rows[:, :, None], P, axis=2)
    i = np.arange(P)
    a["ident"] = np.eye(P, dtype=np.float32)
    a["causal"] = np.where(i[:, None] >= i[None, :], 0, NEG).astype(np.float32)
    a["tri"] = (i[:, None] <= i[None, :]).astype(np.float32)
    li = [0.8 - 0.6 * np.exp(-0.3 * l) for l in range(LAYERS)]
    a["lam_consts"] = np.tile(np.array([v for x in li for v in (x, 1.0 - x)], np.float32), (P, 1))
    return a


def kernel(**inputs):
    import concourse.bacc as bacc
    from concourse.bass_utils import run_bass_kernel_spmd

    arrays = {n: np.ascontiguousarray(v) for n, v in lay_out(inputs).items()}
    nc = bacc.Bacc("TRN2", target_bir_lowering=False, num_devices=1)
    io = {n: nc.dram_tensor("in_" + n, v.shape, mybir.dt.from_np(v.dtype), kind="ExternalInput").ap()
          for n, v in arrays.items()}
    io["y"] = nc.dram_tensor("out_y", (S, D), F32, kind="ExternalOutput").ap()
    program(nc, io)
    r = run_bass_kernel_spmd(nc, [{"in_" + n: v for n, v in arrays.items()}], core_ids=[0])
    return r.results[0]["out_y"].reshape(1, S, D)
```

```python
import numpy as np
import concourse.bass as bass
import concourse.mybir as mybir
from concourse.alu_op_type import AluOpType as ALU

F32, F32R, BF16 = mybir.dt.float32, mybir.dt.float32r, mybir.dt.bfloat16
ACT = mybir.ActivationFunctionType
AXX = mybir.AxisListType.X

P = 128
D = 1024
S = 256
NT = S // P
KD = D // P
HD = 64
LAYERS = 2
NEG = -1e30
FILL = -3e38
TOPK = 64
ALPHA = (2 * LAYERS) ** 0.25
EPS1 = 1e-5
EPS2 = 1e-6
WC = 512
KP = 2

SPLIT1 = [("diff_q", 512), ("diff_k", 512), ("diff_v", 512), ("dsa_q", 256), ("dsa_k", 64),
          ("dsa_v", 64), ("idx_q", 512), ("idx_k", 64), ("idx_w", 8), ("fox_q", 256),
          ("fox_k", 256), ("fox_v", 256), ("fox_f", 4), ("gate", 1024)]
CHUNKS1 = [[("idx_q", 0, 512)],
           [("idx_k", 0, 64), ("dsa_k", 0, 64), ("dsa_q", 0, 256), ("dsa_v", 0, 64),
            ("idx_w", 0, 8), ("fox_f", 0, 4)],
           [("diff_q", 0, 512)], [("diff_k", 0, 512)], [("diff_v", 0, 512)],
           [("fox_q", 0, 256), ("fox_k", 0, 256)],
           [("fox_v", 0, 256), ("gate", 768, 256)],
           [("gate", 0, 512)], [("gate", 512, 256)]]
IQ, DSA, DQ, DK, DV, FQK, FV, GA, GB = range(len(CHUNKS1))
WIDTH1 = [sum(n for _, _, n in c) for c in CHUNKS1]


def offsets(widths, rows):
    out = [0]
    for w in widths:
        out.append(out[-1] + rows * w)
    return out


OFF1 = offsets(WIDTH1, D)
OFFO = offsets([WC, WC], D)


class Engine:

    def __init__(self, engine, sem):
        self.engine, self.sem, self.count, self.seen = engine, sem, 0, {}

    def after(self, *tokens):
        for token in tokens:
            if token is None:
                continue
            sem, value = token
            if self.seen.get(id(sem), 0) < value:
                self.engine.wait_ge(sem, value)
                self.seen[id(sem)] = value
        return self.engine

    def mark(self, instruction):
        self.count += 1
        instruction.then_inc(self.sem, 1)
        return (self.sem, self.count)

    def restart(self):
        self.count, self.seen = 0, {}


class Loads:

    def __init__(self, queue, sems):
        self.queue, self.sems, self.counts = queue, sems, [0] * len(sems)

    def start(self, k, out, in_, *tokens):
        self.queue.after(*tokens).dma_start(out, in_).then_inc(self.sems[k], 16)
        self.counts[k] += 16
        return (self.sems[k], self.counts[k])

    def restart(self):
        self.counts = [0] * len(self.sems)


class Ring:

    def __init__(self, buffers):
        self.buffers = buffers
        self.restart()

    def take(self):
        slot = self.unused.pop(0)
        return self.buffers[slot], self.tokens[slot], slot

    def free(self, slot, *tokens):
        self.tokens[slot] = tokens
        self.unused.append(slot)

    def restart(self):
        self.tokens, self.unused = [()] * len(self.buffers), list(range(len(self.buffers)))


def spread(ap, shape):
    return ap.unsqueeze(1).to_broadcast(shape)


def pipeline(items, stages, lags):
    for step in range(len(items) + lags[-1]):
        for stage, lag in reversed(list(zip(stages, lags))):
            if 0 <= step - lag < len(items):
                stage(items[step - lag])
                yield


class Core:

    SLOTS = 6

    def __init__(self, nc, ctx):
        self.nc, self.ctx = nc, ctx
        sem = lambda name: ctx.enter_context(nc.semaphore(name))
        self.pe = Engine(nc.tensor, sem("pe_done"))
        self.act = Engine(nc.scalar, sem("act_done"))
        self.dve = Engine(nc.vector, sem("dve_done"))
        self.pool = Engine(nc.gpsimd, sem("pool_done"))
        self.sp = Engine(nc.sync, sem("sp_unused"))
        self.weights = Loads(self.sp, [sem(f"weights_in{i}") for i in range(self.SLOTS)])
        self.small = Loads(self.sp, [sem(f"small_in{i}") for i in range(16)])
        self.bank = [ctx.enter_context(nc.psum_tensor(f"bank{i}", [P, 512], F32)) for i in range(8)]
        self.rings = []
        self.share_banks(4, 3)
        self.pieces, self.cut, self.done = [], [], []

    def share_banks(self, proj, aux):
        self.proj, self.aux = Ring(self.bank[0:proj]), Ring(self.bank[proj:proj + aux])
        self.sum_bank = Ring(self.bank[proj + aux:])
        self.rings[0:3] = [self.proj, self.aux, self.sum_bank]

    def sb(self, name, shape, dtype=F32, side="left"):
        return self.ctx.enter_context(self.nc.sbuf_tensor(name, shape, dtype, side=side))

    def ring(self, name, n, shape, dtype=F32):
        whole = self.sb(name, [shape[0], n] + shape[1:], dtype)
        ring = Ring([whole[:, i] for i in range(n)])
        self.rings.append(ring)
        return ring

    def piece_slots(self, name, raw, cut):
        self.RAW, self.CUT = raw, cut
        self.raw = self.sb("w_raw" + name, [P, raw, KP * WC])
        self.hi = self.sb("w_hi" + name, [P, cut, KP * WC], F32R)
        self.lo = self.sb("w_lo" + name, [P, cut, KP * WC], F32R)

    def stream(self, pieces):
        self.pieces += pieces

    def load_piece(self):
        n = len(self.loaded)
        dram, width = self.pieces[n]
        slot = n % self.RAW
        before = self.cut[n - self.RAW] if n >= self.RAW else ()
        self.loaded.append(self.weights.start(slot, self.raw[:, slot, 0:KP * width], dram, *before))

    def cut_piece(self):
        n = len(self.cut)
        _, width = self.pieces[n]
        raw = self.raw[:, n % self.RAW, 0:KP * width]
        hi = self.hi[:, n % self.CUT, 0:KP * width]
        lo = self.lo[:, n % self.CUT, 0:KP * width]
        free = self.done[n - self.CUT] if n >= self.CUT else None
        rounded = self.act.mark(self.act.after(self.loaded[n], free).activation(hi, raw, ACT.Copy))
        rest = self.dve.mark(self.dve.after(self.loaded[n], rounded).tensor_tensor(
            lo, raw, hi.bitcast(F32), ALU.subtract))
        self.cut.append((rounded, rest))

    def next_piece(self):
        n = len(self.done)
        while len(self.loaded) < min(n + self.RAW, len(self.pieces)):
            if len(self.loaded) >= self.RAW and len(self.cut) <= len(self.loaded) - self.RAW:
                break
            self.load_piece()
        while len(self.cut) < min(n + self.CUT, len(self.pieces)):
            self.cut_piece()
            if len(self.loaded) < len(self.pieces):
                self.load_piece()
        width = self.pieces[n][1]
        shape = lambda t: t[:, n % self.CUT, 0:KP * width].rearrange("p (k n) -> p k n", k=KP)
        return shape(self.hi), shape(self.lo), self.cut[n]

    def piece_used(self, token):
        self.done.append(token)

    def project(self, xs, n_k, tiles, width, evacuate, bias=None, width_of=None):
        (xh, xl, ready) = xs
        banks = []
        for t in tiles:
            ps, free, slot = self.proj.take()
            banks.append((ps, free, slot))
        pairs = n_k // KP
        for kp in range(pairs):
            hi, lo, cut = self.next_piece()
            for i, t in enumerate(tiles):
                ps, free, slot = banks[i]
                col = slice(t * P, (t + 1) * P)
                w = width_of(t) if width_of else width
                self.pe.after(*cut, *ready(t), *(free if kp == 0 else ()))
                for kk in range(KP):
                    k = kp * KP + kk
                    first, last = kp == 0 and kk == 0, kp == pairs - 1 and kk == KP - 1
                    mm = self.nc.tensor.matmul
                    if first and bias is not None:
                        bias(ps[:, 0:w], w)
                        first = False
                    mm(ps[:, 0:w], xh[:, k, col], hi[:, kk, 0:w], start=first, stop=False)
                    mm(ps[:, 0:w], xh[:, k, col], lo[:, kk, 0:w], start=False, stop=False)
                    ins = mm(ps[:, 0:w], xl[:, k, col], hi[:, kk, 0:w], start=False, stop=last)
                token = self.pe.mark(ins)
                if kp == pairs - 1:
                    self.proj.free(slot, *evacuate(t, ps, token))
                if i == len(tiles) - 1:
                    self.piece_used(token)
                yield

    def project_t(self, xs, n_k, n_tok, evacuate):
        (xh, xl, ready) = xs
        banks = [self.proj.take() for _ in range(WC // P)]
        for kp in range(n_k // KP):
            hi, lo, cut = self.next_piece()
            for j, (ps, free, slot) in enumerate(banks):
                self.pe.after(*cut, *ready, *(free if kp == 0 else ()))
                for kk in range(KP):
                    k = kp * KP + kk
                    first, last = k == 0, k == n_k - 1
                    mm, cols, out = self.nc.tensor.matmul, slice(j * P, (j + 1) * P), ps[:, 0:n_tok]
                    mm(out, hi[:, kk, cols], xh[:, k, 0:n_tok], start=first, stop=False)
                    mm(out, lo[:, kk, cols], xh[:, k, 0:n_tok], start=False, stop=False)
                    ins = mm(out, hi[:, kk, cols], xl[:, k, 0:n_tok], start=False, stop=last)
                token = self.pe.mark(ins)
                if k == n_k - 1:
                    self.proj.free(slot, *evacuate(j, ps, token))
                if j == len(banks) - 1:
                    self.piece_used(token)
                yield

    def transpose(self, blocks, ready, width=P):
        ps, free, slot = self.aux.take()
        self.pe.after(*ready, *free)
        for i, block in enumerate(blocks):
            ins = self.nc.tensor.transpose(ps[0:width, i * P:(i + 1) * P], block, self.ident[:, :])
        return ps, self.pe.mark(ins), slot

    def transpose_cut(self, src, cols, dst_hi, dst_lo, ready, free=()):
        tokens = []
        for b in range(0, cols // P, 4):
            ps, token, slot = self.transpose([src[:, (b + i) * P:(b + i + 1) * P] for i in range(4)],
                                             ready)
            view = ps[:, :].rearrange("p (k t) -> p k t", k=4)
            hi, lo = dst_hi[:, b:b + 4, :], dst_lo[:, b:b + 4, :]
            rounded = self.act.mark(self.act.after(token, *free).activation(hi, view, ACT.Copy))
            rest = self.dve.mark(self.dve.after(token, rounded).tensor_tensor(
                lo, view, hi.bitcast(F32), ALU.subtract))
            self.aux.free(slot, rest, rounded)
            tokens += [rounded, rest]
            yield
        self.last = tokens

    def fence(self):
        return [(e.sem, e.count) for e in (self.pe, self.act, self.dve, self.pool) if e.count]

    def restart(self):
        nc = self.nc
        nc.all_engine_barrier()
        for e in (self.pe, self.act, self.dve, self.pool, self.sp):
            nc.sync.sem_clear(e.sem)
        for s in self.weights.sems + self.small.sems:
            nc.sync.sem_clear(s)
        nc.all_engine_barrier()
        for x in [self.pe, self.act, self.dve, self.pool, self.sp, self.weights, self.small] + self.rings:
            x.restart()
        self.pieces, self.loaded, self.cut, self.done = [], [], [], []


def weave(main, sides, rates):
    sides = [[i, side, 0.0] for i, side in enumerate(sides)]

    def side_step(side):
        if next(side[1], "end") == "end":
            sides.remove(side)
            return False
        return True
    at = 0
    for n, condition in enumerate(main):
        while condition is not None and not condition():
            at += 1
            side_step(sides[at % len(sides)])
        for side in list(sides):
            side[2] += rates(n)[side[0]]
            while side[2] >= 1:
                side[2] -= 1
                if not side_step(side):
                    break
    while sides:
        at += 1
        side_step(sides[at % len(sides)])


def first_layer(core, layer, io, m):
    nc, pe, act, dve, pool, sp = core.nc, core.pe, core.act, core.dve, core.pool, core.sp
    small = core.small
    piece = lambda array, at, width: (array[layer, at:at + P * KP * width]
                                      .rearrange("(p n) -> p n", p=P), width)
    def stream(array, offs, c, width):
        core.stream([piece(io[array], offs[c] + kp * P * KP * width, width) for kp in range(KD // KP)])
    for c in (0, 1):
        stream("wm2", OFFM, c, WC)
    for c, width in enumerate(WIDTH1):
        stream("w1", OFF1, c, width)
    for c in (2, 3):
        stream("wm2", OFFM, c, WC)
    for c in range(2):
        stream("wo1", OFFO, c, WC)
    for c in (4, 5):
        stream("wm2", OFFM, c, WC)

    def modulation(chunks):
        for c in chunks:
            ps, free, slot = core.proj.take()
            for kp in range(KD // KP):
                hi, lo, cut = core.next_piece()
                pe.after(*cut, *(free if kp == 0 else ()))
                for kk in range(KP):
                    k = kp * KP + kk
                    cols = m.c_cut[:, 4 * k:4 * k + P]
                    nc.tensor.matmul(ps[:, :], cols, hi[:, kk, :], start=k == 0, stop=False)
                    ins = nc.tensor.matmul(ps[:, :], cols, lo[:, kk, :], start=False, stop=k == KD - 1)
                token = pe.mark(ins)
                core.piece_used(token)
                yield
            row, rfree, rslot = m.mod_row.take()
            end = act.mark(act.after(token, *rfree).activation(row, ps[0:4, :], ACT.Copy))
            core.proj.free(slot, end)
            ps, free, slot = core.aux.take()
            pe.after(end, *free)
            for j in range(4):
                ins = nc.tensor.matmul(ps[:, 2 * j:2 * j + 2], row[:, j * P:(j + 1) * P], m.sel4[:, :],
                                       start=True, stop=True)
            token = pe.mark(ins)
            m.mod_row.free(rslot, token)
            end = act.mark(act.after(token).activation(
                m.mod_cols[:, bass.ds(layer * MOD_COLS + 8 * c, 8)], ps[:, 0:8], ACT.Copy))
            core.aux.free(slot, end)
            yield

    row = io["small1"][layer, :].partition_broadcast(P)
    params = small.start(0, m.par[:, :], row)
    bf, lams, gsub = m.par[:, 0:4], m.par[:, 4:260], m.par[:, 260:388]
    ln_g, ln_b = m.par[:, 388:388 + D], m.par[:, 388 + D:388 + 2 * D]

    lp = lams.rearrange("p (a b d) -> p a b d", a=2, b=2)
    prod = dve.mark(dve.after(params).tensor_tensor(m.lprod[:, :, :], lp[:, :, 0, :], lp[:, :, 1, :], ALU.mult))
    dots = dve.mark(dve.after(prod).tensor_reduce(m.lam[:, 0:2], m.lprod[:, :, :], AXX, ALU.add))
    li = act.mark(act.after().activation(m.linit[:, 2:4], m.lconst[:, bass.ds(layer * 2, 2)], ACT.Copy))
    exps = act.mark(act.after(dots, li).activation(m.lam[:, 2:4], m.lam[:, 0:2], ACT.Exp))
    diff = dve.mark(dve.after(exps).tensor_tensor(m.lam[:, 4:5], m.lam[:, 2:3], m.lam[:, 3:4], ALU.subtract))
    lam = dve.mark(dve.after(diff).tensor_tensor(m.lam[:, 5:6], m.lam[:, 4:5], m.linit[:, 2:3], ALU.add))
    gsc = dve.mark(dve.after(li, params).tensor_scalar(m.gs[:, :], gsub, m.linit[:, 3:4], None, ALU.mult))

    x_ready = {}

    def transpose_x():
        for t in range(NT):
            cols = slice(t * P, (t + 1) * P)
            yield from core.transpose_cut(m.x[:, t, :], D, m.xh[:, :, cols], m.xl[:, :, cols], ())
            x_ready[t] = core.last
    weave(modulation((0, 1)), [transpose_x()], lambda n: [1.0])
    xs = (m.xh, m.xl, lambda t: x_ready[t])

    got = {}

    def rope(ps, heads, t, out, token):
        v = ps[:, 0:heads * HD].rearrange("p (h d) -> p h d", d=HD)
        (tmp, free, slot) = m.rope.take()
        a = tmp[:, 0, 0:heads * HD].rearrange("p (h d) -> p h d", d=HD)
        b = tmp[:, 1, 0:heads * HD].rearrange("p (h d) -> p h d", d=HD)
        h = HD // 2
        one = dve.mark(dve.after(token, *free).tensor_tensor(
            a, v, spread(m.cos[:, t, :], [P, heads, HD]), ALU.mult))
        dve.mark(dve.after().tensor_tensor(
            b[:, :, 0:h], v[:, :, h:HD], spread(m.sin[:, t, 0:h], [P, heads, h]), ALU.mult))
        two = dve.mark(dve.after().tensor_tensor(
            b[:, :, h:HD], v[:, :, 0:h], spread(m.sin[:, t, h:HD], [P, heads, h]), ALU.mult))
        end = pool.mark(pool.after(two).tensor_tensor(out, a, b, ALU.add))
        m.rope.free(slot, end)
        return two, end

    def evacuate(chunk):
        def run(t, ps, token):
            if chunk in (IQ, DQ, DK):
                dst = {IQ: m.iq, DQ: m.dq, DK: m.dk}[chunk]
                read, end = rope(ps, 8, t, dst[:, t, :].rearrange("p (h d) -> p h d", d=HD), token)
                got[chunk, t] = [end]
                return [read]
            if chunk == DSA:
                read, end = rope(ps, 6, t, m.sx[:, t, :].rearrange("p (h d) -> p h d", d=HD), token)
                end2 = dve.mark(dve.after().tensor_copy(m.sv[:, t, :], ps[:, 384:460]))
                got[chunk, t] = [end, end2]
                return [end2]
            if chunk == FQK:
                v = ps[:, :].rearrange("p (h d) -> p h d", d=HD)
                end = act.mark(act.after(token).activation(m.fqk[:, t, :, 0:HD], v, ACT.Copy))
            elif chunk == FV:
                dve_end = dve.mark(dve.after(token).tensor_copy(m.fv[:, t, :], ps[:, 0:256]))
                end = act.mark(act.after(dve_end).activation(m.gate[:, t, 768:1024], ps[:, 256:512], ACT.Copy))
                got[chunk, t] = [dve_end, end]
                return [dve_end, end]
            elif chunk == DV:
                end = act.mark(act.after(token).activation(m.dv[:, t, :], ps[:, :], ACT.Copy))
            elif chunk == GA:
                end = act.mark(act.after(token).activation(m.gate[:, t, 0:512], ps[:, :], ACT.Copy))
            else:
                end = act.mark(act.after(token).activation(m.gate[:, t, 512:768], ps[:, 0:256], ACT.Copy))
            got[chunk, t] = [end]
            return [end]
        return run

    def need(*chunks):
        while not all((c, t) in got for c in chunks for t in range(NT)):
            yield

    def tokens(*chunks):
        return [x for c in chunks for t in range(NT) for x in got[c, t]]

    def head_transposes(src, heads, dst, rows, scale, ready, free=()):
        out = []
        for h in range(0, heads, 2):
            n = min(2, heads - h)
            ps, free_ps, slot = core.aux.take()
            pe.after(*ready, *free_ps)
            for i in range(n):
                for t in range(NT):
                    ins = nc.tensor.transpose(ps[0:rows, (i * NT + t) * P:(i * NT + t + 1) * P],
                                              src(h + i, t), m.ident[:, :])
            token = pe.mark(ins)
            view = ps[0:rows, 0:n * S].rearrange("p (h t) -> p h t", h=n)
            if (h // 2) % 2 == 0:
                end = act.mark(act.after(token, *free).activation(dst[0:rows, h:h + n, :], view, ACT.Copy, scale=scale))
            else:
                end = dve.mark(dve.after(token, *free).tensor_scalar(dst[0:rows, h:h + n, :], view, scale, None, ALU.mult))
            core.aux.free(slot, end)
            out.append(end)
            yield
        core.last = out

    mixed = {}

    def sparse_index():
        yield from need(IQ, DSA)
        ready = tokens(IQ, DSA)
        yield from head_transposes(lambda h, t: m.iq[:, t, h * HD:(h + 1) * HD], 8, m.qa, HD, 1.0, ready)
        q_t = core.last
        yield from head_transposes(lambda h, t: m.sx[:, t, h * HD:(h + 1) * HD], 2, m.sk_t, HD, 1.0, ready)
        k_t = core.last
        yield from head_transposes(lambda h, t: m.sx[:, t, (2 + h) * HD:(3 + h) * HD], 4, m.sq_t, HD, HD ** -0.5, ready)
        got["dsa_t"] = k_t + core.last
        w_end = dve.mark(dve.after(*ready).tensor_scalar(m.iw[:, :, :], m.sv[:, :, 64:72], (8 * HD) ** -0.5, None, ALU.mult))
        for qt in range(NT):
            keys = (qt + 1) * P
            acc = None
            items = list(range(0, 8, 2))
            state = {}

            def scores(h):
                ps, free, slot = core.aux.take()
                pe.after(*q_t, *k_t, *free)
                for i in range(2):
                    ins = nc.tensor.matmul(ps[:, i * keys:(i + 1) * keys], m.qa[0:HD, h + i, qt * P:(qt + 1) * P],
                                           m.sk_t[0:HD, 0, 0:keys], start=True, stop=True)
                state[h] = (ps, slot, pe.mark(ins))

            def weigh(h):
                ps, slot, token = state[h]
                r, free, rslot = m.relu.take()
                end = act.mark(act.after(token, *free).activation(r[:, 0:2 * keys], ps[:, 0:2 * keys], ACT.Relu))
                core.aux.free(slot, end)
                for i in range(2):
                    w = m.iw[:, qt, h + i:h + i + 1]
                    part = r[:, i * keys:(i + 1) * keys]
                    if h + i == 0:
                        state["acc"] = dve.mark(dve.after(end, w_end, *state.get("acc_free", ())).tensor_scalar(
                            m.score[:, qt, 0:keys], part, w, None, ALU.mult))
                    else:
                        state["acc"] = dve.mark(dve.after(end, state["acc"]).scalar_tensor_tensor(
                            m.score[:, qt, 0:keys], part, w, m.score[:, qt, 0:keys], ALU.mult, ALU.add))
                m.relu.free(rslot, state["acc"])
            yield from pipeline(items, [scores, weigh], [0, 1])
            diag = m.score[:, qt, qt * P:keys]
            last = dve.mark(dve.after(state["acc"]).tensor_tensor(diag, diag, m.mask[:, :], ALU.add))
            for _ in range(TOPK // 8):
                top = dve.mark(dve.after(last).max(m.top8[:, :], m.score[:, qt, 0:keys]))
                last = dve.mark(dve.after(top).match_replace(m.score[:, qt, 0:keys], m.top8[:, :], m.score[:, qt, 0:keys], FILL))
                yield
            got["sel", qt] = dve.mark(dve.after(last, *m.sel_free).tensor_scalar(
                m.sel[:, qt, 0:keys], m.score[:, qt, 0:keys], 0.5 * FILL, NEG, ALU.is_gt, ALU.mult))
        m.idx_done = [q for q in q_t] + [(pe.sem, pe.count)]

    def attend(name, heads, q_of, k_of, rows, v_of, v_width, out, bias_sel, ready, buf):
        for qt in range(NT):
            keys = (qt + 1) * P
            nb = qt + 1
            diff_kind = name == "diff"
            n_out = 1 if diff_kind else 2
            osum, ofree, oslot = core.sum_bank.take()
            stat, sfree, sslot = buf.stat.take()
            n_maps = 2 * heads
            top_of, sum_of, inv_of, sub_of = (stat[:, i * n_maps:(i + 1) * n_maps] for i in range(4))
            st = {}

            def scores(j):
                ps, free, slot = core.aux.take()
                pe.after(*ready, *free)
                for i in range(2):
                    part = ps[:, i * keys:(i + 1) * keys]
                    nc.tensor.matmul(part, q_of(2 * j + i)[0:rows, qt * P:(qt + 1) * P],
                                     k_of(2 * j + i)[0:rows, 0:keys], start=True, stop=False)
                    if bias_sel:
                        nc.tensor.matmul(part, m.identb[:, :], m.sel[:, qt, 0:keys], start=False, stop=False)
                    ins = nc.tensor.matmul(part[:, qt * P:keys], m.identb[:, :], m.maskb[:, :], start=False, stop=True)
                st[j] = [ps, slot, pe.mark(ins)]

            def soft(j):
                ps, slot, token = st[j]
                view = ps[:, 0:2 * keys].rearrange("p (a b) -> p a b", a=2)
                top = dve.mark(dve.after(token, *sfree).tensor_reduce(
                    top_of[:, 2 * j:2 * j + 2], view, AXX, ALU.max, negate=True))
                pm, free, pslot = buf.prob.take()
                act.after(top, *free)
                for i in range(2):
                    n = 2 * j + i
                    end = act.mark(nc.scalar.activation(pm[:, i, 0:keys], ps[:, i * keys:(i + 1) * keys], ACT.Exp,
                                                        bias=top_of[:, n:n + 1], accum_out=sum_of[:, n:n + 1]))
                core.aux.free(slot, end)
                inv = dve.mark(dve.after(end).reciprocal(inv_of[:, 2 * j:2 * j + 2], sum_of[:, 2 * j:2 * j + 2]))
                if diff_kind:
                    lam_l1 = dve.mark(dve.after(inv).tensor_scalar(
                        sub_of[:, 2 * j:2 * j + 1], inv_of[:, 2 * j + 1:2 * j + 2], m.lam[:, 5:6], None, ALU.mult))
                    second = dve.mark(dve.after(lam_l1).tensor_scalar(
                        pm[:, 1, 0:keys], pm[:, 1, 0:keys], sub_of[:, 2 * j:2 * j + 1], None, ALU.mult))
                    end = dve.mark(dve.after(second).scalar_tensor_tensor(
                        pm[:, 0, 0:keys], pm[:, 0, 0:keys], inv_of[:, 2 * j:2 * j + 1], pm[:, 1, 0:keys],
                        ALU.mult, ALU.subtract))
                st[j] = [pm, pslot, end]
                st["inv"] = inv

            def flip(j):
                pm, pslot, end = st[j]
                ps, free, slot = core.aux.take()
                pe.after(end, *free)
                for i in range(n_out):
                    for b in range(nb):
                        ins = nc.tensor.transpose(ps[:, (i * nb + b) * P:(i * nb + b + 1) * P],
                                                  pm[:, i, b * P:(b + 1) * P], m.ident[:, :])
                token = pe.mark(ins)
                buf.prob.free(pslot, token)
                pt, pfree, ptslot = buf.prob_t.take()
                n = n_out * nb * P
                if j % 2 == 0:
                    end = act.mark(act.after(token, *pfree).activation(pt[:, 0:n], ps[:, 0:n], ACT.Copy))
                else:
                    end = dve.mark(dve.after(token, *pfree).tensor_copy(pt[:, 0:n], ps[:, 0:n]))
                core.aux.free(slot, end)
                st[j] = [pt, ptslot, end]

            def values(j):
                pt, ptslot, end = st[j]
                pe.after(end, *(ofree if j == 0 else ()))
                for i in range(n_out):
                    h = n_out * j + i
                    for b in range(nb):
                        ins = nc.tensor.matmul(osum[:, h * v_width:(h + 1) * v_width],
                                               pt[:, (i * nb + b) * P:(i * nb + b + 1) * P], v_of(h, b),
                                               start=b == 0, stop=b == nb - 1)
                st["sum"] = pe.mark(ins)
                buf.prob_t.free(ptslot, st["sum"])
            yield from pipeline(list(range(heads)), [scores, soft, flip, values], LAGS)
            n_cols = heads * n_out * v_width
            if diff_kind:
                end = act.mark(act.after(st["sum"]).activation(out[:, qt, :], osum[:, 0:n_cols], ACT.Copy))
            else:
                end = dve.mark(dve.after(st["sum"], st["inv"]).tensor_tensor(
                    out[:, qt, :].rearrange("p (h d) -> p h d", d=v_width),
                    osum[:, 0:n_cols].rearrange("p (h d) -> p h d", d=v_width),
                    inv_of.unsqueeze(2).to_broadcast([P, n_maps, v_width]), ALU.mult))
            buf.stat.free(sslot, end)
            core.sum_bank.free(oslot, end)
            mixed[name, qt] = [end]
            yield

    def sub_norm(qt):
        a = m.mix[:, qt, 0:512]
        sq, free, slot = m.relu.take()
        s1 = pool.mark(pool.after(*mixed["diff", qt], *free).tensor_tensor(sq[:, 0:512], a, a, ALU.mult))
        s2 = dve.mark(dve.after(s1).tensor_reduce(m.ms[:, qt, :], sq[:, 0:512].rearrange("p (h d) -> p h d", h=4), AXX, ALU.add))
        m.relu.free(slot, s2)
        s3 = dve.mark(dve.after(s2).tensor_scalar(m.ms[:, qt, :], m.ms[:, qt, :], 1.0 / P, EPS1, ALU.mult, ALU.add))
        s4 = pool.mark(pool.after(s3).tensor_tensor(m.ms2[:, qt, :], m.ms[:, qt, :], m.half[:, 0:4], ALU.pow))
        av = a.rearrange("p (h d) -> p h d", h=4)
        gated = pool.mark(pool.after(gsc).tensor_tensor(av, av, spread(m.gs[:, :], [P, 4, P]), ALU.mult))
        for h in range(4):
            end = dve.mark(dve.after(s4, gated).tensor_scalar(av[:, h, :], av[:, h, :], m.ms2[:, qt, h:h + 1], None, ALU.mult))
        mixed["norm", qt] = [end]

    def side_sparse():
        yield from sparse_index()
        yield from attend("dsa", 2, lambda h: m.sq_t[:, h, :], lambda h: m.sk_t[:, 1, :], HD,
                          lambda h, b: m.sv[:, b, 0:64], HD, m.mix[:, :, 512:768], True,
                          got["dsa_t"] + [got["sel", 0], got["sel", 1]] + tokens(DSA), m.buf_a)

    def side_diff():
        yield from need(DQ, DK)
        yield from head_transposes(lambda h, t: m.dq[:, t, h * HD:(h + 1) * HD], 8, m.qb, HD, HD ** -0.5, tokens(DQ))
        q_t = core.last
        yield from head_transposes(lambda h, t: m.dk[:, t, h * HD:(h + 1) * HD], 8, m.kb, HD, 1.0, tokens(DK))
        q_t = q_t + core.last
        yield from need(DV)
        yield from attend("diff", 4, lambda h: m.qb[:, h, :], lambda h: m.kb[:, h, :], HD,
                          lambda h, b: m.dv[:, b, h * P:(h + 1) * P], P, m.mix[:, :, 0:512], False,
                          q_t + [lam] + tokens(DV), m.buf_b)
        for qt in range(NT):
            sub_norm(qt)
            yield
        yield from need(FQK)
        z = dve.mark(dve.after(*tokens(DSA), params).tensor_tensor(
            m.fz[:, :, :], m.sv[:, :, 72:76], spread(bf, [P, NT, 4]), ALU.add))
        az = dve.mark(dve.after(z).scalar_tensor_tensor(m.fa[:, :, :], m.fz[:, :, :], -1.0, m.fz[:, :, :], ALU.mult, ALU.max))
        ez = act.mark(act.after(az).activation(m.fe[:, :, :], m.fa[:, :, :], ACT.Exp, scale=-1.0))
        lz = act.mark(act.after(ez).activation(m.fl[:, :, :], m.fe[:, :, :], ACT.Ln, bias=1.0))
        lf = dve.mark(dve.after(lz).scalar_tensor_tensor(m.lf[:, :, :], m.fz[:, :, :], 0.0, m.fl[:, :, :], ALU.min, ALU.subtract))
        ps, free, slot = core.aux.take()
        pe.after(lf, *free)
        nc.tensor.matmul(ps[:, 0:4], m.tri[:, :], m.lf[:, 0, :], start=True, stop=True)
        nc.tensor.matmul(ps[:, 4:8], m.ones[:, :], m.lf[:, 0, :], start=True, stop=False)
        cs = pe.mark(nc.tensor.matmul(ps[:, 4:8], m.tri[:, :], m.lf[:, 1, :], start=False, stop=True))
        cv = ps[:, 0:8].rearrange("p (t h) -> p t h", t=NT)
        c1 = dve.mark(dve.after(cs).tensor_scalar(m.fqk[:, :, 0:4, 64], cv, HD ** 0.5, None, ALU.mult))
        c2 = dve.mark(dve.after(cs).tensor_scalar(m.fqk[:, :, 4:8, 65], cv, -HD ** 0.5, None, ALU.mult))
        core.aux.free(slot, c2)
        c3 = dve.mark(dve.after().memset(m.fqk[:, :, 0:4, 65], 1.0))
        c4 = dve.mark(dve.after().memset(m.fqk[:, :, 4:8, 64], 1.0))
        ready = tokens(FQK) + [c1, c2, c3, c4]
        yield
        yield from head_transposes(lambda h, t: m.fqk[:, t, h, :], 4, m.qa, 66, HD ** -0.5, ready, m.idx_done)
        f_t = core.last
        yield from head_transposes(lambda h, t: m.fqk[:, t, 4 + h, :], 4, m.ka, 66, 1.0, ready)
        f_t = f_t + core.last
        yield from need(FV)
        yield from attend("fox", 2, lambda h: m.qa[:, h, :], lambda h: m.ka[:, h, :], 66,
                          lambda h, b: m.fv[:, b, h * HD:(h + 1) * HD], HD, m.mix[:, :, 768:1024], False,
                          f_t + tokens(FV), m.buf_b)

    def main():
        for c, width in enumerate(WIDTH1):
            yield from core.project(xs, KD, range(NT), width, evacuate(c))

    weave(main(), [side_sparse(), side_diff()], lambda n: RATES1)

    proj_done = core.done[-1]
    ready = {}

    def gate_and_cut():
        for t in range(NT):
            sg = act.mark(act.after(*tokens(GA, GB, FV)).activation(m.gate[:, t, :], m.gate[:, t, :], ACT.Silu))
            half = 512
            e1 = pool.mark(pool.after(sg, *mixed["norm", t]).tensor_tensor(
                m.mix[:, t, 0:half], m.mix[:, t, 0:half], m.gate[:, t, 0:half], ALU.mult))
            e2 = dve.mark(dve.after(sg, *mixed["dsa", t], *mixed["fox", t]).tensor_tensor(
                m.mix[:, t, half:D], m.mix[:, t, half:D], m.gate[:, t, half:D], ALU.mult))
            cols = slice(t * P, (t + 1) * P)
            yield from core.transpose_cut(m.mix[:, t, :], D, m.xh[:, :, cols], m.xl[:, :, cols],
                                          (e1, e2), (proj_done,))
            ready[t] = core.last
    weave(modulation((2, 3)), [gate_and_cut()], lambda n: [1.0])

    sums = {}

    def add_residual(c):
        def run(t, ps, token):
            part = m.x[:, t, c * WC:(c + 1) * WC]
            end = dve.mark(dve.after(token).scalar_tensor_tensor(part, part, ALPHA, ps[:, :], ALU.mult, ALU.add))
            st = dve.mark(dve.after(end).bn_stats(m.bn[:, t, c * 6:(c + 1) * 6], part))
            sums[t] = (end, st)
            return [end]
        return run
    for c in range(2):
        for _ in core.project((m.xh, m.xl, lambda t: ready[t]), KD, range(NT), WC, add_residual(c)):
            pass
    for _ in modulation((4, 5)):
        pass
    for t in range(NT):
        ag = dve.mark(dve.after(*sums[t]).bn_aggr(m.mv[:, t, :], m.bn[:, t, :]))
        ve = dve.mark(dve.after(ag).tensor_scalar(m.mv[:, t, 1:2], m.mv[:, t, 1:2], EPS1, None, ALU.add))
        rs = pool.mark(pool.after(ve).tensor_tensor(m.rstd[:, t, :], m.mv[:, t, 1:2], m.half[:, 0:1], ALU.pow))
        xn = dve.mark(dve.after(rs).tensor_scalar(m.x[:, t, :], m.x[:, t, :], m.mv[:, t, 0:1], m.rstd[:, t, :],
                                                  ALU.subtract, ALU.mult))
        halves = ((dve, slice(0, 512)), (pool, slice(512, D)))
        for e, s in halves:
            g = e.mark(e.after(xn).tensor_tensor(m.x[:, t, s], m.x[:, t, s], ln_g[:, s], ALU.mult))
            e.mark(e.after(g).tensor_tensor(m.x[:, t, s], m.x[:, t, s], ln_b[:, s], ALU.add))


RATES1 = [1.0, 1.0]
LAGS = [0, 1, 2, 3]
LAGS2 = [0, 1, 2, 3]
MOD_COLS = 2 * 3 * KD


class Mem:
    pass


def first_block(core, io, shared):
    from contextlib import ExitStack
    nc = core.nc
    with ExitStack() as ctx:
        core.ctx, outer = ctx, core.ctx
        rings = list(core.rings)
        m = Mem()
        m.ident, m.ones, m.half, m.x = shared.ident, shared.ones, shared.half, shared.x
        m.mod_cols = shared.mod_cols
        core.piece_slots("1", 6, 4)
        core.share_banks(3, 3)
        m.xh, m.xl = core.sb("x_hi1", [P, KD, S], F32R), core.sb("x_lo1", [P, KD, S], F32R)
        m.par = core.sb("par1", [P, 388 + 2 * D])
        m.lprod, m.lam = core.sb("lam_prod", [P, 2, HD]), core.sb("lam", [P, 6])
        m.linit, m.gs = core.sb("lam_init", [P, 4]), core.sb("g_sub_scaled", [P, P])
        m.lconst = core.sb("lam_consts", [P, 2 * LAYERS])
        m.cos, m.sin = core.sb("cos1", [P, NT, HD]), core.sb("sin1", [P, NT, HD])
        m.mask, m.maskb = core.sb("causal_bias", [P, P]), core.sb("causal_bias_bf", [P, P], BF16)
        m.identb = core.sb("ident_bf", [P, P], BF16)
        m.tri = core.sb("tri", [P, P])
        m.rope = core.ring("rope_tmp", 1, [P, 2, 512])
        m.iq, m.sx, m.sv = core.sb("idx_q", [P, NT, 512]), core.sb("dsa_roped", [P, NT, 384]), core.sb("dsa_v_w_f", [P, NT, 76])
        m.dq, m.dk, m.dv = (core.sb(n, [P, NT, 512]) for n in ("diff_q", "diff_k", "diff_v"))
        m.fqk, m.fv = core.sb("fox_qk", [P, NT, 8, 66]), core.sb("fox_v", [P, NT, 256])
        m.gate, m.mix = core.sb("gate1", [P, NT, D]), core.sb("mix1", [P, NT, D])
        m.qa, m.ka = core.sb("q_t_a", [66, 8, S]), core.sb("k_t_a", [66, 4, S])
        m.qb, m.kb = core.sb("q_t_b", [HD, 8, S]), core.sb("k_t_b", [HD, 8, S])
        m.sk_t, m.sq_t = core.sb("dsa_k_t", [HD, 2, S]), core.sb("dsa_q_t", [HD, 4, S])
        m.iw, m.relu = core.sb("idx_w", [P, NT, 8]), core.ring("relu", 2, [P, 512])
        m.score, m.top8 = core.sb("idx_score", [P, NT, S]), core.sb("top8", [P, 8])
        m.sel = core.sb("sel_bias", [P, NT, S], BF16)
        m.sel_free = []
        m.out_free = []
        m.buf_a, m.buf_b = Mem(), Mem()
        m.buf_a.stat, m.buf_a.prob, m.buf_a.prob_t = core.ring("stat_a", 2, [P, 32]), core.ring("prob_a", 2, [P, 2, S]), core.ring("prob_t_a", 2, [P, 512])
        m.buf_b.stat, m.buf_b.prob, m.buf_b.prob_t = core.ring("stat_b", 2, [P, 32]), core.ring("prob_b", 3, [P, 2, S]), core.ring("prob_t_b", 2, [P, 512])
        m.mod_row, m.sel4 = core.ring("mod_row", 2, [4, WC]), core.sb("sel4", [4, 2])
        m.c_cut = core.sb("mod_c_cut", [P, 4 * KD + P], F32R)
        m.c_vec = core.sb("mod_c", [P, KD, 2])
        m.ms, m.ms2 = core.sb("ms", [P, NT, 4]), core.sb("ms_inv", [P, NT, 4])
        m.fz, m.fa, m.fe, m.fl, m.lf = (core.sb(n, [P, NT, 4]) for n in ("fox_z", "fox_abs", "fox_exp", "fox_ln", "fox_logf"))
        m.bn, m.mv, m.rstd = core.sb("bn1", [P, NT, 12]), core.sb("mean_var1", [P, NT, 2]), core.sb("rstd1", [P, NT, 1])
        got = core.small.start(1, m.cos[:, :, :], io["cos1"])
        core.small.start(1, m.sin[:, :, :], io["sin1"])
        core.small.start(1, m.mask[:, :], io["causal"])
        core.small.start(1, m.tri[:, :], io["tri"])
        got = core.small.start(1, m.lconst[:, :], io["lam_consts"])
        core.small.start(1, m.sel4[:, :], io["sel4"])
        got = core.small.start(1, m.c_vec[:, :, :], io["c2"])
        core.dve.mark(core.dve.after(got).tensor_copy(m.maskb[:, :], m.mask[:, :]))
        dve, act = core.dve, core.act
        zero = dve.mark(dve.after().memset(m.iq[:, 0, 0:4 * KD + P], 0.0))
        z = dve.mark(dve.after(zero).tensor_copy(m.c_cut[:, :], m.iq[:, 0, 0:4 * KD + P]))
        sc = act.mark(act.after(got).activation(m.c_vec[:, :, :], m.c_vec[:, :, :], ACT.Silu))
        cut = m.c_cut[:, 0:4 * KD].rearrange("p (k a) -> p k a", a=4)
        ch = dve.mark(dve.after(sc, z).tensor_copy(cut[:, :, 0:2], m.c_vec[:, :, :]))
        dve.mark(dve.after(ch).tensor_tensor(cut[:, :, 2:4], m.c_vec[:, :, :], cut[:, :, 0:2].bitcast(F32), ALU.subtract))
        core.dve.mark(core.dve.after().tensor_copy(m.identb[:, :], m.ident[:, :]))
        core.restart()
        with nc.Fori(0, LAYERS) as layer:
            first_layer(core, layer, io, m)
            core.restart()
        core.ctx, core.rings = outer, rings


CONV, QK2, V2, RANK, HEADS2 = 512, 256, 512, 16, 4
SPLIT2 = [("val", CONV), ("glu", CONV), ("cgate", CONV), ("gla_q", QK2), ("gla_k", QK2),
          ("gla_v", V2), ("gla_g", V2), ("low_f", RANK), ("low_b", RANK), ("att_q", 512),
          ("att_k", P), ("att_v", P), ("att_g", 512), ("merge0", D), ("merge1", D), ("merge2", D)]
PAIRED = [4 * (i % 2) + i // 2 for i in range(8)]
CHUNKS2 = [[("val", 0, 512)], [("glu", 0, 512)], [("cgate", 0, 512)],
           [("gla_k", 0, 256), ("att_k", 0, 128), ("att_v", 0, 128)],
           [("gla_v", 0, 512)],
           [("low_f", 0, 16), ("low_b", 0, 16), ("gla_q", 0, 256)],
           [("att_q", h * HD, HD) for h in PAIRED],
           [("merge0", 0, 512)], [("merge0", 512, 512)],
           [("gla_g", 0, 512)],
           [("merge1", 0, 512)], [("merge1", 512, 512)],
           [("att_g", h * HD, HD) for h in PAIRED],
           [("merge2", 0, 512)], [("merge2", 512, 512)]]
VAL, GLU, CGATE, KKV, GV, LRQ, AQ, M0A, M0B, GG, M1A, M1B, AG, M2A, M2B = range(len(CHUNKS2))
WIDTH2 = [sum(n for _, _, n in c) for c in CHUNKS2]
OFF2 = offsets(WIDTH2, D)
N_BIAS = len(CHUNKS2) - 3
OFFM = offsets([WC] * 6, D)
OFFY = offsets([WC] * 2, CONV)
TAPS, PAD = 31, 15
GC = 64
AH, AKV = 8, 2
X_TILES, C_TILES, CX = (0, 1), (2, 3), (2, 3, 0, 1)
PAR_COLS = KD + 12 + 4 * TAPS + 4 + 4 + 4 + 3 * KD


def second_layer(core, layer, io, m):
    from contextlib import ExitStack
    nc, pe, act, dve, pool, sp, small = core.nc, core.pe, core.act, core.dve, core.pool, core.sp, core.small
    full = layer < LAYERS - 1
    tiles = X_TILES + C_TILES if full else X_TILES
    every = X_TILES + C_TILES
    n_tok = len(tiles) * P
    streams = [0, 1] if full else [0]

    def pieces(array, offs, c, width, n_k):
        at0 = offs[c]
        return [(array[layer, at0 + kp * P * KP * width:at0 + (kp + 1) * P * KP * width]
                 .rearrange("(p n) -> p n", p=P), width) for kp in range(n_k // KP)]
    order = [("in", c) for c in (KKV, VAL, GLU, LRQ, GV, CGATE, M0A, AQ)]
    order += [("conv", 0), ("in", M0B), ("conv", 1), ("in", GG)]
    order += [("in", M1A), ("gla", 0), ("in", M1B), ("gla", 1), ("in", AG)]
    order += [("in", M2A), ("att", 0), ("in", M2B), ("att", 1), ("out", 0), ("out", 1)]
    for kind, c in order:
        if kind == "in":
            core.stream(pieces(io["w2"], OFF2, c, WIDTH2[c], KD))
        elif kind == "out":
            core.stream(pieces(io["wo2"], OFFO, c, WC, KD))
        else:
            core.stream(pieces(io["wy_" + kind], OFFY, c, WC, CONV // P))

    par, rows = m.par[:, layer, :], m.rows[:, layer, :]
    b_conv = par[:, KD:KD + 12]
    taps = par[:, KD + 12:KD + 12 + 4 * TAPS].rearrange("p (c k) -> p c k", k=TAPS)
    o = KD + 12 + 4 * TAPS
    dw_b, cln_g, cln_b = (par[:, o + 4 * i:o + 4 * i + 4] for i in range(3))
    gla_g, qn_g, kn_g = rows[:, 0:P], rows[:, P:P + HD], rows[:, P + HD:P + 2 * HD]
    shift, scale, gate = m.mod[:, layer, 0], m.scale[:, layer], m.mod[:, layer, 2]

    with ExitStack() as scope:
        core.ctx, outer = scope, core.ctx
        xn = core.ring(f"x_normed{layer}", 2, [P, D])
        mod = core.ring(f"x_mod{layer}", 3, [P, 4, P])
        ss = core.sb(f"sum_sq{layer}", [P, 8])
        hx = {}
        source = lambda t: m.x[:, t, :] if t < 2 else m.acc[:, t, :]
        rinv, squared = {}, {}
        for n, t in enumerate(CX):
            junk = m.sigma[:, 2 * (n % 2):2 * (n % 2) + 2, :].rearrange("p a b -> p (a b)")
            squared[n] = act.mark(act.after(m.ctx_in, *core.x_ready.get(t, ()), squared.get(n - 2), *core.sigma_read).activation(
                junk, source(t), ACT.Square, accum_out=ss[:, t:t + 1]))
            mean = dve.mark(dve.after(squared[n]).tensor_scalar(ss[:, 4 + t:5 + t], ss[:, t:t + 1], 1.0 / D, EPS2, ALU.mult, ALU.add))
            rinv[t] = pool.mark(pool.after(mean).tensor_tensor(ss[:, t:t + 1], ss[:, 4 + t:5 + t], m.half[:, 0:1], ALU.pow))
        st = {}

        def normed(tb):
            t, b = tb
            if b == 0:
                buf, free, slot = xn.take()
                st[t] = (buf, slot, dve.mark(dve.after(rinv[t], *free).tensor_scalar(buf, source(t), ss[:, t:t + 1], None, ALU.mult)))
                hx[t] = []

        def flip(tb):
            t, b = tb
            buf, slot, norm = st[t]
            st[tb] = core.transpose([buf[:, (b + i) * P:(b + i + 1) * P] for i in range(4)], [norm])
            if b > 0:
                xn.free(slot, st[tb][1])

        def scale_shift(tb):
            t, b = tb
            ps, token, pslot = st[tb]
            tmp, free, slot = mod.take()
            s = t // 2
            act.after(token, m.scale_ready, *free)
            for i in range(4):
                a = act.mark(nc.scalar.activation(tmp[:, i, :], ps[:, i * P:(i + 1) * P], ACT.Identity,
                                                  scale=scale[:, b + i, s:s + 1], bias=shift[:, b + i, s:s + 1]))
            core.aux.free(pslot, a)
            st[tb] = (tmp, slot, a)

        def cut(tb):
            t, b = tb
            tmp, slot, a = st[tb]
            hi, lo = m.xh[:, b:b + 4, t * P:(t + 1) * P], m.xl[:, b:b + 4, t * P:(t + 1) * P]
            h = act.mark(act.after(a).activation(hi, tmp, ACT.Copy))
            l = dve.mark(dve.after(h).tensor_tensor(lo, tmp, hi.bitcast(F32), ALU.subtract))
            mod.free(slot, l)
            hx[t] += [h, l]
        for _ in pipeline([(t, b) for t in CX for b in (0, 4)], [normed, flip, scale_shift, cut], [0, 1, 2, 3]):
            pass
        core.rings.remove(xn), core.rings.remove(mod)
        core.ctx = outer
    hx_all = [x for t in tiles for x in hx[t]]
    xs = (m.xh, m.xl, lambda t: hx[t])
    got = {}
    pre_fence = core.fence()
    for e in (pe, act, dve, pool):
        e.after(m.set_up, m.consts_in)

    def bias_of(c):
        def add(out, w):
            nc.tensor.matmul(out, m.sel[:, c - 3, :], m.bias[0:96, layer, 0:w], start=True, stop=False)
        return add

    def need(*keys):
        while not all(k in got for k in keys):
            yield

    def toks(*keys):
        return [x for k in keys for x in got[k]]

    shape = {}

    def ev_val(j, ps, token):
        e = act.mark(act.after(token, *pre_fence).activation(m.cv[:, j, 0:n_tok], ps[:, 0:n_tok], ACT.Identity, bias=b_conv[:, j:j + 1]))
        got["val", j] = [e]
        return [e]

    def ev_glu(j, ps, token):
        e = act.mark(act.after(token, *pre_fence).activation(m.cg[:, j, 0:n_tok], ps[:, 0:n_tok], ACT.Sigmoid, bias=b_conv[:, 4 + j:5 + j]))
        u = m.u[:, j, 0:len(streams), PAD:PAD + S]
        w = lambda b: b[:, j, 0:n_tok].rearrange("p (s t) -> p s t", t=S)
        e2 = pool.mark(pool.after(e, *toks(("val", j)), got["u_zero"]).tensor_tensor(u, w(m.cv), w(m.cg), ALU.mult))
        got["u", j] = [e2]
        return [e]

    def ev_cgate(j, ps, token):
        e = act.mark(act.after(token, *toks(("u", j))).activation(m.cg[:, j, 0:n_tok], ps[:, 0:n_tok], ACT.Silu, bias=b_conv[:, 8 + j:9 + j]))
        got["cg", j] = [e]
        return [e]

    def ev_kkv(t, ps, token):
        e = act.mark(act.after(token).activation(m.kkv[:, t, :], ps[:, :], ACT.Copy))
        got[KKV, t] = [e]
        return [e]

    def ev_gv(t, ps, token):
        e = act.mark(act.after(token).activation(m.gv[:, t, :], ps[:, :], ACT.Copy))
        got[GV, t] = [e]
        return [e]

    def ev_lrq(t, ps, token):
        w = 288 if t in tiles else 32
        e = dve.mark(dve.after(token).tensor_copy(m.lrq[:, t, 0:w], ps[:, 0:w]))
        got[LRQ, t] = [e]
        return [e]

    def ev_aq(t, ps, token):
        e = act.mark(act.after(token, *got["conv_cut"]).activation(m.aq[:, t, :], ps[:, :], ACT.Copy))
        got[AQ, t] = [e]
        return [e]

    def ev_sigma(t, ps, token):
        e = act.mark(act.after(token, *got.get(("sigma_read", t), ())).activation(m.sigma[:, t, :], ps[:, :], ACT.Sigmoid))
        got["sigma", t] = [e]
        return [e]

    def ev_y(branch, c):
        def run(t, ps, token):
            out = m.acc[:, t, c * WC:(c + 1) * WC]
            if branch == 0:
                e = dve.mark(dve.after(token, *toks(("sigma", t)), *pre_fence).tensor_tensor(out, ps[:, :], m.sigma[:, t, :], ALU.mult))
                got["sigma_read", t] = [e]
                got["acc", t, c] = [e]
                return [e]
            e = dve.mark(dve.after(token, *toks(("sigma", t))).tensor_tensor(m.sigma[:, t, :], ps[:, :], m.sigma[:, t, :], ALU.mult))
            e2 = pool.mark(pool.after(e, *toks(("acc", t, c))).tensor_tensor(out, out, m.sigma[:, t, :], ALU.add))
            got["sigma_read", t] = [e2]
            got["acc", t, c] = [e2]
            return [e]
        return run

    def ev_gate(o, key):
        def run(t, ps, token):
            g, free, slot = m.gtmp.take()
            e = act.mark(act.after(token, *free).activation(g, ps[:, :], ACT.Silu))
            e2 = pool.mark(pool.after(e, *toks((key, t))).tensor_tensor(o[:, t, :], o[:, t, :], g, ALU.mult))
            m.gtmp.free(slot, e2)
            got["gated", t] = [e2]
            return [e]
        return run

    def cut_gated(o):
        for t in tiles:
            cols = slice(t * P, (t + 1) * P)
            yield from core.transpose_cut(o[:, t, :], 512, m.yh[:, :, cols], m.yl[:, :, cols], got["gated", t], toks("y_read"))
            got["y", t] = core.last

    def along(steps, side, every):
        for n, step in enumerate(steps):
            yield step
            if (n + 1) % every == 0:
                next(side, None)
        for _ in side:
            pass

    def main():
        def inp(c, tt, ev, **kw):
            yield from core.project(xs, KD, tt, WIDTH2[c], ev, bias_of(c), **kw)
        def y_out(branch, c):
            yield from core.project((m.yh, m.yl, lambda t: got["y", t]), CONV // P, tiles, WC, ev_y(branch, c))
            got["y_read"] = [core.done[-1]]
        yield from inp(KKV, CX, ev_kkv)
        for ev in (ev_val, ev_glu):
            yield from core.project_t((m.xh, m.xl, hx_all), KD, n_tok, ev)
        yield from inp(LRQ, CX, ev_lrq, width_of=lambda t: 288 if t in tiles else 32)
        yield from inp(GV, CX, ev_gv)
        yield from core.project_t((m.xh, m.xl, hx_all), KD, n_tok, ev_cgate)
        yield from inp(M0A, tiles, ev_sigma)
        yield lambda: ("conv_cut" in got)
        for t in tiles:
            got["y", t] = got["conv_cut"]
        yield from inp(AQ, tiles, ev_aq)
        yield from y_out(0, 0)
        yield from inp(M0B, tiles, ev_sigma)
        yield from y_out(0, 1)
        yield lambda: all(("gla_o", t) in got for t in tiles)
        yield from inp(GG, tiles, ev_gate(m.gv, "gla_o"))
        yield from along(inp(M1A, tiles, ev_sigma), cut_gated(m.gv), 3)
        yield from y_out(1, 0)
        yield from inp(M1B, tiles, ev_sigma)
        yield from y_out(1, 1)
        yield lambda: all(("att_o", t) in got for t in tiles)
        yield from inp(AG, tiles, ev_gate(m.aq, "att_o"))
        yield from along(inp(M2A, tiles, ev_sigma), cut_gated(m.aq), 3)
        yield from y_out(2, 0)
        yield from inp(M2B, tiles, ev_sigma)
        yield from y_out(2, 1)
        got["main_end"] = []

    n_st = len(streams)

    def conv():
        yield from need(*[("u", j) for j in range(4)])
        end = {}
        for k in range(TAPS):
            for j in range(4):
                src = m.u[:, j, 0:n_st, k:k + S]
                out = m.cv[:, j, 0:n_tok].rearrange("p (s t) -> p s t", t=S)
                if k == 0:
                    end[j] = dve.mark(dve.after(*toks(("u", j))).tensor_scalar(
                        out, src, taps[:, j, k:k + 1], dw_b[:, j:j + 1], ALU.mult, ALU.add))
                else:
                    end[j] = dve.mark(dve.after(end[j]).scalar_tensor_tensor(
                        out, src, taps[:, j, k:k + 1], out, ALU.mult, ALU.add))
            yield
        ps, free, slot = core.aux.take()
        pe.after(*end.values(), *free)
        for j in range(4):
            ins = nc.tensor.matmul(ps[:, 0:n_tok], m.mean_w[:, :], m.cv[:, j, 0:n_tok], start=j == 0, stop=j == 3)
        mu = pe.mark(ins)
        yield
        sqs = []
        for j in range(4):
            d = dve.mark(dve.after(mu).tensor_tensor(m.cv[:, j, 0:n_tok], m.cv[:, j, 0:n_tok], ps[:, 0:n_tok], ALU.subtract))
            end[j] = d
            sqs.append(act.mark(act.after(d).activation(m.u2[:, j, 0:n_tok], m.cv[:, j, 0:n_tok], ACT.Square)))
            yield
        core.aux.free(slot, d)
        ps, free, slot = core.aux.take()
        pe.after(*sqs, *free)
        for j in range(4):
            ins = nc.tensor.matmul(ps[:, 0:n_tok], m.mean_w[:, :], m.u2[:, j, 0:n_tok], start=j == 0, stop=j == 3)
        var = pe.mark(ins)
        ve = dve.mark(dve.after(var).tensor_scalar(ps[:, 0:n_tok], ps[:, 0:n_tok], EPS2, None, ALU.add))
        sd = act.mark(act.after(ve).activation(ps[:, 0:n_tok], ps[:, 0:n_tok], ACT.Sqrt))
        rs = dve.mark(dve.after(sd).reciprocal(ps[:, 0:n_tok], ps[:, 0:n_tok]))
        yield
        for j in range(4):
            w = m.cv[:, j, 0:n_tok]
            n = dve.mark(dve.after(rs, end[j]).tensor_tensor(w, w, ps[:, 0:n_tok], ALU.mult))
            end[j] = act.mark(act.after(n).activation(w, w, ACT.Silu, scale=cln_g[:, j:j + 1], bias=cln_b[:, j:j + 1]))
        core.aux.free(slot, n)
        m.open_y()
        yield from need(*[("cg", j) for j in range(4)])
        cut = []
        for j in range(4):
            w = m.cv[:, j, 0:n_tok]
            g = pool.mark(pool.after(end[j], *toks(("cg", j))).tensor_tensor(w, w, m.cg[:, j, 0:n_tok], ALU.mult))
            hi, lo = m.yh[:, j, 0:n_tok], m.yl[:, j, 0:n_tok]
            h = act.mark(act.after(g).activation(hi, w, ACT.Copy))
            l = dve.mark(dve.after(h).tensor_tensor(lo, w, hi.bitcast(F32), ALU.subtract))
            cut += [h, l]
            yield
        got["conv_cut"] = cut

    def gla():
        fence = pre_fence
        yield from need(*[(c, t) for c in (KKV, GV, LRQ) for t in every])
        zw = pool.mark(pool.after(*fence).memset(m.wup[:, :], 0.0))
        for d in range(2):
            small.start(8, m.wup[d * RANK:(d + 1) * RANK, d * QK2:(d + 1) * QK2], io["w_gate2"][layer, d], zw)
        wup_in = small.start(8, m.wup[2 * RANK:2 * RANK + 1, :], io["b_gate2"][layer:layer + 1, :], zw)
        one = dve.mark(dve.after(*fence).memset(m.lr_t[32:33, :], 1.0))
        za = pool.mark(pool.after(*fence).memset(m.att[:, :, :, :, :], 0.0))
        z0 = pool.mark(pool.after(*fence).memset(m.st[:, :, :, 0, :], 0.0))
        ps, free, slot = core.aux.take()
        pe.after(*toks(*[(LRQ, t) for t in every]), *free)
        for t in every:
            ins = nc.tensor.transpose(ps[0:32, t * P:(t + 1) * P], m.lrq[:, t, 0:32], m.ident[:, :])
        tr = pe.mark(ins)
        lr = act.mark(act.after(tr, *fence).activation(m.lr_t[0:32, :], ps[0:32, :], ACT.Copy))
        core.aux.free(slot, lr)
        yield
        state = {}
        last_state = None
        inter_read = []

        def gates(t):
            i = t % 2
            out = t in tiles
            ps, free, slot = core.aux.take()
            zt = pe.mark(pe.after(lr, one, wup_in, *free).matmul(ps[:, :], m.lr_t[0:33, t * P:(t + 1) * P], m.wup[0:33, :], start=True, stop=True))
            e = act.mark(act.after(zt, *fence, *state.get("tmp_read", ())).activation(m.e3[:, i, :], ps[:, :], ACT.Abs))
            e = act.mark(act.after(e).activation(m.e3[:, i, :], m.e3[:, i, :], ACT.Exp, scale=-1.0))
            e = act.mark(act.after(e).activation(m.e3[:, i, :], m.e3[:, i, :], ACT.Ln, bias=1.0))
            la = dve.mark(dve.after(e, *fence, *state.get("la_read", ())).scalar_tensor_tensor(
                m.la[:, :], ps[:, :], 0.0, m.e3[:, i, :], ALU.min, ALU.subtract))
            core.aux.free(slot, la)
            yield
            n = 1.0 / 16.0
            ps3, free3, slot3 = core.aux.take()
            pe.after(la, *free3)
            for dp in range(4):
                ins = nc.tensor.matmul(ps3[:, 2 * dp:2 * dp + 2], m.la[:, dp * P:(dp + 1) * P], m.halves[:, :], start=True, stop=True)
            tot = pe.mark(ins)
            dec = act.mark(act.after(tot, *state.get("dec_read", ())).activation(
                m.dec[:, :, 2 * i:2 * i + 2], ps3[:, 0:8].rearrange("p (a b) -> p a b", b=2), ACT.Exp, scale=n))
            core.aux.free(slot3, dec)
            state["dec"] = dec
            ps2, free2, slot2 = core.aux.take()
            pe.after(*free2)
            for d in range(2):
                ins = nc.tensor.matmul(ps2[:, d * QK2:(d + 1) * QK2], m.tri2[:, 2 + d, :], m.la[:, d * QK2:(d + 1) * QK2], start=True, stop=True)
            left = pe.mark(ins)
            state["la_read"] = [left]
            e3 = act.mark(act.after(left, la).activation(m.e3[:, i, :], ps2[:, :], ACT.Exp, scale=n))
            core.aux.free(slot2, e3)
            if out:
                ps1, free1, slot1 = core.aux.take()
                pe.after(*free1)
                for d in range(2):
                    ins = nc.tensor.matmul(ps1[:, d * QK2:(d + 1) * QK2], m.tri2[:, d, :], m.la[:, d * QK2:(d + 1) * QK2], start=True, stop=True)
                cum = pe.mark(ins)
                state["la_read"] = [cum]
                e1 = act.mark(act.after(cum, *state.get("tmp_read", ())).activation(m.e1[:, :], ps1[:, :], ACT.Exp, scale=n))
                e2 = act.mark(act.after().activation(m.e2[:, :], ps1[:, :], ACT.Exp, scale=-n))
                core.aux.free(slot1, e2)
            v = lambda b: b.rearrange("p (d n) -> p d n", d=2)
            k_b = spread(m.kkv[:, t, 0:QK2], [P, 2, QK2])
            ks = pool.mark(pool.after(e3, *toks((KKV, t))).tensor_tensor(v(m.e3[:, i, :]), v(m.e3[:, i, :]), k_b, ALU.mult))
            state["ks", t] = ks
            yield
            if out:
                q_b = spread(m.lrq[:, t, 32:32 + QK2], [P, 2, QK2])
                qi = dve.mark(dve.after(e1, *toks((LRQ, t))).scalar_tensor_tensor(v(m.e1[:, :]), q_b, GC ** -0.5, v(m.e1[:, :]), ALU.mult, ALU.mult))
                ki = pool.mark(pool.after(e2).tensor_tensor(v(m.e2[:, :]), v(m.e2[:, :]), k_b, ALU.mult))
                ps, tok_q, slot = core.transpose([m.e1[:, dp * P:(dp + 1) * P] for dp in range(4)], [qi])
                view = ps[:, :].rearrange("p (a t) -> p a t", a=4)
                qt = act.mark(act.after(tok_q, *fence, *inter_read).activation(m.q_t[:, :, i, :], view, ACT.Copy))
                core.aux.free(slot, qt)
                ps, tok_k, slot = core.transpose([m.e2[:, dp * P:(dp + 1) * P] for dp in range(4)], [ki])
                kt = dve.mark(dve.after(tok_k, *fence, cum).tensor_copy(m.k_t[:, :], ps[:, :]))
                core.aux.free(slot, kt)
                state["tmp_read"] = [tok_q, tok_k]
                yield
                for par in range(2):
                    ps, free, slot = core.aux.take()
                    rows = slice(par * HD, (par + 1) * HD)
                    pe.after(qt, kt, *free)
                    for dp in range(4):
                        ins = nc.tensor.matmul(ps[:, dp * P:(dp + 1) * P], m.k_t[rows, dp * P:(dp + 1) * P],
                                               m.q_t[rows, dp, i, :], start=True, stop=True)
                    a = pe.mark(ins)
                    am = dve.mark(dve.after(a, za, *inter_read).copy_predicated(m.att[:, i, par, :, :], m.gmask[:, :, :],
                                                                     ps[:, :].rearrange("p (a t) -> p a t", a=4)))
                    core.aux.free(slot, am)
                    state["att", t, par] = am
                state["la_read"] = [a]
                yield

        for s in (1, 0):
            tl = C_TILES if s else X_TILES
            out = tl[0] in tiles
            for t in tl:
                yield from gates(t)
            upd = last_state or [z0]
            for step in range(4):
                psd = []
                for d in range(2):
                    c = step if d == 0 else 3 - step
                    i, half = c // 2, c % 2
                    rows = slice(half * GC, (half + 1) * GC)
                    ps, free, slot = core.aux.take()
                    pe.after(state["ks", tl[i]], *free, *toks((GV, tl[i])))
                    for h in range(HEADS2):
                        par, pair = h % 2, h // 2
                        ins = nc.tensor.matmul(ps[par * HD:(par + 1) * HD, pair * P:(pair + 1) * P],
                                               m.e3[rows, i, d * QK2 + h * HD:d * QK2 + (h + 1) * HD],
                                               m.gv[rows, tl[i], h * P:(h + 1) * P], start=True, stop=True)
                    con = pe.mark(ins)
                    ends = []
                    for pair in range(2):
                        ends.append(dve.mark(dve.after(con, *upd, *inter_read, state["dec"]).scalar_tensor_tensor(
                            m.st[:, d, pair, step + 1, :], m.st[:, d, pair, step, :],
                            m.dec[:, 2 * d + pair, c:c + 1], ps[:, pair * P:(pair + 1) * P], ALU.mult, ALU.add)))
                    core.aux.free(slot, ends[-1])
                    psd += ends
                upd = psd
                yield
            state["dec_read"] = upd
            state["tmp_read"] = state.get("tmp_read", []) + [con]
            if out:
                for t in tl:
                    i = t % 2
                    be, fe, se = core.aux.take()
                    bo, fo, so = core.sum_bank.take()
                    pe.after(*fe, *fo, *upd, state["att", t, 0], state["att", t, 1])
                    for h in range(HEADS2):
                        par, pair = h % 2, h // 2
                        bk = (be, bo)[par][:, pair * P:(pair + 1) * P]
                        rows = slice(par * HD, (par + 1) * HD)
                        v_h = m.gv[:, t, h * P:(h + 1) * P]
                        for d in range(2):
                            nc.tensor.matmul(bk, m.att[:, i, par, 2 * d + pair, :], v_h, start=d == 0, stop=False)
                        for d in range(2):
                            for half in range(2):
                                c = 2 * i + half
                                step = c if d == 0 else 3 - c
                                hs = slice(half * GC, (half + 1) * GC)
                                ins = nc.tensor.matmul(bk[hs, :], m.q_t[rows, 2 * d + pair, i, hs],
                                                       m.st[rows, d, pair, step, :], start=False, stop=d == 1)
                    token = pe.mark(ins)
                    inter_read = [token]
                    og = m.gv[:, t, :].rearrange("p (a b n) -> p a b n", a=2, b=2)
                    bv = lambda b: b[:, 0:256].rearrange("p (a n) -> p a n", a=2)
                    o1 = act.mark(act.after(token, *fence).activation(og[:, :, 0, :], bv(be), ACT.Copy))
                    o2 = dve.mark(dve.after(token, *fence).tensor_copy(og[:, :, 1, :], bv(bo)))
                    core.aux.free(se, o1)
                    core.sum_bank.free(so, o2)
                    yield
                    g, gf, gs = m.gtmp.take()
                    sq = pool.mark(pool.after(o1, o2, *gf).tensor_tensor(g, m.gv[:, t, :], m.gv[:, t, :], ALU.mult))
                    sm = dve.mark(dve.after(sq).tensor_reduce(m.gms[:, t, 0:4], g.rearrange("p (h n) -> p h n", h=4), AXX, ALU.add))
                    m.gtmp.free(gs, sm)
                    me = dve.mark(dve.after(sm).tensor_scalar(m.gms[:, t, 4:8], m.gms[:, t, 0:4], 1.0 / P, EPS2, ALU.mult, ALU.add))
                    iv = pool.mark(pool.after(me).tensor_tensor(m.gms[:, t, 0:4], m.gms[:, t, 4:8], m.half[:, 0:4], ALU.pow))
                    ov = m.gv[:, t, :].rearrange("p (h n) -> p h n", h=4)
                    n1 = pool.mark(pool.after(iv).tensor_tensor(ov, ov, spread(gla_g, [P, 4, P]), ALU.mult))
                    n2 = dve.mark(dve.after(n1).tensor_tensor(ov, ov, m.gms[:, t, 0:4].unsqueeze(2).to_broadcast([P, 4, P]), ALU.mult))
                    got["gla_o", t] = [n2]
                    yield
            if s == 1:
                cp = pool.mark(pool.after(*upd, *inter_read).tensor_copy(m.st[:, :, :, 0, :], m.st[:, :, :, 4, :]))
                last_state = [cp] + upd
                inter_read = inter_read + [cp]

    def norm_rope(src, heads, g, t, ready, roped):
        v = src.rearrange("p (h d) -> p h d", d=HD)
        n = heads * HD
        a, free, slot = m.gtmp.take()
        b, free_b, slot_b = m.gtmp.take()
        a, b = a[:, 0:n], b[:, 0:n]
        st = m.ams
        sq = pool.mark(pool.after(*ready, *free).tensor_tensor(a, src, src, ALU.mult))
        sm = dve.mark(dve.after(sq, *got.get("ams_read", ())).tensor_reduce(st[:, 0, 0:heads], a.rearrange("p (h d) -> p h d", d=HD), AXX, ALU.add))
        me = dve.mark(dve.after(sm).tensor_scalar(st[:, 1, 0:heads], st[:, 0, 0:heads], 1.0 / HD, EPS2, ALU.mult, ALU.add))
        iv = pool.mark(pool.after(me).tensor_tensor(st[:, 2, 0:heads], st[:, 1, 0:heads], m.half[:, 0:heads], ALU.pow))
        n1 = pool.mark(pool.after().tensor_tensor(v, v, spread(g, [P, heads, HD]), ALU.mult))
        n2 = dve.mark(dve.after(iv, n1).tensor_tensor(v, v, st[:, 2, 0:heads].unsqueeze(2).to_broadcast([P, heads, HD]), ALU.mult))
        got["ams_read"] = [n2]
        if not roped:
            m.gtmp.free(slot, sm)
            m.gtmp.free(slot_b, *free_b)
            return n2
        q = HD // 4
        w = lambda x: x.rearrange("p (h a b i) -> p h a b i", a=2, b=2, i=q)
        av = a.rearrange("p (h d) -> p h d", d=HD)
        one = dve.mark(dve.after(n2, sm, *free_b).tensor_tensor(av, v, spread(m.cos[:, t, :], [P, heads, HD]), ALU.mult))
        sn = m.sin[:, t, :].rearrange("p (a b i) -> p a b i", a=2, b=2)
        for x in range(2):
            for half in range(2):
                two = dve.mark(dve.after().tensor_tensor(
                    w(b)[:, :, x, half, :], w(src)[:, :, x, 1 - half, :], spread(sn[:, x, half, :], [P, heads, q]), ALU.mult))
        end = pool.mark(pool.after(two).tensor_tensor(src, a, b, ALU.add))
        m.gtmp.free(slot, end)
        m.gtmp.free(slot_b, end)
        return end

    k_end, q_end = {}, {}

    def att_heads():
        yield from need(*[(KKV, t) for t in every])
        for t in every:
            k_end[t] = norm_rope(m.kkv[:, t, QK2:QK2 + P], AKV, kn_g, t, toks((KKV, t)), t < 2)
            yield
        yield from need(*[(AQ, t) for t in tiles])
        for t in tiles:
            q_end[t] = norm_rope(m.aq[:, t, :], AH, qn_g, t, toks((AQ, t)), t < 2)
            yield
        got["heads"] = []

    def att():
        fence = core.fence()
        for e in (act, dve, pool):
            e.after(*fence)
        yield from need("heads")
        def pairs(src, tl, dst, scale, ready, odd):
            ps, free, slot = core.aux.take()
            pe.after(*ready, *free)
            for i, t in enumerate(tl):
                ins = nc.tensor.transpose(ps[:, i * P:(i + 1) * P], src(t), m.ident[:, :])
            token = pe.mark(ins)
            n = len(tl) * P
            if odd:
                e = act.mark(act.after(token).activation(dst[:, 0:n], ps[:, 0:n], ACT.Copy, scale=scale))
            else:
                e = dve.mark(dve.after(token).tensor_scalar(dst[:, 0:n], ps[:, 0:n], scale, None, ALU.mult))
            core.aux.free(slot, e)
            return e
        ready = [pairs(lambda t: m.kkv[:, t, QK2:QK2 + P], every, m.ak_t, 1.0, [k_end[t] for t in every], False)]
        yield
        for j in range(AH // 2):
            ready.append(pairs(lambda t: m.aq[:, t, j * P:(j + 1) * P], tiles, m.aq_t[:, j, :], HD ** -0.5, [q_end[t] for t in tiles], j % 2 == 0))
            yield
        by_pair = lambda x: x.rearrange("p (a b d) -> p a b d", b=2, d=HD)
        for qt in tiles:
            key_tiles = every if qt < 2 else C_TILES
            keys = len(key_tiles) * P
            k0 = key_tiles[0] * P
            n_maps = 512 // keys
            osum, ofree, oslot = core.sum_bank.take()
            stat, sfree, sslot = m.astat.take()
            top_of, sum_of, inv_of = (stat[:, i * AH:(i + 1) * AH] for i in range(3))
            st = {}

            def scores(j):
                ps, free, slot = core.aux.take()
                pe.after(*ready, *free)
                for i in range(n_maps):
                    h = j * n_maps + i
                    rows = slice(h // 4 * HD, (h // 4 + 1) * HD)
                    ins = nc.tensor.matmul(ps[:, i * keys:(i + 1) * keys], m.aq_t[rows, h % 4, qt * P:(qt + 1) * P],
                                           m.ak_t[rows, k0:k0 + keys], start=True, stop=True)
                st[j] = [ps, slot, pe.mark(ins)]

            def soft(j):
                ps, slot, token = st[j]
                h = j * n_maps
                view = ps[:, :].rearrange("p (a b) -> p a b", a=n_maps)
                top = dve.mark(dve.after(token, *sfree).tensor_reduce(top_of[:, h:h + n_maps], view, AXX, ALU.max, negate=True))
                pm, free, pslot = m.aprob.take()
                act.after(top, *free)
                for i in range(n_maps):
                    end = act.mark(nc.scalar.activation(pm[:, i * keys:(i + 1) * keys], ps[:, i * keys:(i + 1) * keys], ACT.Exp,
                                                        bias=top_of[:, h + i:h + i + 1], accum_out=sum_of[:, h + i:h + i + 1]))
                core.aux.free(slot, end)
                st["inv"] = dve.mark(dve.after(end).reciprocal(inv_of[:, h:h + n_maps], sum_of[:, h:h + n_maps]))
                st[j] = [pm, pslot, end]

            def flip(j):
                pm, pslot, end = st[j]
                ps, token, slot = core.transpose([pm[:, b * P:(b + 1) * P] for b in range(4)], [end])
                m.aprob.free(pslot, token)
                pt, pfree, ptslot = m.aprob_t.take()
                if j % 2:
                    end = act.mark(act.after(token, *pfree).activation(pt, ps[:, :], ACT.Copy))
                else:
                    end = dve.mark(dve.after(token, *pfree).tensor_copy(pt, ps[:, :]))
                core.aux.free(slot, end)
                st[j] = [pt, ptslot, end]

            def values(j):
                pt, ptslot, end = st[j]
                pe.after(end, *(ofree if j == 0 else ()))
                nb = len(key_tiles)
                for i in range(n_maps):
                    h = j * n_maps + i
                    kh, at = h // 4, (h % 4) * 2 + h // 4
                    for b, t in enumerate(key_tiles):
                        ins = nc.tensor.matmul(osum[:, at * HD:(at + 1) * HD], pt[:, (i * nb + b) * P:(i * nb + b + 1) * P],
                                               m.kkv[:, t, QK2 + P + kh * HD:QK2 + P + (kh + 1) * HD],
                                               start=b == 0, stop=b == nb - 1)
                st["sum"] = pe.mark(ins)
                m.aprob_t.free(ptslot, st["sum"])
            yield from pipeline(list(range(AH // n_maps)), [scores, soft, flip, values], LAGS2)
            end = dve.mark(dve.after(st["sum"], st["inv"]).tensor_tensor(
                by_pair(m.ao[:, qt, :]), by_pair(osum[:, :]),
                inv_of.rearrange("p (b a) -> p a b", b=2).unsqueeze(3).to_broadcast([P, AH // 2, 2, HD]), ALU.mult))
            m.astat.free(sslot, end)
            core.sum_bank.free(oslot, end)
            got["att_o", qt] = [end]
            yield

    with ExitStack() as scope:
        core.ctx, outer = scope, core.ctx
        base_rings = list(core.rings)

        def open_gla(ctx):
            core.ctx = ctx
            m.wup, m.lr_t = core.sb(f"w_up{layer}", [33, 512]), core.sb(f"low_t{layer}", [33, 512])
            m.att = core.sb(f"gla_att{layer}", [P, 2, 2, 4, P])
            m.st = core.sb(f"gla_state{layer}", [P, 2, 2, 5, P])
            m.la, m.e1, m.e2 = (core.sb(f"{n}{layer}", [P, 512]) for n in ("gla_la", "gla_e1", "gla_e2"))
            m.e3 = core.sb(f"gla_k_state{layer}", [P, 2, 512])
            m.q_t, m.k_t = core.sb(f"gla_q_t{layer}", [P, 4, 2, P]), m.la
            m.dec, m.gms = core.sb(f"gla_decay{layer}", [P, 4, 4]), core.sb(f"gla_ms{layer}", [P, 4, 8])
            core.ctx = outer

        def open_att(ctx):
            core.ctx = ctx
            m.aq_t, m.ak_t = core.sb(f"att_q_t{layer}", [P, AH // 2, 512]), core.sb(f"att_k_t{layer}", [P, 512])
            m.aprob, m.aprob_t = core.ring(f"att_p{layer}", 3, [P, 512]), core.ring(f"att_pt{layer}", 2, [P, 512])
            m.astat = core.ring(f"att_stat{layer}", 2, [P, 24])
            m.ao = m.aq
            core.ctx = outer

        right = ExitStack()
        m.u = right.enter_context(nc.sbuf_tensor(f"conv_u{layer}", [P, 4, 2, S + 2 * PAD], F32, side="right"))

        def open_y():
            right.close()
            m.yh, m.yl = (scope.enter_context(nc.sbuf_tensor(f"{n}{layer}", [P, 4, 2 * S], F32R, side="right"))
                          for n in ("y_hi", "y_lo"))
        m.open_y = open_y
        got["u_zero"] = pool.mark(pool.after(*pre_fence).memset(m.u[:, :, :, :], 0.0))

        def attentions():
            with ExitStack() as c:
                open_gla(c)
                yield from gla()
            with ExitStack() as c:
                open_att(c)
                yield from att()
                yield from need("main_end")
        weave(main(), [conv(), attentions(), att_heads()], lambda n: RATES2[layer])

    proj_done = core.done[-1]
    fence = core.fence()
    ready = {}
    for t in tiles:
        cols = slice(t * P, (t + 1) * P)
        for _ in core.transpose_cut(m.acc[:, t, :], D, m.xh[:, :, cols], m.xl[:, :, cols],
                                    toks(("acc", t, 0), ("acc", t, 1)), (proj_done,)):
            pass
        ready[t] = core.last
    flipped = core.fence()
    dve.after(*flipped)
    diag_scope = ExitStack()
    diag = diag_scope.enter_context(nc.sbuf_tensor(f"gate_diag{layer}", [P, 4, P], F32))
    gates, dread = [], {}
    for s in streams:
        for c in range(2):
            ps, free, slot = core.aux.take()
            for i in range(4):
                j = (s * 2 + c) * 4 + i
                buf = diag[:, j % 4, :]
                d = dve.mark(dve.after(dread.get(j - 4)).tensor_scalar(buf, m.ident[:, :], gate[:, 4 * c + i, s:s + 1], None, ALU.mult))
                token = pe.mark(pe.after(d, *free).matmul(ps[:, i * P:(i + 1) * P], m.ones[:, :], buf, start=True, stop=True))
                dread[j] = token
            e = act.mark(act.after(token, *flipped).activation(m.acc[:, s, c * WC:(c + 1) * WC], ps[:, :], ACT.Copy))
            core.aux.free(slot, e)
            gates.append(e)
    diag_scope.close()
    if full:
        ctx_again = small.start(9, m.acc[:, 2:4, :], io["ctx2"].rearrange("(t p) d -> p t d", p=P), *flipped)
    else:
        ctx_again = None
    core.x_ready, core.sigma_read = {}, fence

    def add_gated(c):
        def run(t, ps, token):
            cs = slice(c * WC, (c + 1) * WC)
            g, free, slot = m.gtmp.take()
            dst = m.x[:, t, cs] if t < 2 else m.acc[:, t, cs]
            e = dve.mark(dve.after(token, *gates, *free).tensor_tensor(g, ps[:, :], m.acc[:, t // 2, cs], ALU.mult))
            e2 = pool.mark(pool.after(e, ctx_again).tensor_tensor(dst, dst, g, ALU.add))
            m.gtmp.free(slot, e2)
            core.x_ready.setdefault(t, []).append(e2)
            if not full:
                small.start(10, io["y"].rearrange("(t p) d -> p t d", p=P)[:, t, cs], dst, e2)
            return [e]
        return run
    for c in range(2):
        for _ in core.project((m.xh, m.xl, lambda t: ready[t]), KD, tiles, WC, add_gated(c)):
            pass


RATES2 = [[0.5, 0.75, 0.25], [1.0, 1.25, 0.5]]


def second_block(core, io, shared):
    from contextlib import ExitStack
    nc, small = core.nc, core.small
    with ExitStack() as ctx:
        core.ctx, outer = ctx, core.ctx
        m = Mem()
        m.ident, m.ones, m.half, m.x = shared.ident, shared.ones, shared.half, shared.x
        m.mod_cols = shared.mod_cols
        core.piece_slots("2", 4, 3)
        core.share_banks(4, 3)
        m.xh, m.xl = core.sb("x_hi2", [P, KD, 2 * S], F32R), core.sb("x_lo2", [P, KD, 2 * S], F32R)
        m.acc, m.sigma = core.sb("merged", [P, 4, D]), core.sb("sigma", [P, 4, WC])
        m.cv, m.u2 = (m.acc[:, i:i + 2, :].rearrange("p a (b t) -> p (a b) t", t=2 * S) for i in (0, 2))
        m.kkv, m.gv = core.sb("gla_k_att_kv", [P, 4, 512]), core.sb("gla_v", [P, 4, 512])
        m.lrq, m.aq = core.sb("low_gla_q", [P, 4, 288]), core.sb("att_q", [P, 4, 512])
        m.par, m.rows = core.sb("par2", [P, LAYERS, PAR_COLS]), core.sb("rows2", [P, LAYERS, 2 * P])
        m.bias, m.sel = core.sb("bias_parts", [96, LAYERS, WC], BF16), core.sb("bias_sel", [96, N_BIAS, P], BF16)
        m.cg, m.ams = m.aq, core.sb("att_ms", [P, 3, 8])
        m.scale = core.sb("scale", [P, LAYERS, KD, 2])
        m.cos, m.sin = core.sb("cos2", [P, NT, HD]), core.sb("sin2", [P, NT, HD])
        m.tri2, m.halves = core.sb("tri2", [P, 4, P]), core.sb("halves", [P, 2])
        m.gmask = core.sb("gla_mask", [P, 4, P], mybir.dt.uint32)
        m.mean_w = core.sb("mean_w", [P, P])
        m.gtmp = core.ring("gate_tmp", 2, [P, 512])
        temporary = ExitStack()
        m.bias_part = temporary.enter_context(nc.sbuf_tensor("bias_part", [96, LAYERS, WC], BF16))
        small, dve = core.small, core.dve
        m.ctx_in = small.start(7, m.acc[:, 2:4, :], io["ctx2"].rearrange("(t p) d -> p t d", p=P))
        z = dve.mark(dve.after().memset(m.kkv[0:96, 0:2, :], 0.0))
        sel_rows = m.acc[0:96, 0:2, :].rearrange("p a b -> p (a b)")[:, 0:N_BIAS * P]
        par_in = small.start(4, m.par[:, :, :], io["par2"].rearrange("l p n -> p l n"))
        sel_in = small.start(6, sel_rows, io["bias_sel"])
        for i in range(3):
            bias_in = small.start(5, m.kkv[32 * i:32 * i + N_BIAS, 0:2, :], io["bias2"].rearrange("l c n -> c l n"), z)
        for name, place in (("cos2", m.cos[:, :, :]), ("sin2", m.sin[:, :, :]), ("tri2", m.tri2[:, :, :]),
                            ("halves", m.halves[:, :]), ("gla_mask", m.gmask[:, :, :])):
            m.consts_in = small.start(3, place, io[name])
        rows_in = small.start(4, m.rows[:, :, :].rearrange("p l n -> p (l n)"),
                              io["rows2"].rearrange("l n -> (l n)").partition_broadcast(P))
        dve.after(rows_in)
        m.mod = m.mod_cols[:, :].rearrange("p (l a k s) -> p l a k s", l=LAYERS, a=3, k=KD)
        for l in range(LAYERS):
            b_mod = m.par[:, l, PAR_COLS - 3 * KD:PAR_COLS].rearrange("p (a k) -> p a k", a=3)
            mb = dve.mark(dve.after(par_in).tensor_tensor(m.mod[:, l], m.mod[:, l], b_mod.unsqueeze(3).to_broadcast([P, 3, KD, 2]), ALU.add))
            s1 = dve.mark(dve.after(mb).tensor_scalar(m.scale[:, l], m.mod[:, l, 1], 1.0, None, ALU.add))
            m.scale_ready = dve.mark(dve.after(s1).tensor_tensor(m.scale[:, l], m.scale[:, l],
                                                                 m.par[:, l, 0:KD].unsqueeze(2).to_broadcast([P, KD, 2]), ALU.mult))
        dve.mark(dve.after(sel_in).tensor_copy(m.sel[:, :, :].rearrange("p a b -> p (a b)"), sel_rows))
        raw, rest = m.kkv[0:96, 0:2, :], m.kkv[0:96, 2:4, :]
        part = m.bias_part[:, :, :]
        t0 = dve.mark(dve.after(bias_in).tensor_copy(part, raw))
        b0 = dve.mark(dve.after(t0).tensor_copy(m.bias[0:32, :, :], part[0:32]))
        r1 = dve.mark(dve.after().tensor_tensor(rest, raw, part, ALU.subtract))
        t1 = dve.mark(dve.after(r1).tensor_copy(part, rest))
        b1 = dve.mark(dve.after(t1).tensor_copy(m.bias[32:64, :, :], part[32:64]))
        r2 = dve.mark(dve.after().tensor_tensor(raw, rest, part, ALU.subtract))
        dve.mark(dve.after(r2).tensor_copy(m.bias[64:96, :, :], raw[64:96]))
        m.set_up = dve.mark(dve.after().memset(m.mean_w[:, :], 1.0 / CONV))
        temporary.close()
        core.x_ready, core.sigma_read = {}, []
        for layer in range(LAYERS):
            second_layer(core, layer, io, m)
        core.sp.after((small.sems[10], small.counts[10]))
        core.ctx = outer


def shared_memory(core, io):
    m = Mem()
    m.ident, m.ones = core.sb("ident", [P, P]), core.sb("ones", [P, P])
    m.half = core.sb("minus_half", [P, 32])
    m.mod_cols = core.sb("mod_cols", [P, LAYERS * MOD_COLS])
    m.x = core.sb("x", [P, NT, D])
    core.ident = m.ident
    core.small.start(0, m.ident[:, :], io["ident"])
    got = core.small.start(0, m.x[:, :, :], io["x"].rearrange("(t p) d -> p t d", p=P))
    core.dve.mark(core.dve.after(got).memset(m.ones[:, :], 1.0))
    core.dve.mark(core.dve.after().memset(m.half[:, :], -0.5))
    return m


def program(nc, io):
    from contextlib import ExitStack
    with ExitStack() as ctx:
        core = Core(nc, ctx)
        core.loaded = []
        m = shared_memory(core, io)
        first_block(core, io, m)
        if "dbg_x1" not in io:
            second_block(core, io, m)
        else:
            t = core.small.start(2, io["dbg_x1"].rearrange("(t p) d -> p t d", p=P), m.x[:, :, :])
            core.sp.after(t)


def chunk_pieces(w, cols):
    k = w.shape[0] // P
    part = w[:, cols]
    n = part.shape[1]
    return part.reshape(k // KP, KP, P, n).transpose(0, 2, 1, 3).reshape(-1)


def columns(split, chunk):
    at, start = {}, 0
    for name, n in split:
        at[name] = start
        start += n
    return np.concatenate([np.arange(at[name] + first, at[name] + first + n) for name, first, n in chunk])


def rope_1():
    inv = np.float32(10000.0) ** (-np.arange(0, HD, 2, dtype=np.float32) / np.float32(HD))
    ang = np.arange(S, dtype=np.float32)[:, None] * inv[None, :]
    cos, sin = np.cos(ang), np.sin(ang)
    lay = lambda a: np.ascontiguousarray(a.reshape(NT, P, HD).transpose(1, 0, 2).astype(np.float32))
    return lay(np.concatenate([cos, cos], 1)), lay(np.concatenate([-sin, sin], 1))


def rope_2():
    rows, n_freq = S // 64, HD // 4
    pos_r = np.repeat(np.arange(rows, dtype=np.float32), 64)
    pos_c = np.tile(np.arange(64, dtype=np.float32), rows)
    freqs = np.float32(10000.0) ** (-np.arange(n_freq, dtype=np.float32) / np.float32(n_freq))
    ar, ac = pos_r[:, None] * freqs, pos_c[:, None] * freqs
    cos = np.concatenate([np.cos(ar), np.cos(ar), np.cos(ac), np.cos(ac)], 1)
    sin = np.concatenate([-np.sin(ar), np.sin(ar), -np.sin(ac), np.sin(ac)], 1)
    lay = lambda a: np.ascontiguousarray(a.reshape(NT, P, HD).transpose(1, 0, 2).astype(np.float32))
    return lay(cos), lay(sin)


def lay_out(inp):
    a = {}
    f = lambda n: np.asarray(inp[n])
    a["x"] = f("x").reshape(S, D)
    w, wo = f("w_in"), f("w_out")
    cols = [columns(SPLIT1, c) for c in CHUNKS1]
    a["w1"] = np.stack([np.concatenate([chunk_pieces(w[l], c) for c in cols]) for l in range(LAYERS)])
    a["wo1"] = np.stack([np.concatenate([chunk_pieces(wo[l], slice(c * WC, (c + 1) * WC)) for c in range(2)])
                         for l in range(LAYERS)])
    a["small1"] = np.concatenate([f("b_f"), f("lam_q1"), f("lam_k1"), f("lam_q2"), f("lam_k2"),
                                  f("g_subln"), f("ln_g"), f("ln_b")], axis=1)
    a["cos1"], a["sin1"] = rope_1()
    w, wm, bi = f("w_in_2"), f("w_mod_2"), f("b_in_2")
    cols = [columns(SPLIT2, c) for c in CHUNKS2]
    per = lambda fn: np.stack([fn(l) for l in range(LAYERS)])
    halves = lambda mat, n: np.concatenate([chunk_pieces(mat, slice(c * WC, (c + 1) * WC)) for c in range(n)])
    a["w2"] = per(lambda l: np.concatenate([chunk_pieces(w[l], c) for c in cols]))
    a["wm2"] = per(lambda l: halves(wm[l], 6))
    a["wo2"] = per(lambda l: halves(f("w_out_2")[l], 2))
    for n, key in (("conv", "w_conv_out_2"), ("gla", "w_gla_out_2")):
        a["wy_" + n] = per(lambda l: halves(f(key)[l], 2))
    rows = np.concatenate([np.arange(h * HD, (h + 1) * HD) for h in PAIRED])
    a["wy_att"] = per(lambda l: halves(f("w_attn_out_2")[l][rows], 2))
    col = lambda v: v.reshape(-1, P).T
    dw = f("conv_dw_w_2")
    a["par2"] = per(lambda l: np.concatenate(
        [col(f("norm_g_2")[l]), col(bi[l][cols[0]]), col(bi[l][cols[1]]), col(bi[l][cols[2]]),
         dw[l].T.reshape(4, P, TAPS).transpose(1, 0, 2).reshape(P, 4 * TAPS),
         col(f("conv_dw_b_2")[l]), col(f("conv_ln_g_2")[l]), col(f("conv_ln_b_2")[l]),
         col(f("b_mod_2")[l])], axis=1))
    a["rows2"] = np.concatenate([f("gla_norm_g_2"), f("q_norm_g_2"), f("k_norm_g_2")], axis=1)
    a["bias2"] = np.zeros((LAYERS, N_BIAS, WC), np.float32)
    for l in range(LAYERS):
        for c in range(N_BIAS):
            a["bias2"][l, c, :WIDTH2[c + 3]] = bi[l][cols[c + 3]]
    a["w_gate2"], a["b_gate2"] = f("gla_w_gate_2"), f("gla_b_gate_2").reshape(LAYERS, 2 * QK2)
    a["c2"] = np.stack([f("c_2").reshape(KD, P).T, f("c_ctx_2").reshape(KD, P).T], axis=2)
    a["ctx2"] = f("ctx_2").reshape(S, D)
    a["cos2"], a["sin2"] = rope_2()
    i = np.arange(P)
    t_from, t_to = i[:, None], i[None, :]
    same = t_from // GC == t_to // GC
    a["tri2"] = np.stack([same & (t_from <= t_to), same & (t_from >= t_to),
                          same & (t_from > t_to), same & (t_from < t_to)], axis=1).astype(np.float32)
    a["halves"] = np.stack([i < GC, i >= GC], axis=1).astype(np.float32)
    a["gla_mask"] = np.stack([same & (t_from <= t_to)] * 2 + [same & (t_from >= t_to)] * 2, axis=1).astype(np.uint32)
    sel = np.zeros((96, N_BIAS, P), np.float32)
    for c in range(N_BIAS):
        sel[[c, 32 + c, 64 + c], c, :] = 1.0
    a["bias_sel"] = sel.reshape(96, N_BIAS * P)
    i = np.arange(P)
    a["ident"] = np.eye(P, dtype=np.float32)
    a["causal"] = np.where(i[:, None] >= i[None, :], 0, NEG).astype(np.float32)
    a["tri"] = (i[:, None] <= i[None, :]).astype(np.float32)
    li = [0.8 - 0.6 * np.exp(-0.3 * l) for l in range(LAYERS)]
    a["lam_consts"] = np.tile(np.array([v for x in li for v in (x, 1.0 - x)], np.float32), (P, 1))
    a["sel4"] = np.array([[1, 0], [0, 1], [1, 0], [0, 1]], np.float32)
    return a


def kernel(**inputs):
    import concourse.bacc as bacc
    from concourse.bass_utils import run_bass_kernel_spmd

    arrays = {n: np.ascontiguousarray(v) for n, v in lay_out(inputs).items()}
    nc = bacc.Bacc("TRN2", target_bir_lowering=False, num_devices=1)
    io = {n: nc.dram_tensor("in_" + n, v.shape, mybir.dt.from_np(v.dtype), kind="ExternalInput").ap()
          for n, v in arrays.items()}
    io["y"] = nc.dram_tensor("out_y", (S, D), F32, kind="ExternalOutput").ap()
    program(nc, io)
    r = run_bass_kernel_spmd(nc, [{"in_" + n: v for n, v in arrays.items()}], core_ids=[0])
    return r.results[0]["out_y"].reshape(1, S, D)
```

```python
import numpy as np
import concourse.bass as bass
import concourse.mybir as mybir
from concourse.alu_op_type import AluOpType as ALU

F32, F32R, BF16 = mybir.dt.float32, mybir.dt.float32r, mybir.dt.bfloat16
ACT = mybir.ActivationFunctionType
AXX = mybir.AxisListType.X

P = 128
D = 1024
S = 256
NT = S // P
KD = D // P
HD = 64
LAYERS = 2
NEG = -1e30
FILL = -3e38
TOPK = 64
ALPHA = (2 * LAYERS) ** 0.25
EPS1 = 1e-5
EPS2 = 1e-6
WC = 512
KP = 2

SPLIT1 = [("diff_q", 512), ("diff_k", 512), ("diff_v", 512), ("dsa_q", 256), ("dsa_k", 64),
          ("dsa_v", 64), ("idx_q", 512), ("idx_k", 64), ("idx_w", 8), ("fox_q", 256),
          ("fox_k", 256), ("fox_v", 256), ("fox_f", 4), ("gate", 1024)]
CHUNKS1 = [[("idx_q", 0, 512)],
           [("idx_k", 0, 64), ("dsa_k", 0, 64), ("dsa_q", 0, 256), ("dsa_v", 0, 64),
            ("idx_w", 0, 8), ("fox_f", 0, 4)],
           [("diff_q", 0, 512)], [("diff_k", 0, 512)], [("diff_v", 0, 512)],
           [("fox_q", 0, 256), ("fox_k", 0, 256)],
           [("fox_v", 0, 256), ("gate", 768, 256)],
           [("gate", 0, 512)], [("gate", 512, 256)]]
IQ, DSA, DQ, DK, DV, FQK, FV, GA, GB = range(len(CHUNKS1))
WIDTH1 = [sum(n for _, _, n in c) for c in CHUNKS1]


def offsets(widths, rows):
    out = [0]
    for w in widths:
        out.append(out[-1] + rows * w)
    return out


OFF1 = offsets(WIDTH1, D)
OFFO = offsets([WC, WC], D)


RATES1 = [
    (2.94, 0.96, 1.88),
    (0.63, 0.46, 0.96),
    (0.75, 1.02, 1.8),
    (1.26, 0.29, 1.25)]
PHASE2 = 32
RATES2 = [[
    (2.06, 0.75, 0.38),
    (1.72, 0.38, 0.32),
    (3.12, 0.27, 0.56),
    (1.4, 0.38, 0.45),
    (1.0, 0.9, 0.54),
    (1.09, 1.5, 0.57),
    (1.41, 1.8, 0.33),
    (1.18, 1.8, 0.39),
    (7.44, 0.72, 0.76)], [
    (1.6, 0.41, 1.0),
    (2.6, 1.94, 0.5),
    (4.12, 0.35, 0.4),
    (2.88, 0.95, 0.28),
    (4.0, 1.36, 0.56),
    (2.4, 1.33, 0.48),
    (12.0, 1.59, 1.5)]]
BESIDE = [3.0, 0.25]
LAGS, LAGS2 = [0, 1, 3, 4], [0, 1, 2, 3]
SLACK = [4, 2, 3, 3, 4]


class Engine:

    def __init__(self, engine, sem):
        self.engine, self.sem, self.count, self.seen = engine, sem, 0, {}

    def after(self, *tokens):
        for token in tokens:
            if token is None:
                continue
            sem, value = token
            if self.seen.get(id(sem), 0) < value:
                self.engine.wait_ge(sem, value)
                self.seen[id(sem)] = value
        return self.engine

    def mark(self, instruction):
        self.count += 1
        instruction.then_inc(self.sem, 1)
        return (self.sem, self.count)

    def restart(self):
        self.count, self.seen = 0, {}


class Loads:

    def __init__(self, queue, sems):
        self.queue, self.sems, self.counts = queue, sems, [0] * len(sems)

    def start(self, k, out, in_, *tokens):
        self.queue.after(*tokens).dma_start(out, in_).then_inc(self.sems[k], 16)
        self.counts[k] += 16
        return (self.sems[k], self.counts[k])

    def restart(self):
        self.counts = [0] * len(self.sems)


class Ring:

    def __init__(self, buffers):
        self.buffers = buffers
        self.restart()

    def take(self):
        slot = self.unused.pop(0)
        return self.buffers[slot], self.tokens[slot], slot

    def free(self, slot, *tokens):
        self.tokens[slot] = tokens
        self.unused.append(slot)

    def restart(self):
        self.tokens, self.unused = [()] * len(self.buffers), list(range(len(self.buffers)))


def spread(ap, shape):
    return ap.unsqueeze(1).to_broadcast(shape)


def pipeline(items, stages, lags):
    for step in range(len(items) + lags[-1]):
        for stage, lag in reversed(list(zip(stages, lags))):
            if 0 <= step - lag < len(items):
                stage(items[step - lag])
                yield


class Core:

    SLOTS = 6

    def __init__(self, nc, ctx):
        self.nc, self.ctx = nc, ctx
        sem = lambda name: ctx.enter_context(nc.semaphore(name))
        self.pe = Engine(nc.tensor, sem("pe_done"))
        self.act = Engine(nc.scalar, sem("act_done"))
        self.dve = Engine(nc.vector, sem("dve_done"))
        self.pool = Engine(nc.gpsimd, sem("pool_done"))
        self.sp = Engine(nc.sync, sem("sp_unused"))
        self.weights = Loads(self.sp, [sem(f"weights_in{i}") for i in range(self.SLOTS)])
        self.small = Loads(self.sp, [sem(f"small_in{i}") for i in range(16)])
        self.bank = [ctx.enter_context(nc.psum_tensor(f"bank{i}", [P, 512], F32)) for i in range(8)]
        self.rings = []
        self.share_banks(4, 3)
        self.pieces, self.cut, self.done = [], [], []

    def share_banks(self, proj, aux):
        self.proj, self.aux = Ring(self.bank[0:proj]), Ring(self.bank[proj:proj + aux])
        self.sum_bank = Ring(self.bank[proj + aux:])
        self.rings[0:3] = [self.proj, self.aux, self.sum_bank]

    def sb(self, name, shape, dtype=F32, side="left"):
        return self.ctx.enter_context(self.nc.sbuf_tensor(name, shape, dtype, side=side))

    def ring(self, name, n, shape, dtype=F32):
        whole = self.sb(name, [shape[0], n] + shape[1:], dtype)
        ring = Ring([whole[:, i] for i in range(n)])
        self.rings.append(ring)
        return ring

    def piece_slots(self, name, raw, cut):
        self.RAW, self.CUT = raw, cut
        self.raw = self.sb("w_raw" + name, [P, raw, KP * WC])
        self.hi = self.sb("w_hi" + name, [P, cut, KP * WC], F32R)
        self.lo = self.sb("w_lo" + name, [P, cut, KP * WC], F32R)

    def stream(self, pieces):
        self.pieces += pieces

    def load_piece(self):
        n = len(self.loaded)
        dram, width = self.pieces[n]
        slot = n % self.RAW
        before = self.cut[n - self.RAW] if n >= self.RAW else ()
        self.loaded.append(self.weights.start(slot, self.raw[:, slot, 0:KP * width], dram, *before))

    def cut_piece(self):
        n = len(self.cut)
        _, width = self.pieces[n]
        raw = self.raw[:, n % self.RAW, 0:KP * width]
        hi = self.hi[:, n % self.CUT, 0:KP * width]
        lo = self.lo[:, n % self.CUT, 0:KP * width]
        free = self.done[n - self.CUT] if n >= self.CUT else None
        rounded = self.act.mark(self.act.after(self.loaded[n], free).activation(hi, raw, ACT.Copy))
        rest = self.dve.mark(self.dve.after(self.loaded[n], rounded).tensor_tensor(
            lo, raw, hi.bitcast(F32), ALU.subtract))
        self.cut.append((rounded, rest))

    def load_ahead(self):
        n = len(self.done)
        while len(self.loaded) < min(n + self.RAW, len(self.pieces)):
            if len(self.loaded) >= self.RAW and len(self.cut) <= len(self.loaded) - self.RAW:
                break
            self.load_piece()

    def prepare_pieces(self):
        self.load_ahead()
        n = len(self.done)
        while len(self.cut) < min(n + self.CUT, len(self.pieces)):
            self.cut_piece()
            if len(self.loaded) < len(self.pieces):
                self.load_piece()

    def next_piece(self):
        self.prepare_pieces()
        n = len(self.done)
        width = self.pieces[n][1]
        shape = lambda t: t[:, n % self.CUT, 0:KP * width].rearrange("p (k n) -> p k n", k=KP)
        return shape(self.hi), shape(self.lo), self.cut[n]

    def piece_used(self, token):
        self.done.append(token)

    def project(self, xs, n_k, tiles, width, evacuate, bias=None, width_of=None):
        (xh, xl, ready) = xs
        banks = []
        for t in tiles:
            ps, free, slot = self.proj.take()
            banks.append((ps, free, slot))
        pairs = n_k // KP
        for kp in range(pairs):
            hi, lo, cut = self.next_piece()
            for i, t in enumerate(tiles):
                ps, free, slot = banks[i]
                col = slice(t * P, (t + 1) * P)
                w = width_of(t) if width_of else width
                self.pe.after(*cut, *ready(t, kp), *(free if kp == 0 else ()))
                for kk in range(KP):
                    k = kp * KP + kk
                    first, last = kp == 0 and kk == 0, kp == pairs - 1 and kk == KP - 1
                    mm = self.nc.tensor.matmul
                    if first and bias is not None:
                        bias(ps[:, 0:w], w)
                        first = False
                    mm(ps[:, 0:w], xh[:, k, col], hi[:, kk, 0:w], start=first, stop=False)
                    mm(ps[:, 0:w], xh[:, k, col], lo[:, kk, 0:w], start=False, stop=False)
                    ins = mm(ps[:, 0:w], xl[:, k, col], hi[:, kk, 0:w], start=False, stop=last)
                token = self.pe.mark(ins)
                if kp == pairs - 1:
                    self.proj.free(slot, *evacuate(t, ps, token))
                if i == len(tiles) - 1:
                    self.piece_used(token)
                yield

    def project_t(self, xs, n_k, n_tok, evacuate):
        (xh, xl, ready) = xs
        banks = [self.proj.take() for _ in range(WC // P)]
        for kp in range(n_k // KP):
            hi, lo, cut = self.next_piece()
            for j, (ps, free, slot) in enumerate(banks):
                self.pe.after(*cut, *ready, *(free if kp == 0 else ()))
                for kk in range(KP):
                    k = kp * KP + kk
                    first, last = k == 0, k == n_k - 1
                    mm, cols, out = self.nc.tensor.matmul, slice(j * P, (j + 1) * P), ps[:, 0:n_tok]
                    mm(out, hi[:, kk, cols], xh[:, k, 0:n_tok], start=first, stop=False)
                    mm(out, lo[:, kk, cols], xh[:, k, 0:n_tok], start=False, stop=False)
                    ins = mm(out, hi[:, kk, cols], xl[:, k, 0:n_tok], start=False, stop=last)
                token = self.pe.mark(ins)
                if k == n_k - 1:
                    self.proj.free(slot, *evacuate(j, ps, token))
                if j == len(banks) - 1:
                    self.piece_used(token)
                yield

    def transpose(self, blocks, ready, width=P):
        ps, free, slot = self.aux.take()
        self.pe.after(*ready, *free)
        for i, block in enumerate(blocks):
            ins = self.nc.tensor.transpose(ps[0:width, i * P:(i + 1) * P], block, self.ident[:, :])
        return ps, self.pe.mark(ins), slot

    def transpose_cut(self, src, blocks, dst_hi, dst_lo, ready, free=()):
        tokens = []
        for b in range(blocks.start, blocks.stop, 4):
            n = min(4, blocks.stop - b)
            ps, token, slot = self.transpose([src[:, (b + i) * P:(b + i + 1) * P] for i in range(n)],
                                             ready)
            view = ps[:, 0:n * P].rearrange("p (k t) -> p k t", k=n)
            hi, lo = dst_hi[:, b:b + n, :], dst_lo[:, b:b + n, :]
            rounded = self.act.mark(self.act.after(token, *free).activation(hi, view, ACT.Copy))
            rest = self.dve.mark(self.dve.after(token, rounded).tensor_tensor(
                lo, view, hi.bitcast(F32), ALU.subtract))
            self.aux.free(slot, rest, rounded)
            tokens += [rounded, rest]
            yield
        self.last = tokens

    def fence(self):
        return [(e.sem, e.count) for e in (self.pe, self.act, self.dve, self.pool) if e.count]

    def restart(self):
        nc = self.nc
        nc.all_engine_barrier()
        for e in (self.pe, self.act, self.dve, self.pool, self.sp):
            nc.sync.sem_clear(e.sem)
        for s in self.weights.sems + self.small.sems:
            nc.sync.sem_clear(s)
        nc.all_engine_barrier()
        for x in [self.pe, self.act, self.dve, self.pool, self.sp, self.weights, self.small] + self.rings:
            x.restart()
        self.pieces, self.loaded, self.cut, self.done = [], [], [], []


def weave(main, sides, rates):
    sides = [[i, side, 0.0] for i, side in enumerate(sides)]

    def side_step(side):
        if next(side[1], "end") == "end":
            sides.remove(side)
            return False
        return True
    at = 0
    for n, step in enumerate(main):
        while step is not None and not step[0]():
            some = [side for side in sides if side[0] in step[1]]
            at += 1
            side_step(some[at % len(some)])
        for side in list(sides):
            side[2] += rates(n)[side[0]]
            while side[2] >= 1:
                side[2] -= 1
                if not side_step(side):
                    break
    while sides:
        at += 1
        side_step(sides[at % len(sides)])


def first_layer(core, layer, io, m):
    nc, pe, act, dve, pool, sp = core.nc, core.pe, core.act, core.dve, core.pool, core.sp
    small = core.small
    piece = lambda array, at, width: (array[layer, at:at + P * KP * width]
                                      .rearrange("(p n) -> p n", p=P), width)
    def stream(array, offs, c, width):
        core.stream([piece(io[array], offs[c] + kp * P * KP * width, width) for kp in range(KD // KP)])
    for c in (0, 1):
        stream("wm2", OFFM, c, WC)
    for c, width in enumerate(WIDTH1):
        stream("w1", OFF1, c, width)
    for c in (2, 3):
        stream("wm2", OFFM, c, WC)
    for c in range(2):
        stream("wo1", OFFO, c, WC)
    for c in (4, 5):
        stream("wm2", OFFM, c, WC)

    def modulation(chunks):
        def to_columns(c, row, end, rslot):
            ps, free, slot = core.aux.take()
            pe.after(end, *free)
            for j in range(4):
                ins = nc.tensor.matmul(ps[:, 2 * j:2 * j + 2], row[:, j * P:(j + 1) * P], m.sel4[:, :],
                                       start=True, stop=True)
            token = pe.mark(ins)
            m.mod_row.free(rslot, token)
            end = act.mark(act.after(token).activation(
                m.mod_cols[:, bass.ds(layer * MOD_COLS + 8 * c, 8)], ps[:, 0:8], ACT.Copy))
            core.aux.free(slot, end)
        last = None
        for c in chunks:
            ps, free, slot = core.proj.take()
            for kp in range(KD // KP):
                hi, lo, cut = core.next_piece()
                pe.after(*cut, *(free if kp == 0 else ()))
                for kk in range(KP):
                    k = kp * KP + kk
                    cols = m.c_cut[:, 4 * k:4 * k + P]
                    nc.tensor.matmul(ps[:, :], cols, hi[:, kk, :], start=k == 0, stop=False)
                    ins = nc.tensor.matmul(ps[:, :], cols, lo[:, kk, :], start=False, stop=k == KD - 1)
                token = pe.mark(ins)
                core.piece_used(token)
                if kp == 1 and last:
                    to_columns(*last)
                yield
            row, rfree, rslot = m.mod_row.take()
            end = act.mark(act.after(token, *rfree).activation(row, ps[0:4, :], ACT.Copy))
            core.proj.free(slot, end)
            last = (c, row, end, rslot)
            yield
        to_columns(*last)
        yield

    core.load_ahead()
    row = io["small1"][layer, :].partition_broadcast(P)
    params = small.start(0, m.par[:, :], row)
    bf, lams, gsub = m.par[:, 0:4], m.par[:, 4:260], m.par[:, 260:388]
    ln_g, ln_b = m.par[:, 388:388 + D], m.par[:, 388 + D:388 + 2 * D]

    x_ready = {}

    def transpose_x():
        for t in range(NT):
            cols = slice(t * P, (t + 1) * P)
            yield from core.transpose_cut(m.x[:, t, :], range(KD), m.xh[:, :, cols], m.xl[:, :, cols], ())
            x_ready[t] = core.last
    weave(modulation((0, 1)), [transpose_x()], lambda n: [1.0])
    xs = (m.xh, m.xl, lambda t, kp: x_ready[t])

    lp = lams.rearrange("p (a b d) -> p a b d", a=2, b=2)
    prod = dve.mark(dve.after(params).tensor_tensor(m.lprod[:, :, :], lp[:, :, 0, :], lp[:, :, 1, :], ALU.mult))
    dots = dve.mark(dve.after(prod).tensor_reduce(m.lam[:, 0:2], m.lprod[:, :, :], AXX, ALU.add))
    li = act.mark(act.after().activation(m.linit[:, 2:4], m.lconst[:, bass.ds(layer * 2, 2)], ACT.Copy))
    exps = act.mark(act.after(dots, li).activation(m.lam[:, 2:4], m.lam[:, 0:2], ACT.Exp))
    diff = dve.mark(dve.after(exps).tensor_tensor(m.lam[:, 4:5], m.lam[:, 2:3], m.lam[:, 3:4], ALU.subtract))
    lam = dve.mark(dve.after(diff).tensor_tensor(m.lam[:, 5:6], m.lam[:, 4:5], m.linit[:, 2:3], ALU.add))
    gsc = dve.mark(dve.after(li, params).tensor_scalar(m.gs[:, :], gsub, m.linit[:, 3:4], None, ALU.mult))

    got = {}

    def rope(ps, heads, t, out, token):
        v = ps[:, 0:heads * HD].rearrange("p (h d) -> p h d", d=HD)
        (tmp, free, slot) = m.rope.take()
        a = tmp[:, 0, 0:heads * HD].rearrange("p (h d) -> p h d", d=HD)
        b = tmp[:, 1, 0:heads * HD].rearrange("p (h d) -> p h d", d=HD)
        h = HD // 2
        one = dve.mark(dve.after(token, *free).tensor_tensor(
            a, v, spread(m.cos[:, t, :], [P, heads, HD]), ALU.mult))
        dve.mark(dve.after().tensor_tensor(
            b[:, :, 0:h], v[:, :, h:HD], spread(m.sin[:, t, 0:h], [P, heads, h]), ALU.mult))
        two = dve.mark(dve.after().tensor_tensor(
            b[:, :, h:HD], v[:, :, 0:h], spread(m.sin[:, t, h:HD], [P, heads, h]), ALU.mult))
        end = pool.mark(pool.after(two).tensor_tensor(out, a, b, ALU.add))
        m.rope.free(slot, end)
        return two, end

    def evacuate(chunk):
        def run(t, ps, token):
            if chunk in (IQ, DQ, DK):
                dst = {IQ: m.iq, DQ: m.dq, DK: m.dk}[chunk]
                read, end = rope(ps, 8, t, dst[:, t, :].rearrange("p (h d) -> p h d", d=HD), token)
                got[chunk, t] = [end]
                return [read]
            if chunk == DSA:
                read, end = rope(ps, 6, t, m.sx[:, t, :].rearrange("p (h d) -> p h d", d=HD), token)
                end2 = dve.mark(dve.after().tensor_copy(m.sv[:, t, :], ps[:, 384:460]))
                got[chunk, t] = [end, end2]
                return [end2]
            if chunk == FQK:
                v = ps[:, :].rearrange("p (h d) -> p h d", d=HD)
                end = act.mark(act.after(token).activation(m.fqk[:, t, :, 0:HD], v, ACT.Copy))
            elif chunk == FV:
                dve_end = dve.mark(dve.after(token).tensor_copy(m.fv[:, t, :], ps[:, 0:256]))
                end = act.mark(act.after(dve_end).activation(m.gate[:, t, 768:1024], ps[:, 256:512], ACT.Copy))
                got[chunk, t] = [dve_end, end]
                return [dve_end, end]
            elif chunk == DV:
                end = act.mark(act.after(token).activation(m.dv[:, t, :], ps[:, :], ACT.Copy))
            elif chunk == GA:
                end = act.mark(act.after(token).activation(m.gate[:, t, 0:512], ps[:, :], ACT.Copy))
            else:
                end = act.mark(act.after(token).activation(m.gate[:, t, 512:768], ps[:, 0:256], ACT.Copy))
            got[chunk, t] = [end]
            return [end]
        return run

    def need(*chunks):
        while not all((c, t) in got for c in chunks for t in range(NT)):
            yield

    def tokens(*chunks):
        return [x for c in chunks for t in range(NT) for x in got[c, t]]

    def head_transposes(src, heads, dst, rows, scale, ready, free=()):
        out = []
        for h in range(0, heads, 2):
            n = min(2, heads - h)
            ps, free_ps, slot = core.aux.take()
            pe.after(*ready, *free_ps)
            for i in range(n):
                for t in range(NT):
                    ins = nc.tensor.transpose(ps[0:rows, (i * NT + t) * P:(i * NT + t + 1) * P],
                                              src(h + i, t), m.ident[:, :])
            token = pe.mark(ins)
            view = ps[0:rows, 0:n * S].rearrange("p (h t) -> p h t", h=n)
            if (h // 2) % 2 == 0:
                end = act.mark(act.after(token, *free).activation(dst[0:rows, h:h + n, :], view, ACT.Copy, scale=scale))
            else:
                end = dve.mark(dve.after(token, *free).tensor_scalar(dst[0:rows, h:h + n, :], view, scale, None, ALU.mult))
            core.aux.free(slot, end)
            out.append(end)
            yield
        core.last = out

    mixed = {}

    def sparse_index():
        yield from need(IQ, DSA)
        for _ in range(SLACK[3]):
            yield
        ready = tokens(IQ, DSA)
        yield from head_transposes(lambda h, t: m.iq[:, t, h * HD:(h + 1) * HD], 8, m.qa, HD, 1.0, ready)
        q_t = core.last
        yield from head_transposes(lambda h, t: m.sx[:, t, h * HD:(h + 1) * HD], 2, m.sk_t, HD, 1.0, ready)
        k_t = core.last
        yield from head_transposes(lambda h, t: m.sx[:, t, (2 + h) * HD:(3 + h) * HD], 4, m.sq_t, HD, HD ** -0.5, ready)
        got["dsa_t"] = k_t + core.last
        w_end = dve.mark(dve.after(*ready).tensor_scalar(m.iw[:, :, :], m.sv[:, :, 64:72], (8 * HD) ** -0.5, None, ALU.mult))
        for qt in range(NT):
            keys = (qt + 1) * P
            acc = None
            items = list(range(0, 8, 2))
            state = {}

            def scores(h):
                ps, free, slot = core.aux.take()
                pe.after(*q_t, *k_t, *free)
                for i in range(2):
                    ins = nc.tensor.matmul(ps[:, i * keys:(i + 1) * keys], m.qa[0:HD, h + i, qt * P:(qt + 1) * P],
                                           m.sk_t[0:HD, 0, 0:keys], start=True, stop=True)
                state[h] = (ps, slot, pe.mark(ins))

            def weigh(h):
                ps, slot, token = state[h]
                r, free, rslot = m.relu.take()
                end = act.mark(act.after(token, *free).activation(r[:, 0:2 * keys], ps[:, 0:2 * keys], ACT.Relu))
                core.aux.free(slot, end)
                for i in range(2):
                    w = m.iw[:, qt, h + i:h + i + 1]
                    part = r[:, i * keys:(i + 1) * keys]
                    if h + i == 0:
                        state["acc"] = dve.mark(dve.after(end, w_end, *state.get("acc_free", ())).tensor_scalar(
                            m.score[:, qt, 0:keys], part, w, None, ALU.mult))
                    else:
                        state["acc"] = dve.mark(dve.after(end, state["acc"]).scalar_tensor_tensor(
                            m.score[:, qt, 0:keys], part, w, m.score[:, qt, 0:keys], ALU.mult, ALU.add))
                m.relu.free(rslot, state["acc"])
            yield from pipeline(items, [scores, weigh], [0, 1])
            diag = m.score[:, qt, qt * P:keys]
            last = dve.mark(dve.after(state["acc"]).tensor_tensor(diag, diag, m.mask[:, :], ALU.add))
            for _ in range(TOPK // 8):
                top = dve.mark(dve.after(last).max(m.top8[:, :], m.score[:, qt, 0:keys]))
                last = dve.mark(dve.after(top).match_replace(m.score[:, qt, 0:keys], m.top8[:, :], m.score[:, qt, 0:keys], FILL))
                yield
            got["sel", qt] = dve.mark(dve.after(last).tensor_scalar(
                m.sel[:, qt, 0:keys], m.score[:, qt, 0:keys], 0.5 * FILL, NEG, ALU.is_gt, ALU.mult))

    def attend(name, heads, q_of, k_of, rows, v_of, v_width, out, bias_sel, ready, buf):
        for qt in range(NT):
            keys = (qt + 1) * P
            nb = qt + 1
            diff_kind = name == "diff"
            n_out = 1 if diff_kind else 2
            osum, ofree, oslot = core.sum_bank.take()
            stat, sfree, sslot = buf.stat.take()
            n_maps = 2 * heads
            top_of, sum_of, inv_of, sub_of = (stat[:, i * n_maps:(i + 1) * n_maps] for i in range(4))
            st = {}

            def scores(j):
                ps, free, slot = core.aux.take()
                pe.after(*ready, *free)
                for i in range(2):
                    part = ps[:, i * keys:(i + 1) * keys]
                    nc.tensor.matmul(part, q_of(2 * j + i)[0:rows, qt * P:(qt + 1) * P],
                                     k_of(2 * j + i)[0:rows, 0:keys], start=True, stop=False)
                    if bias_sel:
                        nc.tensor.matmul(part, m.identb[:, :], m.sel[:, qt, 0:keys], start=False, stop=False)
                    ins = nc.tensor.matmul(part[:, qt * P:keys], m.identb[:, :], m.maskb[:, :], start=False, stop=True)
                st[j] = [ps, slot, pe.mark(ins)]

            def soft(j):
                ps, slot, token = st[j]
                view = ps[:, 0:2 * keys].rearrange("p (a b) -> p a b", a=2)
                top = dve.mark(dve.after(token, *sfree).tensor_reduce(
                    top_of[:, 2 * j:2 * j + 2], view, AXX, ALU.max, negate=True))
                pm, free, pslot = buf.prob.take()
                act.after(top, *free)
                for i in range(2):
                    n = 2 * j + i
                    end = act.mark(nc.scalar.activation(pm[:, i, 0:keys], ps[:, i * keys:(i + 1) * keys], ACT.Exp,
                                                        bias=top_of[:, n:n + 1], accum_out=sum_of[:, n:n + 1]))
                core.aux.free(slot, end)
                inv = dve.mark(dve.after(end).reciprocal(inv_of[:, 2 * j:2 * j + 2], sum_of[:, 2 * j:2 * j + 2]))
                if diff_kind:
                    lam_l1 = dve.mark(dve.after(inv).tensor_scalar(
                        sub_of[:, 2 * j:2 * j + 1], inv_of[:, 2 * j + 1:2 * j + 2], m.lam[:, 5:6], None, ALU.mult))
                    second = dve.mark(dve.after(lam_l1).tensor_scalar(
                        pm[:, 1, 0:keys], pm[:, 1, 0:keys], sub_of[:, 2 * j:2 * j + 1], None, ALU.mult))
                    end = dve.mark(dve.after(second).scalar_tensor_tensor(
                        pm[:, 0, 0:keys], pm[:, 0, 0:keys], inv_of[:, 2 * j:2 * j + 1], pm[:, 1, 0:keys],
                        ALU.mult, ALU.subtract))
                st[j] = [pm, pslot, end]
                st["inv"] = inv

            def flip(j):
                pm, pslot, end = st[j]
                ps, free, slot = core.aux.take()
                pe.after(end, *free)
                for i in range(n_out):
                    for b in range(nb):
                        ins = nc.tensor.transpose(ps[:, (i * nb + b) * P:(i * nb + b + 1) * P],
                                                  pm[:, i, b * P:(b + 1) * P], m.ident[:, :])
                token = pe.mark(ins)
                buf.prob.free(pslot, token)
                pt, pfree, ptslot = buf.prob_t.take()
                n = n_out * nb * P
                if j % 2 == 0:
                    end = act.mark(act.after(token, *pfree).activation(pt[:, 0:n], ps[:, 0:n], ACT.Copy))
                else:
                    end = dve.mark(dve.after(token, *pfree).tensor_copy(pt[:, 0:n], ps[:, 0:n]))
                core.aux.free(slot, end)
                st[j] = [pt, ptslot, end]

            def values(j):
                pt, ptslot, end = st[j]
                pe.after(end, *(ofree if j == 0 else ()))
                for i in range(n_out):
                    h = n_out * j + i
                    for b in range(nb):
                        ins = nc.tensor.matmul(osum[:, h * v_width:(h + 1) * v_width],
                                               pt[:, (i * nb + b) * P:(i * nb + b + 1) * P], v_of(h, b),
                                               start=b == 0, stop=b == nb - 1)
                st["sum"] = pe.mark(ins)
                buf.prob_t.free(ptslot, st["sum"])
            yield from pipeline(list(range(heads)), [scores, soft, flip, values], LAGS)
            n_cols = heads * n_out * v_width
            if diff_kind:
                end = act.mark(act.after(st["sum"]).activation(out[:, qt, :], osum[:, 0:n_cols], ACT.Copy))
            else:
                end = dve.mark(dve.after(st["sum"], st["inv"]).tensor_tensor(
                    out[:, qt, :].rearrange("p (h d) -> p h d", d=v_width),
                    osum[:, 0:n_cols].rearrange("p (h d) -> p h d", d=v_width),
                    inv_of.unsqueeze(2).to_broadcast([P, n_maps, v_width]), ALU.mult))
            buf.stat.free(sslot, end)
            core.sum_bank.free(oslot, end)
            mixed[name, qt] = [end]
            yield

    def sub_norm(qt):
        a = m.mix[:, qt, 0:512]
        sq, free, slot = m.relu.take()
        s1 = pool.mark(pool.after(*mixed["diff", qt], *free).tensor_tensor(sq[:, 0:512], a, a, ALU.mult))
        s2 = dve.mark(dve.after(s1).tensor_reduce(m.ms[:, qt, :], sq[:, 0:512].rearrange("p (h d) -> p h d", h=4), AXX, ALU.add))
        m.relu.free(slot, s2)
        s3 = dve.mark(dve.after(s2).tensor_scalar(m.ms[:, qt, :], m.ms[:, qt, :], 1.0 / P, EPS1, ALU.mult, ALU.add))
        s4 = pool.mark(pool.after(s3).tensor_tensor(m.ms2[:, qt, :], m.ms[:, qt, :], m.half[:, 0:4], ALU.pow))
        av = a.rearrange("p (h d) -> p h d", h=4)
        gated = pool.mark(pool.after(gsc).tensor_tensor(av, av, spread(m.gs[:, :], [P, 4, P]), ALU.mult))
        for h in range(4):
            end = dve.mark(dve.after(s4, gated).tensor_scalar(av[:, h, :], av[:, h, :], m.ms2[:, qt, h:h + 1], None, ALU.mult))
        mixed["norm", qt] = [end]

    def side_sparse():
        yield from sparse_index()
        yield from attend("dsa", 2, lambda h: m.sq_t[:, h, :], lambda h: m.sk_t[:, 1, :], HD,
                          lambda h, b: m.sv[:, b, 0:64], HD, m.mix[:, :, 512:768], True,
                          got["dsa_t"] + [got["sel", 0], got["sel", 1]] + tokens(DSA), m.buf_a)

    def side_diff():
        yield from need(DQ, DK)
        yield from head_transposes(lambda h, t: m.dq[:, t, h * HD:(h + 1) * HD], 8, m.qb, HD, HD ** -0.5, tokens(DQ))
        q_t = core.last
        yield from head_transposes(lambda h, t: m.dk[:, t, h * HD:(h + 1) * HD], 8, m.kb, HD, 1.0, tokens(DK))
        q_t = q_t + core.last
        yield from need(DV)
        yield from attend("diff", 4, lambda h: m.qb[:, h, :], lambda h: m.kb[:, h, :], HD,
                          lambda h, b: m.dv[:, b, h * P:(h + 1) * P], P, m.mix[:, :, 0:512], False,
                          q_t + [lam] + tokens(DV), m.buf_b)
        got["diff"] = []
        for qt in range(NT):
            sub_norm(qt)
            yield

    def side_fox():
        yield from need(DSA)
        z = dve.mark(dve.after(*tokens(DSA), params).tensor_tensor(
            m.fz[:, :, :], m.sv[:, :, 72:76], spread(bf, [P, NT, 4]), ALU.add))
        az = dve.mark(dve.after(z).scalar_tensor_tensor(m.fa[:, :, :], m.fz[:, :, :], -1.0, m.fz[:, :, :], ALU.mult, ALU.max))
        ez = act.mark(act.after(az).activation(m.fe[:, :, :], m.fa[:, :, :], ACT.Exp, scale=-1.0))
        lz = act.mark(act.after(ez).activation(m.fl[:, :, :], m.fe[:, :, :], ACT.Ln, bias=1.0))
        for _ in range(SLACK[4]):
            yield
        lf = dve.mark(dve.after(lz).scalar_tensor_tensor(m.lf[:, :, :], m.fz[:, :, :], 0.0, m.fl[:, :, :], ALU.min, ALU.subtract))
        ps, free, slot = core.aux.take()
        pe.after(lf, *free)
        nc.tensor.matmul(ps[:, 0:4], m.tri[:, :], m.lf[:, 0, :], start=True, stop=True)
        nc.tensor.matmul(ps[:, 4:8], m.ones[:, :], m.lf[:, 0, :], start=True, stop=False)
        cs = pe.mark(nc.tensor.matmul(ps[:, 4:8], m.tri[:, :], m.lf[:, 1, :], start=False, stop=True))
        cum = dve.mark(dve.after(cs).tensor_copy(m.fcum[:, :, :], ps[:, 0:8].rearrange("p (t h) -> p t h", t=NT)))
        core.aux.free(slot, cum)
        yield from need(FQK)
        c1 = dve.mark(dve.after(cum).tensor_scalar(m.fqk[:, :, 0:4, 64], m.fcum[:, :, :], HD ** 0.5, None, ALU.mult))
        c2 = dve.mark(dve.after(cum).tensor_scalar(m.fqk[:, :, 4:8, 65], m.fcum[:, :, :], -HD ** 0.5, None, ALU.mult))
        c3 = dve.mark(dve.after().memset(m.fqk[:, :, 0:4, 65], 1.0))
        c4 = dve.mark(dve.after().memset(m.fqk[:, :, 4:8, 64], 1.0))
        ready = tokens(FQK) + [c1, c2, c3, c4]
        yield
        yield from head_transposes(lambda h, t: m.fqk[:, t, h, :], 4, m.qf, 66, HD ** -0.5, ready)
        f_t = core.last
        yield from head_transposes(lambda h, t: m.fqk[:, t, 4 + h, :], 4, m.kf, 66, 1.0, ready)
        f_t = f_t + core.last
        yield from need(FV)
        while "diff" not in got:
            yield
        yield from attend("fox", 2, lambda h: m.qf[:, h, :], lambda h: m.kf[:, h, :], 66,
                          lambda h, b: m.fv[:, b, h * HD:(h + 1) * HD], HD, m.mix[:, :, 768:1024], False,
                          f_t + tokens(FV), m.buf_b)

    def gated(part, cols):
        proj_done = core.piece_of_x
        ends = []
        for t in range(NT):
            e = act.mark(act.after(*tokens(*part[1])).activation(m.gate[:, t, cols], m.gate[:, t, cols], ACT.Silu))
            ends.append(dve.mark(dve.after(e, *mixed[part[0], t]).tensor_tensor(
                m.mix[:, t, cols], m.mix[:, t, cols], m.gate[:, t, cols], ALU.mult)))
            yield
        for t in range(NT):
            rows = slice(t * P, (t + 1) * P)
            yield from core.transpose_cut(m.mix[:, t, :], range(cols.start // P, cols.stop // P),
                                          m.xh[:, :, rows], m.xl[:, :, rows], (ends[t],), (proj_done,))
            for k in range(cols.start // P, cols.stop // P):
                ready[t, k // KP] = core.last

    ready, sums = {}, {}

    def add_residual(c):
        def run(t, ps, token):
            part = m.x[:, t, c * WC:(c + 1) * WC]
            end = dve.mark(dve.after(token).scalar_tensor_tensor(part, part, ALPHA, ps[:, :], ALU.mult, ALU.add))
            st = dve.mark(dve.after(end).bn_stats(m.bn[:, t, c * 6:(c + 1) * 6], part))
            sums[t] = (end, st)
            return [end]
        return run

    def main():
        for c, width in enumerate(WIDTH1):
            yield from core.project(xs, KD, range(NT), width, evacuate(c))
        core.piece_of_x = core.done[-1]
        fill = modulation((2, 3))
        done = lambda name: all((name, t) in mixed for t in range(NT))
        def beside(steps):
            for step in steps:
                yield
                next(fill, None)
        for name, part, cols in (("norm", (GA,), slice(0, 512)), ("dsa", (GB,), slice(512, 768))):
            while not done(name):
                yield
                next(fill, None)
            yield from beside(gated((name, part), cols))
        yield from fill
        w_out = core.project((m.xh, m.xl, lambda t, kp: ready[t, kp]), KD, range(NT), WC, add_residual(0))
        for _ in range((KD // KP - 1) * NT):
            next(w_out)
            yield
        yield lambda: done("fox"), (0, 1, 2)
        yield from gated(("fox", (FV,)), slice(768, D))
        yield from w_out
        yield from core.project((m.xh, m.xl, lambda t, kp: ready[t, kp]), KD, range(NT), WC, add_residual(1))

    weave(main(), [side_sparse(), side_diff(), side_fox()], lambda n: RATES1[min(n // 24, len(RATES1) - 1)])

    def normalise():
        for t in range(NT):
            ag = dve.mark(dve.after(*sums[t]).bn_aggr(m.mv[:, t, :], m.bn[:, t, :]))
            ve = dve.mark(dve.after(ag).tensor_scalar(m.mv[:, t, 1:2], m.mv[:, t, 1:2], EPS1, None, ALU.add))
            rs = pool.mark(pool.after(ve).tensor_tensor(m.rstd[:, t, :], m.mv[:, t, 1:2], m.half[:, 0:1], ALU.pow))
            yield
            xn = dve.mark(dve.after(rs).tensor_scalar(m.x[:, t, :], m.x[:, t, :], m.mv[:, t, 0:1], m.rstd[:, t, :],
                                                      ALU.subtract, ALU.mult))
            for e, s in ((dve, slice(0, 512)), (pool, slice(512, D))):
                g = e.mark(e.after(xn).tensor_tensor(m.x[:, t, s], m.x[:, t, s], ln_g[:, s], ALU.mult))
                e.mark(e.after(g).tensor_tensor(m.x[:, t, s], m.x[:, t, s], ln_b[:, s], ALU.add))
            yield
    weave(modulation((4, 5)), [normalise()], lambda n: [1.0])


MOD_COLS = 2 * 3 * KD


class Mem:
    pass


def first_block(core, io, shared):
    from contextlib import ExitStack
    nc = core.nc
    with ExitStack() as ctx:
        core.ctx, outer = ctx, core.ctx
        rings = list(core.rings)
        m = Mem()
        m.ident, m.ones, m.half, m.x = shared.ident, shared.ones, shared.half, shared.x
        m.mod_cols = shared.mod_cols
        core.piece_slots("1", 6, 4)
        core.share_banks(3, 3)
        m.xh, m.xl = core.sb("x_hi1", [P, KD, S], F32R), core.sb("x_lo1", [P, KD, S], F32R)
        m.par = core.sb("par1", [P, 388 + 2 * D])
        m.lprod, m.lam = core.sb("lam_prod", [P, 2, HD]), core.sb("lam", [P, 6])
        m.linit, m.gs = core.sb("lam_init", [P, 4]), core.sb("g_sub_scaled", [P, P])
        m.lconst = core.sb("lam_consts", [P, 2 * LAYERS])
        m.cos, m.sin = core.sb("cos1", [P, NT, HD]), core.sb("sin1", [P, NT, HD])
        m.mask, m.maskb = core.sb("causal_bias", [P, P]), core.sb("causal_bias_bf", [P, P], BF16)
        m.identb = core.sb("ident_bf", [P, P], BF16)
        m.tri = core.sb("tri", [P, P])
        m.rope = core.ring("rope_tmp", 1, [P, 2, 512])
        m.iq, m.sx, m.sv = core.sb("idx_q", [P, NT, 512]), core.sb("dsa_roped", [P, NT, 384]), core.sb("dsa_v_w_f", [P, NT, 76])
        m.dq, m.dk, m.dv = (core.sb(n, [P, NT, 512]) for n in ("diff_q", "diff_k", "diff_v"))
        m.fqk, m.fv = core.sb("fox_qk", [P, NT, 8, 66]), core.sb("fox_v", [P, NT, 256])
        m.gate, m.mix = core.sb("gate1", [P, NT, D]), core.sb("mix1", [P, NT, D])
        m.qa = core.sb("idx_q_t", [HD, 8, S])
        m.qf, m.kf = core.sb("fox_q_t", [66, 4, S]), core.sb("fox_k_t", [66, 4, S])
        m.qb, m.kb = core.sb("q_t_b", [HD, 8, S]), core.sb("k_t_b", [HD, 8, S])
        m.sk_t, m.sq_t = core.sb("dsa_k_t", [HD, 2, S]), core.sb("dsa_q_t", [HD, 4, S])
        m.iw, m.relu = core.sb("idx_w", [P, NT, 8]), core.ring("relu", 2, [P, 512])
        m.score, m.top8 = core.sb("idx_score", [P, NT, S]), core.sb("top8", [P, 8])
        m.sel = core.sb("sel_bias", [P, NT, S], BF16)
        m.buf_a, m.buf_b = Mem(), Mem()
        m.buf_a.stat, m.buf_a.prob, m.buf_a.prob_t = core.ring("stat_a", 2, [P, 32]), core.ring("prob_a", 2, [P, 2, S]), core.ring("prob_t_a", 2, [P, 512])
        m.buf_b.stat, m.buf_b.prob, m.buf_b.prob_t = core.ring("stat_b", 2, [P, 32]), core.ring("prob_b", 3, [P, 2, S]), core.ring("prob_t_b", 2, [P, 512])
        m.mod_row, m.sel4 = core.ring("mod_row", 1, [4, WC]), core.sb("sel4", [4, 2])
        m.c_cut = core.sb("mod_c_cut", [P, 4 * KD + P], F32R)
        m.c_vec = core.sb("mod_c", [P, KD, 2])
        m.ms, m.ms2 = core.sb("ms", [P, NT, 4]), core.sb("ms_inv", [P, NT, 4])
        m.fz, m.fa, m.fe, m.fl, m.lf, m.fcum = (core.sb(n, [P, NT, 4]) for n in ("fox_z", "fox_abs", "fox_exp", "fox_ln", "fox_logf", "fox_cumsum"))
        m.bn, m.mv, m.rstd = core.sb("bn1", [P, NT, 12]), core.sb("mean_var1", [P, NT, 2]), core.sb("rstd1", [P, NT, 1])
        got = core.small.start(1, m.cos[:, :, :], io["cos1"])
        core.small.start(1, m.sin[:, :, :], io["sin1"])
        core.small.start(1, m.mask[:, :], io["causal"])
        core.small.start(1, m.tri[:, :], io["tri"])
        got = core.small.start(1, m.lconst[:, :], io["lam_consts"])
        core.small.start(1, m.sel4[:, :], io["sel4"])
        got = core.small.start(1, m.c_vec[:, :, :], io["c2"])
        core.dve.mark(core.dve.after(got).tensor_copy(m.maskb[:, :], m.mask[:, :]))
        dve, act = core.dve, core.act
        zero = dve.mark(dve.after().memset(m.iq[:, 0, 0:4 * KD + P], 0.0))
        z = dve.mark(dve.after(zero).tensor_copy(m.c_cut[:, :], m.iq[:, 0, 0:4 * KD + P]))
        sc = act.mark(act.after(got).activation(m.c_vec[:, :, :], m.c_vec[:, :, :], ACT.Silu))
        cut = m.c_cut[:, 0:4 * KD].rearrange("p (k a) -> p k a", a=4)
        ch = dve.mark(dve.after(sc, z).tensor_copy(cut[:, :, 0:2], m.c_vec[:, :, :]))
        dve.mark(dve.after(ch).tensor_tensor(cut[:, :, 2:4], m.c_vec[:, :, :], cut[:, :, 0:2].bitcast(F32), ALU.subtract))
        core.dve.mark(core.dve.after().tensor_copy(m.identb[:, :], m.ident[:, :]))
        core.restart()
        with nc.Fori(0, LAYERS) as layer:
            first_layer(core, layer, io, m)
            core.restart()
        core.ctx, core.rings = outer, rings


CONV, QK2, V2, RANK, HEADS2 = 512, 256, 512, 16, 4
SPLIT2 = [("val", CONV), ("glu", CONV), ("cgate", CONV), ("gla_q", QK2), ("gla_k", QK2),
          ("gla_v", V2), ("gla_g", V2), ("low_f", RANK), ("low_b", RANK), ("att_q", 512),
          ("att_k", P), ("att_v", P), ("att_g", 512), ("merge0", D), ("merge1", D), ("merge2", D)]
PAIRED = [4 * (i % 2) + i // 2 for i in range(8)]
CHUNKS2 = [[("val", 0, 512)], [("glu", 0, 512)], [("cgate", 0, 512)],
           [("gla_k", 0, 256), ("att_k", 0, 128), ("att_v", 0, 128)],
           [("gla_v", 0, 512)],
           [("low_f", 0, 16), ("low_b", 0, 16), ("gla_q", 0, 256)],
           [("att_q", h * HD, HD) for h in PAIRED],
           [("merge0", 0, 512)], [("merge0", 512, 512)],
           [("gla_g", 0, 512)],
           [("merge1", 0, 512)], [("merge1", 512, 512)],
           [("att_g", h * HD, HD) for h in PAIRED],
           [("merge2", 0, 512)], [("merge2", 512, 512)]]
VAL, GLU, CGATE, KKV, GV, LRQ, AQ, M0A, M0B, GG, M1A, M1B, AG, M2A, M2B = range(len(CHUNKS2))
WIDTH2 = [sum(n for _, _, n in c) for c in CHUNKS2]
OFF2 = offsets(WIDTH2, D)
N_BIAS = len(CHUNKS2) - 3
OFFM = offsets([WC] * 6, D)
OFFY = offsets([WC] * 2, CONV)
TAPS, PAD = 31, 15
GC = 64
AH, AKV = 8, 2
X_TILES, C_TILES = (0, 1), (2, 3)
PAR_COLS = KD + 12 + 4 * TAPS + 4 + 4 + 4 + 3 * KD


FIRST_CHUNKS = [(KKV, VAL, GLU), (VAL, GLU, KKV)]


def stream_second(core, layer, io):
    def pieces(array, offs, c, width, n_k):
        at0 = offs[c]
        return [(array[layer, at0 + kp * P * KP * width:at0 + (kp + 1) * P * KP * width]
                 .rearrange("(p n) -> p n", p=P), width) for kp in range(n_k // KP)]
    order = [("in", c) for c in FIRST_CHUNKS[layer] + (LRQ, GV, CGATE, M0A, AQ)]
    order += [("conv", 0), ("in", M0B), ("conv", 1), ("in", GG)]
    order += [("in", M1A), ("gla", 0), ("in", M1B), ("gla", 1), ("in", AG)]
    order += [("in", M2A), ("att", 0), ("in", M2B), ("att", 1)]
    order += [("out", 0), ("out", 1)] * (2 if layer < LAYERS - 1 else 1)
    for kind, c in order:
        if kind == "in":
            core.stream(pieces(io["w2"], OFF2, c, WIDTH2[c], KD))
        elif kind == "out":
            core.stream(pieces(io["wo2"], OFFO, c, WC, KD))
        else:
            core.stream(pieces(io["wy_" + kind], OFFY, c, WC, CONV // P))


def modulated_input(core, m, layer, tiles, hx):
    from contextlib import ExitStack
    nc, act, dve, pool = core.nc, core.act, core.dve, core.pool
    shift, scale = m.mod[:, layer, 0], m.scale[:, layer]
    source = lambda t: m.x[:, t, :] if t in X_TILES else m.acc[:, t, :]
    name = f"{layer}{tiles[0]}"
    with ExitStack() as scope:
        outer, rings = core.ctx, list(core.rings)
        core.ctx = scope
        xn = core.ring("x_normed" + name, 2, [P, D])
        mod = core.ring("x_mod" + name, 4, [P, 4, P])
        ss = core.sb("sum_sq" + name, [P, 8])
        core.ctx, core.rings = outer, rings
        for e in (act, dve, pool):
            e.after(*m.scope_free)
        st, rinv, squared = {}, {}, {}

        def deviation(t):
            junk = m.sigma[:, 2 * (t % 2):2 * (t % 2) + 2, :].rearrange("p a b -> p (a b)")
            squared[t] = act.mark(act.after(
                m.ctx_in if t in C_TILES else None, *core.x_ready.get(t, ()), squared.get(t - 2), *core.sigma_read).activation(
                    junk, source(t), ACT.Square, accum_out=ss[:, t:t + 1]))
            mean = dve.mark(dve.after(squared[t]).tensor_scalar(
                ss[:, 4 + t:5 + t], ss[:, t:t + 1], 1.0 / D, EPS2, ALU.mult, ALU.add))
            rinv[t] = pool.mark(pool.after(mean).tensor_tensor(
                ss[:, t:t + 1], ss[:, 4 + t:5 + t], m.half[:, 0:1], ALU.pow))

        def measured(tb):
            if tb[0] not in tiles[:2] and tb[1] == 0:
                deviation(tb[0])

        def normed(tb):
            t, b = tb
            if layer == 0 and tb == (tiles[-1], 0):
                core.prepare_pieces()
            if b == 0 and t not in st:
                buf, free, slot = xn.take()
                st[t] = (buf, slot, dve.mark(dve.after(rinv[t], *free).tensor_scalar(
                    buf, source(t), ss[:, t:t + 1], None, ALU.mult)))

        def flip(tb):
            t, b = tb
            buf, slot, norm = st[t]
            st[tb] = core.transpose([buf[:, (b + i) * P:(b + i + 1) * P] for i in range(4)], [norm])
            if b > 0:
                xn.free(slot, st[tb][1])

        def wide(v, tb):
            return v[:, tb[1]:tb[1] + 4, tb[0] // 2:tb[0] // 2 + 1].to_broadcast([P, 4, P])

        def scale_shift(tb):
            t, b = tb
            ps, token, pslot = st[tb]
            tmp, free, slot = mod.take()
            s = t // 2
            if b == 0:
                act.after(token, m.scale_ready, *free)
                for i in range(4):
                    a = act.mark(nc.scalar.activation(tmp[:, i, :], ps[:, i * P:(i + 1) * P], ACT.Identity,
                                                      scale=scale[:, b + i, s:s + 1], bias=shift[:, b + i, s:s + 1]))
            else:
                a = dve.mark(dve.after(token, m.scale_ready, *free).tensor_tensor(
                    tmp, ps[:, :].rearrange("p (k t) -> p k t", k=4), wide(scale, tb), ALU.mult))
            core.aux.free(pslot, a)
            st[tb] = (tmp, slot, a)

        def add_shift(tb):
            tmp, slot, a = st[tb]
            if tb[1]:
                a = pool.mark(pool.after(a).tensor_tensor(tmp, tmp, wide(shift, tb), ALU.add))
            st[tb] = (tmp, slot, a)

        def cut_hi(tb):
            t, b = tb
            tmp, slot, a = st[tb]
            h = act.mark(act.after(a).activation(m.xh[:, b:b + 4, t * P:(t + 1) * P], tmp, ACT.Copy))
            st[tb] = (tmp, slot, h)

        def cut_lo(tb):
            t, b = tb
            tmp, slot, h = st[tb]
            hi, lo = m.xh[:, b:b + 4, t * P:(t + 1) * P], m.xl[:, b:b + 4, t * P:(t + 1) * P]
            l = dve.mark(dve.after(h).tensor_tensor(lo, tmp, hi.bitcast(F32), ALU.subtract))
            mod.free(slot, l)
            st[tb] = [h, l]
            if b > 0:
                hx[t] = st[t, 0] + st[tb]

        for t in tiles[:2]:
            deviation(t)
            normed((t, 0))
        if layer == 0:
            m.set_up_first()
        yield from pipeline([(t, b) for t in tiles for b in (0, 4)],
                            [measured, normed, flip, scale_shift, add_shift, cut_hi, cut_lo], [0, 2, 3, 4, 5, 6, 7])
        if layer == 0:
            m.set_up_rest()


def second_layer(core, layer, io, m):
    from contextlib import ExitStack
    nc, pe, act, dve, pool, sp, small = core.nc, core.pe, core.act, core.dve, core.pool, core.sp, core.small
    full = layer < LAYERS - 1
    tiles = X_TILES + C_TILES if full else X_TILES
    every = X_TILES + C_TILES
    n_tok = len(tiles) * P
    streams = [0, 1] if full else [0]

    par, rows = m.par[:, layer, :], m.rows[:, layer, :]
    b_conv = par[:, KD:KD + 12]
    taps = par[:, KD + 12:KD + 12 + 4 * TAPS].rearrange("p (c k) -> p c k", k=TAPS)
    o = KD + 12 + 4 * TAPS
    dw_b, cln_g, cln_b = (par[:, o + 4 * i:o + 4 * i + 4] for i in range(3))
    gla_g, qn_g, kn_g = rows[:, 0:P], rows[:, P:P + HD], rows[:, P + HD:P + 2 * HD]
    shift, scale, gate = m.mod[:, layer, 0], m.scale[:, layer], m.mod[:, layer, 2]

    hx = {}
    if layer == 0:
        for _ in modulated_input(core, m, layer, every, hx):
            pass
    else:
        weave(m.context_end, [modulated_input(core, m, layer, X_TILES, hx)], lambda n: [BESIDE[0]])
    xs = (m.xh, m.xl, lambda t, kp: hx[t])
    got = {}
    pre_fence = core.fence()
    for e in (pe, act, dve, pool):
        e.after(*m.set_up[layer], m.consts_in)

    def bias_of(c):
        def add(out, w):
            nc.tensor.matmul(out, m.sel[:, c - 3, :], m.bias[0:96, layer, 0:w], start=True, stop=False)
        return add

    def need(*keys):
        while not all(k in got for k in keys):
            yield

    def toks(*keys):
        return [x for k in keys for x in got[k]]

    def ev_val(j, ps, token):
        e = act.mark(act.after(token, *pre_fence).activation(m.cv[:, j, 0:n_tok], ps[:, 0:n_tok], ACT.Identity, bias=b_conv[:, j:j + 1]))
        got["val", j] = [e]
        return [e]

    def ev_glu(j, ps, token):
        e = act.mark(act.after(token, *pre_fence).activation(m.cg[:, j, 0:n_tok], ps[:, 0:n_tok], ACT.Sigmoid, bias=b_conv[:, 4 + j:5 + j]))
        u = m.u[:, j, 0:len(streams), PAD:PAD + S]
        w = lambda b: b[:, j, 0:n_tok].rearrange("p (s t) -> p s t", t=S)
        e2 = pool.mark(pool.after(e, *toks(("val", j)), got["u_zero"]).tensor_tensor(u, w(m.cv), w(m.cg), ALU.mult))
        got["u", j] = [e2]
        return [e]

    def ev_cgate(j, ps, token):
        e = act.mark(act.after(token, *toks(("u", j))).activation(m.cg[:, j, 0:n_tok], ps[:, 0:n_tok], ACT.Silu, bias=b_conv[:, 8 + j:9 + j]))
        got["cg", j] = [e]
        return [e]

    def ev_kkv(t, ps, token):
        e = act.mark(act.after(token).activation(m.kkv[:, t, :], ps[:, :], ACT.Copy))
        got[KKV, t] = [e]
        return [e]

    def ev_gv(t, ps, token):
        e = act.mark(act.after(token, *m.set_up[1]).activation(m.gv[:, t, :], ps[:, :], ACT.Copy))
        got[GV, t] = [e]
        return [e]

    def ev_lrq(t, ps, token):
        w = 288 if t in tiles else 32
        e = act.mark(act.after(token).activation(m.lrq[:, t, 0:w], ps[:, 0:w], ACT.Copy))
        got[LRQ, t] = [e]
        return [e]

    def ev_aq(t, ps, token):
        e = act.mark(act.after(token, *got["conv_cut"]).activation(m.aq[:, t, :], ps[:, :], ACT.Copy))
        got[AQ, t] = [e]
        return [e]

    def ev_sigma(t, ps, token):
        e = act.mark(act.after(token, *got.get(("sigma_read", t), ())).activation(m.sigma[:, t, :], ps[:, :], ACT.Sigmoid))
        got["sigma", t] = [e]
        return [e]

    def ev_y(branch, c):
        def run(t, ps, token):
            out = m.acc[:, t, c * WC:(c + 1) * WC]
            if branch == 0:
                e = dve.mark(dve.after(token, *toks(("sigma", t)), *pre_fence).tensor_tensor(out, ps[:, :], m.sigma[:, t, :], ALU.mult))
                got["sigma_read", t] = [e]
                got["acc", t, c] = [e]
                return [e]
            e = dve.mark(dve.after(token, *toks(("sigma", t))).tensor_tensor(m.sigma[:, t, :], ps[:, :], m.sigma[:, t, :], ALU.mult))
            e2 = pool.mark(pool.after(e, *toks(("acc", t, c))).tensor_tensor(out, out, m.sigma[:, t, :], ALU.add))
            got["sigma_read", t] = [e2]
            got["acc", t, c] = [e2]
            return [e]
        return run

    def ev_gate(o, key):
        def run(t, ps, token):
            g, free, slot = m.gtmp.take()
            e = act.mark(act.after(token, *free).activation(g, ps[:, :], ACT.Silu))
            e2 = pool.mark(pool.after(e, *toks((key, t))).tensor_tensor(o[:, t, :], o[:, t, :], g, ALU.mult))
            m.gtmp.free(slot, e2)
            got["gated", t] = [e2]
            return [e]
        return run

    def cut_gated(o):
        for t in tiles:
            cols = slice(t * P, (t + 1) * P)
            yield from core.transpose_cut(o[:, t, :], range(CONV // P), m.yh[:, :, cols], m.yl[:, :, cols], got["gated", t], toks("y_read"))
            got["y", t] = core.last

    def along(steps, side, every):
        for n, step in enumerate(steps):
            yield step
            if (n + 1) % every == 0:
                next(side, None)
        for _ in side:
            pass

    def main():
        def inp(c, tt, ev, **kw):
            yield from core.project(xs, KD, tt, WIDTH2[c], ev, bias_of(c), **kw)
        def y_out(branch, c):
            yield from core.project((m.yh, m.yl, lambda t, kp: got["y", t]), CONV // P, tiles, WC, ev_y(branch, c))
            got["y_read"] = [core.done[-1]]
        for c in FIRST_CHUNKS[layer]:
            if c == KKV:
                yield lambda: all(t in hx for t in every), (1,)
                yield from inp(KKV, every, ev_kkv)
            else:
                yield from core.project_t((m.xh, m.xl, [x for t in tiles for x in hx[t]]), KD, n_tok, ev_val if c == VAL else ev_glu)
        yield from inp(LRQ, every, ev_lrq, width_of=lambda t: 288 if t in tiles else 32)
        yield from inp(GV, every, ev_gv)
        yield from core.project_t((m.xh, m.xl, [x for t in tiles for x in hx[t]]), KD, n_tok, ev_cgate)
        yield from inp(M0A, tiles, ev_sigma)
        yield lambda: "conv_cut" in got, (0, 1, 2)
        for t in tiles:
            got["y", t] = got["conv_cut"]
        yield from inp(AQ, tiles, ev_aq)
        yield from y_out(0, 0)
        yield from inp(M0B, tiles, ev_sigma)
        yield from y_out(0, 1)
        yield lambda: all(("gla_o", t) in got for t in tiles), (0, 1, 2)
        yield from inp(GG, tiles, ev_gate(m.gv, "gla_o"))
        yield from along(inp(M1A, tiles, ev_sigma), cut_gated(m.gv), 3)
        yield from y_out(1, 0)
        yield from inp(M1B, tiles, ev_sigma)
        yield from y_out(1, 1)
        yield lambda: all(("att_o", t) in got for t in tiles), (0, 1, 2)
        yield from inp(AG, tiles, ev_gate(m.aq, "att_o"))
        yield from along(inp(M2A, tiles, ev_sigma), cut_gated(m.aq), 3)
        yield from y_out(2, 0)
        yield from inp(M2B, tiles, ev_sigma)
        yield from y_out(2, 1)
        got["main_end"] = []

    n_st = len(streams)

    def conv():
        yield from need(*[("u", j) for j in range(4)])
        end = {}
        for k in range(TAPS):
            for j in range(4):
                src = m.u[:, j, 0:n_st, k:k + S]
                out = m.cv[:, j, 0:n_tok].rearrange("p (s t) -> p s t", t=S)
                if k == 0:
                    end[j] = dve.mark(dve.after(*toks(("u", j))).tensor_scalar(
                        out, src, taps[:, j, k:k + 1], dw_b[:, j:j + 1], ALU.mult, ALU.add))
                else:
                    end[j] = dve.mark(dve.after(end[j]).scalar_tensor_tensor(
                        out, src, taps[:, j, k:k + 1], out, ALU.mult, ALU.add))
                yield
        for _ in range(4 * SLACK[2]):
            yield
        ps, free, slot = core.aux.take()
        pe.after(*end.values(), *free)
        for j in range(4):
            ins = nc.tensor.matmul(ps[:, 0:n_tok], m.mean_w[:, :], m.cv[:, j, 0:n_tok], start=j == 0, stop=j == 3)
        mu = pe.mark(ins)
        yield
        sqs = []
        for j in range(4):
            d = dve.mark(dve.after(mu).tensor_tensor(m.cv[:, j, 0:n_tok], m.cv[:, j, 0:n_tok], ps[:, 0:n_tok], ALU.subtract))
            end[j] = d
            sqs.append(act.mark(act.after(d, *hx[2], *hx[3]).activation(m.u2[:, j, 0:n_tok], m.cv[:, j, 0:n_tok], ACT.Square)))
            yield
        core.aux.free(slot, d)
        ps, free, slot = core.aux.take()
        pe.after(*sqs, *free)
        for j in range(4):
            ins = nc.tensor.matmul(ps[:, 0:n_tok], m.mean_w[:, :], m.u2[:, j, 0:n_tok], start=j == 0, stop=j == 3)
        var = pe.mark(ins)
        ve = dve.mark(dve.after(var).tensor_scalar(ps[:, 0:n_tok], ps[:, 0:n_tok], EPS2, None, ALU.add))
        sd = act.mark(act.after(ve).activation(ps[:, 0:n_tok], ps[:, 0:n_tok], ACT.Sqrt))
        rs = dve.mark(dve.after(sd).reciprocal(ps[:, 0:n_tok], ps[:, 0:n_tok]))
        yield
        for j in range(4):
            w = m.cv[:, j, 0:n_tok]
            n = dve.mark(dve.after(rs, end[j]).tensor_tensor(w, w, ps[:, 0:n_tok], ALU.mult))
            end[j] = act.mark(act.after(n).activation(w, w, ACT.Silu, scale=cln_g[:, j:j + 1], bias=cln_b[:, j:j + 1]))
        core.aux.free(slot, n)
        m.open_y()
        yield from need(*[("cg", j) for j in range(4)])
        cut = []
        for j in range(4):
            w = m.cv[:, j, 0:n_tok]
            g = pool.mark(pool.after(end[j], *toks(("cg", j))).tensor_tensor(w, w, m.cg[:, j, 0:n_tok], ALU.mult))
            hi, lo = m.yh[:, j, 0:n_tok], m.yl[:, j, 0:n_tok]
            h = act.mark(act.after(g).activation(hi, w, ACT.Copy))
            l = dve.mark(dve.after(h).tensor_tensor(lo, w, hi.bitcast(F32), ALU.subtract))
            cut += [h, l]
            yield
        got["conv_cut"] = cut

    def gla():
        fence = pre_fence + hx[2] + hx[3]
        yield from need(*[(c, t) for c in (KKV, GV, LRQ) for t in every])
        zw = pool.mark(pool.after(*fence).memset(m.wup[:, :], 0.0))
        for d in range(2):
            small.start(8, m.wup[d * RANK:(d + 1) * RANK, d * QK2:(d + 1) * QK2], io["w_gate2"][layer, d], zw)
        wup_in = small.start(8, m.wup[2 * RANK:2 * RANK + 1, :], io["b_gate2"][layer:layer + 1, :], zw)
        one = dve.mark(dve.after(*fence).memset(m.lr_t[32:33, :], 1.0))
        za = pool.mark(pool.after(*fence).memset(m.att[:, :, :, :, :], 0.0))
        z0 = pool.mark(pool.after(*fence).memset(m.st[:, :, :, 0, :], 0.0))
        ps, free, slot = core.aux.take()
        pe.after(*toks(*[(LRQ, t) for t in every]), *free)
        for t in every:
            ins = nc.tensor.transpose(ps[0:32, t * P:(t + 1) * P], m.lrq[:, t, 0:32], m.ident[:, :])
        tr = pe.mark(ins)
        lr = act.mark(act.after(tr, *fence).activation(m.lr_t[0:32, :], ps[0:32, :], ACT.Copy))
        core.aux.free(slot, lr)
        yield
        state = {}
        last_state = None
        inter_read = []

        def gates(t):
            i = t % 2
            out = t in tiles
            ps, free, slot = core.aux.take()
            zt = pe.mark(pe.after(lr, one, wup_in, *free).matmul(ps[:, :], m.lr_t[0:33, t * P:(t + 1) * P], m.wup[0:33, :], start=True, stop=True))
            e = act.mark(act.after(zt, *fence, *state.get("tmp_read", ())).activation(m.e3[:, i, :], ps[:, :], ACT.Abs))
            e = act.mark(act.after(e).activation(m.e3[:, i, :], m.e3[:, i, :], ACT.Exp, scale=-1.0))
            e = act.mark(act.after(e).activation(m.e3[:, i, :], m.e3[:, i, :], ACT.Ln, bias=1.0))
            la = dve.mark(dve.after(e, *fence, *state.get("la_read", ())).scalar_tensor_tensor(
                m.la[:, :], ps[:, :], 0.0, m.e3[:, i, :], ALU.min, ALU.subtract))
            core.aux.free(slot, la)
            for _ in range(SLACK[0]):
                yield
            n = 1.0 / 16.0
            ps3, free3, slot3 = core.aux.take()
            pe.after(la, *free3)
            for dp in range(4):
                ins = nc.tensor.matmul(ps3[:, 2 * dp:2 * dp + 2], m.la[:, dp * P:(dp + 1) * P], m.halves[:, :], start=True, stop=True)
            tot = pe.mark(ins)
            dec = act.mark(act.after(tot, *state.get("dec_read", ())).activation(
                m.dec[:, :, 2 * i:2 * i + 2], ps3[:, 0:8].rearrange("p (a b) -> p a b", b=2), ACT.Exp, scale=n))
            core.aux.free(slot3, dec)
            state["dec"] = dec
            ps2, free2, slot2 = core.aux.take()
            pe.after(*free2)
            for d in range(2):
                ins = nc.tensor.matmul(ps2[:, d * QK2:(d + 1) * QK2], m.tri2[:, 2 + d, :], m.la[:, d * QK2:(d + 1) * QK2], start=True, stop=True)
            left = pe.mark(ins)
            state["la_read"] = [left]
            e3 = act.mark(act.after(left, la).activation(m.e3[:, i, :], ps2[:, :], ACT.Exp, scale=n))
            core.aux.free(slot2, e3)
            if out:
                ps1, free1, slot1 = core.aux.take()
                pe.after(*free1)
                for d in range(2):
                    ins = nc.tensor.matmul(ps1[:, d * QK2:(d + 1) * QK2], m.tri2[:, d, :], m.la[:, d * QK2:(d + 1) * QK2], start=True, stop=True)
                cum = pe.mark(ins)
                state["la_read"] = [cum]
                e1 = act.mark(act.after(cum, *state.get("tmp_read", ())).activation(m.e1[:, :], ps1[:, :], ACT.Exp, scale=n))
                e2 = act.mark(act.after().activation(m.e2[:, :], ps1[:, :], ACT.Exp, scale=-n))
                core.aux.free(slot1, e2)
            v = lambda b: b.rearrange("p (d n) -> p d n", d=2)
            k_b = spread(m.kkv[:, t, 0:QK2], [P, 2, QK2])
            ks = pool.mark(pool.after(e3, *toks((KKV, t))).tensor_tensor(v(m.e3[:, i, :]), v(m.e3[:, i, :]), k_b, ALU.mult))
            state["ks", t] = ks
            yield
            if out:
                q_b = spread(m.lrq[:, t, 32:32 + QK2], [P, 2, QK2])
                qi = dve.mark(dve.after(e1, *toks((LRQ, t))).scalar_tensor_tensor(v(m.e1[:, :]), q_b, GC ** -0.5, v(m.e1[:, :]), ALU.mult, ALU.mult))
                ki = pool.mark(pool.after(e2).tensor_tensor(v(m.e2[:, :]), v(m.e2[:, :]), k_b, ALU.mult))
                for _ in range(SLACK[1]):
                    yield
                ps, tok_q, slot = core.transpose([m.e1[:, dp * P:(dp + 1) * P] for dp in range(4)], [qi])
                view = ps[:, :].rearrange("p (a t) -> p a t", a=4)
                qt = act.mark(act.after(tok_q, *fence, *inter_read).activation(m.q_t[:, :, i, :], view, ACT.Copy))
                core.aux.free(slot, qt)
                ps, tok_k, slot = core.transpose([m.e2[:, dp * P:(dp + 1) * P] for dp in range(4)], [ki])
                kt = dve.mark(dve.after(tok_k, *fence, cum).tensor_copy(m.k_t[:, :], ps[:, :]))
                core.aux.free(slot, kt)
                state["tmp_read"] = [tok_q, tok_k]
                yield
                for par in range(2):
                    ps, free, slot = core.aux.take()
                    rows = slice(par * HD, (par + 1) * HD)
                    pe.after(qt, kt, *free)
                    for dp in range(4):
                        ins = nc.tensor.matmul(ps[:, dp * P:(dp + 1) * P], m.k_t[rows, dp * P:(dp + 1) * P],
                                               m.q_t[rows, dp, i, :], start=True, stop=True)
                    a = pe.mark(ins)
                    am = dve.mark(dve.after(a, za, *inter_read).copy_predicated(m.att[:, i, par, :, :], m.gmask[:, :, :],
                                                                     ps[:, :].rearrange("p (a t) -> p a t", a=4)))
                    core.aux.free(slot, am)
                    state["att", t, par] = am
                state["la_read"] = [a]
                yield

        for s in (1, 0):
            tl = C_TILES if s else X_TILES
            out = tl[0] in tiles
            for t in tl:
                yield from gates(t)
            upd = last_state or [z0]
            for step in range(4):
                psd = []
                for d in range(2):
                    c = step if d == 0 else 3 - step
                    i, half = c // 2, c % 2
                    rows = slice(half * GC, (half + 1) * GC)
                    ps, free, slot = core.aux.take()
                    pe.after(state["ks", tl[i]], *free, *toks((GV, tl[i])))
                    for h in range(HEADS2):
                        par, pair = h % 2, h // 2
                        ins = nc.tensor.matmul(ps[par * HD:(par + 1) * HD, pair * P:(pair + 1) * P],
                                               m.e3[rows, i, d * QK2 + h * HD:d * QK2 + (h + 1) * HD],
                                               m.gv[rows, tl[i], h * P:(h + 1) * P], start=True, stop=True)
                    con = pe.mark(ins)
                    ends = []
                    for pair in range(2):
                        ends.append(dve.mark(dve.after(con, *upd, *inter_read, state["dec"]).scalar_tensor_tensor(
                            m.st[:, d, pair, step + 1, :], m.st[:, d, pair, step, :],
                            m.dec[:, 2 * d + pair, c:c + 1], ps[:, pair * P:(pair + 1) * P], ALU.mult, ALU.add)))
                    core.aux.free(slot, ends[-1])
                    psd += ends
                upd = psd
                yield
            state["dec_read"] = upd
            state["tmp_read"] = state.get("tmp_read", []) + [con]
            if out:
                for t in tl:
                    i = t % 2
                    be, fe, se = core.aux.take()
                    bo, fo, so = core.sum_bank.take()
                    pe.after(*fe, *fo, *upd, state["att", t, 0], state["att", t, 1])
                    for h in range(HEADS2):
                        par, pair = h % 2, h // 2
                        bk = (be, bo)[par][:, pair * P:(pair + 1) * P]
                        rows = slice(par * HD, (par + 1) * HD)
                        v_h = m.gv[:, t, h * P:(h + 1) * P]
                        for d in range(2):
                            nc.tensor.matmul(bk, m.att[:, i, par, 2 * d + pair, :], v_h, start=d == 0, stop=False)
                        for d in range(2):
                            for half in range(2):
                                c = 2 * i + half
                                step = c if d == 0 else 3 - c
                                hs = slice(half * GC, (half + 1) * GC)
                                ins = nc.tensor.matmul(bk[hs, :], m.q_t[rows, 2 * d + pair, i, hs],
                                                       m.st[rows, d, pair, step, :], start=False, stop=d == 1)
                    token = pe.mark(ins)
                    inter_read = [token]
                    og = m.gv[:, t, :].rearrange("p (a b n) -> p a b n", a=2, b=2)
                    bv = lambda b: b[:, 0:256].rearrange("p (a n) -> p a n", a=2)
                    o1 = act.mark(act.after(token, *fence).activation(og[:, :, 0, :], bv(be), ACT.Copy))
                    o2 = dve.mark(dve.after(token, *fence).tensor_copy(og[:, :, 1, :], bv(bo)))
                    core.aux.free(se, o1)
                    core.sum_bank.free(so, o2)
                    yield
                    g, gf, gs = m.gtmp.take()
                    sq = pool.mark(pool.after(o1, o2, *gf).tensor_tensor(g, m.gv[:, t, :], m.gv[:, t, :], ALU.mult))
                    sm = dve.mark(dve.after(sq).tensor_reduce(m.gms[:, t, 0:4], g.rearrange("p (h n) -> p h n", h=4), AXX, ALU.add))
                    m.gtmp.free(gs, sm)
                    me = dve.mark(dve.after(sm).tensor_scalar(m.gms[:, t, 4:8], m.gms[:, t, 0:4], 1.0 / P, EPS2, ALU.mult, ALU.add))
                    iv = pool.mark(pool.after(me).tensor_tensor(m.gms[:, t, 0:4], m.gms[:, t, 4:8], m.half[:, 0:4], ALU.pow))
                    ov = m.gv[:, t, :].rearrange("p (h n) -> p h n", h=4)
                    n1 = pool.mark(pool.after(iv).tensor_tensor(ov, ov, spread(gla_g, [P, 4, P]), ALU.mult))
                    n2 = dve.mark(dve.after(n1).tensor_tensor(ov, ov, m.gms[:, t, 0:4].unsqueeze(2).to_broadcast([P, 4, P]), ALU.mult))
                    got["gla_o", t] = [n2]
                    yield
            if s == 1:
                cp = pool.mark(pool.after(*upd, *inter_read).tensor_copy(m.st[:, :, :, 0, :], m.st[:, :, :, 4, :]))
                last_state = [cp] + upd
                inter_read = inter_read + [cp]

    def norm_rope(src, heads, g, t, ready, roped):
        v = src.rearrange("p (h d) -> p h d", d=HD)
        n = heads * HD
        a, free, slot = m.gtmp.take()
        b, free_b, slot_b = m.gtmp.take()
        a, b = a[:, 0:n], b[:, 0:n]
        st = m.ams
        sq = pool.mark(pool.after(*ready, *free).tensor_tensor(a, src, src, ALU.mult))
        sm = dve.mark(dve.after(sq, *got.get("ams_read", ())).tensor_reduce(st[:, 0, 0:heads], a.rearrange("p (h d) -> p h d", d=HD), AXX, ALU.add))
        me = dve.mark(dve.after(sm).tensor_scalar(st[:, 1, 0:heads], st[:, 0, 0:heads], 1.0 / HD, EPS2, ALU.mult, ALU.add))
        iv = pool.mark(pool.after(me).tensor_tensor(st[:, 2, 0:heads], st[:, 1, 0:heads], m.half[:, 0:heads], ALU.pow))
        n1 = pool.mark(pool.after().tensor_tensor(v, v, spread(g, [P, heads, HD]), ALU.mult))
        n2 = dve.mark(dve.after(iv, n1).tensor_tensor(v, v, st[:, 2, 0:heads].unsqueeze(2).to_broadcast([P, heads, HD]), ALU.mult))
        got["ams_read"] = [n2]
        if not roped:
            m.gtmp.free(slot, sm)
            m.gtmp.free(slot_b, *free_b)
            return n2
        q = HD // 4
        w = lambda x: x.rearrange("p (h a b i) -> p h a b i", a=2, b=2, i=q)
        av = a.rearrange("p (h d) -> p h d", d=HD)
        one = dve.mark(dve.after(n2, sm, *free_b).tensor_tensor(av, v, spread(m.cos[:, t, :], [P, heads, HD]), ALU.mult))
        sn = m.sin[:, t, :].rearrange("p (a b i) -> p a b i", a=2, b=2)
        for x in range(2):
            for half in range(2):
                two = dve.mark(dve.after().tensor_tensor(
                    w(b)[:, :, x, half, :], w(src)[:, :, x, 1 - half, :], spread(sn[:, x, half, :], [P, heads, q]), ALU.mult))
        end = pool.mark(pool.after(two).tensor_tensor(src, a, b, ALU.add))
        m.gtmp.free(slot, end)
        m.gtmp.free(slot_b, end)
        return end

    k_end, q_end = {}, {}

    def att_heads():
        yield from need(*[(KKV, t) for t in every])
        for t in every:
            k_end[t] = norm_rope(m.kkv[:, t, QK2:QK2 + P], AKV, kn_g, t, toks((KKV, t)), t < 2)
            yield
        yield from need(*[(AQ, t) for t in tiles])
        for t in tiles:
            q_end[t] = norm_rope(m.aq[:, t, :], AH, qn_g, t, toks((AQ, t)), t < 2)
            yield
        got["heads"] = []

    def att():
        fence = core.fence()
        for e in (act, dve, pool):
            e.after(*fence)
        yield from need("heads")
        def pairs(src, tl, dst, scale, ready, odd):
            ps, free, slot = core.aux.take()
            pe.after(*ready, *free)
            for i, t in enumerate(tl):
                ins = nc.tensor.transpose(ps[:, i * P:(i + 1) * P], src(t), m.ident[:, :])
            token = pe.mark(ins)
            n = len(tl) * P
            if odd:
                e = act.mark(act.after(token).activation(dst[:, 0:n], ps[:, 0:n], ACT.Copy, scale=scale))
            else:
                e = dve.mark(dve.after(token).tensor_scalar(dst[:, 0:n], ps[:, 0:n], scale, None, ALU.mult))
            core.aux.free(slot, e)
            return e
        ready = [pairs(lambda t: m.kkv[:, t, QK2:QK2 + P], every, m.ak_t, 1.0, [k_end[t] for t in every], False)]
        yield
        for j in range(AH // 2):
            ready.append(pairs(lambda t: m.aq[:, t, j * P:(j + 1) * P], tiles, m.aq_t[:, j, :], HD ** -0.5, [q_end[t] for t in tiles], j % 2 == 0))
            yield
        by_pair = lambda x: x.rearrange("p (a b d) -> p a b d", b=2, d=HD)
        for qt in tiles:
            key_tiles = every if qt < 2 else C_TILES
            keys = len(key_tiles) * P
            k0 = key_tiles[0] * P
            n_maps = 512 // keys
            osum, ofree, oslot = core.sum_bank.take()
            stat, sfree, sslot = m.astat.take()
            top_of, sum_of, inv_of = (stat[:, i * AH:(i + 1) * AH] for i in range(3))
            st = {}

            def scores(j):
                ps, free, slot = core.aux.take()
                pe.after(*ready, *free)
                for i in range(n_maps):
                    h = j * n_maps + i
                    rows = slice(h // 4 * HD, (h // 4 + 1) * HD)
                    ins = nc.tensor.matmul(ps[:, i * keys:(i + 1) * keys], m.aq_t[rows, h % 4, qt * P:(qt + 1) * P],
                                           m.ak_t[rows, k0:k0 + keys], start=True, stop=True)
                st[j] = [ps, slot, pe.mark(ins)]

            def soft(j):
                ps, slot, token = st[j]
                h = j * n_maps
                view = ps[:, :].rearrange("p (a b) -> p a b", a=n_maps)
                top = dve.mark(dve.after(token, *sfree).tensor_reduce(top_of[:, h:h + n_maps], view, AXX, ALU.max, negate=True))
                pm, free, pslot = m.aprob.take()
                act.after(top, *free)
                for i in range(n_maps):
                    end = act.mark(nc.scalar.activation(pm[:, i * keys:(i + 1) * keys], ps[:, i * keys:(i + 1) * keys], ACT.Exp,
                                                        bias=top_of[:, h + i:h + i + 1], accum_out=sum_of[:, h + i:h + i + 1]))
                core.aux.free(slot, end)
                st["inv"] = dve.mark(dve.after(end).reciprocal(inv_of[:, h:h + n_maps], sum_of[:, h:h + n_maps]))
                st[j] = [pm, pslot, end]

            def flip(j):
                pm, pslot, end = st[j]
                ps, token, slot = core.transpose([pm[:, b * P:(b + 1) * P] for b in range(4)], [end])
                m.aprob.free(pslot, token)
                pt, pfree, ptslot = m.aprob_t.take()
                if j % 2:
                    end = act.mark(act.after(token, *pfree).activation(pt, ps[:, :], ACT.Copy))
                else:
                    end = dve.mark(dve.after(token, *pfree).tensor_copy(pt, ps[:, :]))
                core.aux.free(slot, end)
                st[j] = [pt, ptslot, end]

            def values(j):
                pt, ptslot, end = st[j]
                pe.after(end, *(ofree if j == 0 else ()))
                nb = len(key_tiles)
                for i in range(n_maps):
                    h = j * n_maps + i
                    kh, at = h // 4, (h % 4) * 2 + h // 4
                    for b, t in enumerate(key_tiles):
                        ins = nc.tensor.matmul(osum[:, at * HD:(at + 1) * HD], pt[:, (i * nb + b) * P:(i * nb + b + 1) * P],
                                               m.kkv[:, t, QK2 + P + kh * HD:QK2 + P + (kh + 1) * HD],
                                               start=b == 0, stop=b == nb - 1)
                st["sum"] = pe.mark(ins)
                m.aprob_t.free(ptslot, st["sum"])
            yield from pipeline(list(range(AH // n_maps)), [scores, soft, flip, values], LAGS2)
            end = dve.mark(dve.after(st["sum"], st["inv"]).tensor_tensor(
                by_pair(m.ao[:, qt, :]), by_pair(osum[:, :]),
                inv_of.rearrange("p (b a) -> p a b", b=2).unsqueeze(3).to_broadcast([P, AH // 2, 2, HD]), ALU.mult))
            m.astat.free(sslot, end)
            core.sum_bank.free(oslot, end)
            got["att_o", qt] = [end]
            yield

    with ExitStack() as scope:
        core.ctx, outer = scope, core.ctx
        base_rings = list(core.rings)

        def open_gla(ctx):
            core.ctx = ctx
            m.wup, m.lr_t = core.sb(f"w_up{layer}", [33, 512]), core.sb(f"low_t{layer}", [33, 512])
            m.att = core.sb(f"gla_att{layer}", [P, 2, 2, 4, P])
            m.st = core.sb(f"gla_state{layer}", [P, 2, 2, 5, P])
            m.la, m.e1, m.e2 = (core.sb(f"{n}{layer}", [P, 512]) for n in ("gla_la", "gla_e1", "gla_e2"))
            m.e3 = core.sb(f"gla_k_state{layer}", [P, 2, 512])
            m.q_t, m.k_t = core.sb(f"gla_q_t{layer}", [P, 4, 2, P]), m.la
            m.dec, m.gms = core.sb(f"gla_decay{layer}", [P, 4, 4]), core.sb(f"gla_ms{layer}", [P, 4, 8])
            core.ctx = outer

        def open_att(ctx):
            core.ctx = ctx
            m.aq_t, m.ak_t = core.sb(f"att_q_t{layer}", [P, AH // 2, 512]), core.sb(f"att_k_t{layer}", [P, 512])
            m.aprob, m.aprob_t = core.ring(f"att_p{layer}", 3, [P, 512]), core.ring(f"att_pt{layer}", 2, [P, 512])
            m.astat = core.ring(f"att_stat{layer}", 2, [P, 24])
            m.ao = m.aq
            core.ctx = outer

        right = ExitStack()
        m.u = right.enter_context(nc.sbuf_tensor(f"conv_u{layer}", [P, 4, 2, S + 2 * PAD], F32, side="right"))

        def open_y():
            right.close()
            m.yh, m.yl = (scope.enter_context(nc.sbuf_tensor(f"{n}{layer}", [P, 4, 2 * S], F32R, side="right"))
                          for n in ("y_hi", "y_lo"))
        m.open_y = open_y
        got["u_zero"] = pool.mark(pool.after(*pre_fence).memset(m.u[:, :, :, :], 0.0))

        def attentions():
            if layer > 0:
                yield from modulated_input(core, m, layer, C_TILES, hx)
            with ExitStack() as c:
                open_gla(c)
                yield from gla()
            with ExitStack() as c:
                open_att(c)
                yield from att()
                yield from need("main_end")
        weave(main(), [conv(), attentions(), att_heads()], lambda n: RATES2[layer][min(n // PHASE2, len(RATES2[layer]) - 1)])

    proj_done = core.done[-1]
    fence = core.fence()
    ready = {}

    def cut_merged(some):
        for t in some:
            cols = slice(t * P, (t + 1) * P)
            yield from core.transpose_cut(m.acc[:, t, :], range(KD), m.xh[:, :, cols], m.xl[:, :, cols],
                                          toks(("acc", t, 0), ("acc", t, 1)), (proj_done,))
            ready[t] = core.last
    for _ in cut_merged(X_TILES):
        pass
    merged_read = core.fence()
    dve.after(*merged_read)
    diag_scope = ExitStack()
    diag = diag_scope.enter_context(nc.sbuf_tensor(f"gate_diag{layer}", [P, 4, P], F32))
    gates, dread = [], {}
    for s in streams:
        for c in range(2):
            ps, free, slot = core.aux.take()
            for i in range(4):
                j = (s * 2 + c) * 4 + i
                buf = diag[:, j % 4, :]
                d = dve.mark(dve.after(dread.get(j - 4)).tensor_scalar(buf, m.ident[:, :], gate[:, 4 * c + i, s:s + 1], None, ALU.mult))
                token = pe.mark(pe.after(d, *free).matmul(ps[:, i * P:(i + 1) * P], m.ones[:, :], buf, start=True, stop=True))
                dread[j] = token
            e = act.mark(act.after(token, *merged_read).activation(m.acc[:, s, c * WC:(c + 1) * WC], ps[:, :], ACT.Copy))
            core.aux.free(slot, e)
            gates.append(e)
    diag_scope.close()
    core.x_ready, core.sigma_read, m.scope_free = {}, fence, core.fence()

    def add_gated(c, context=None):
        def run(t, ps, token):
            cs = slice(c * WC, (c + 1) * WC)
            g, free, slot = m.gtmp.take()
            dst = m.x[:, t, cs] if t in X_TILES else m.acc[:, t, cs]
            e = dve.mark(dve.after(token, *gates, *free).tensor_tensor(g, ps[:, :], m.acc[:, t // 2, cs], ALU.mult))
            e2 = pool.mark(pool.after(e, context).tensor_tensor(dst, dst, g, ALU.add))
            m.gtmp.free(slot, e2)
            core.x_ready.setdefault(t, []).append(e2)
            if not full:
                small.start(10, io["y"].rearrange("(t p) d -> p t d", p=P)[:, t, cs], dst, e2)
            return [e]
        return run

    def out(some, context=None):
        for c in range(2):
            yield from core.project((m.xh, m.xl, lambda t, kp: ready[t]), KD, some, WC, add_gated(c, context))

    def context_end():
        again = small.start(9, m.acc[:, 2:4, :], io["ctx2"].rearrange("(t p) d -> p t d", p=P), *ready[2], *ready[3])
        yield from out(C_TILES, again)
    weave(out(X_TILES), [cut_merged(C_TILES)] if full else [], lambda n: [BESIDE[1]])
    m.context_end = context_end()


def second_block(core, io, shared):
    from contextlib import ExitStack
    nc, small = core.nc, core.small
    with ExitStack() as ctx:
        core.ctx, outer = ctx, core.ctx
        m = Mem()
        m.ident, m.ones, m.half, m.x = shared.ident, shared.ones, shared.half, shared.x
        m.mod_cols = shared.mod_cols
        core.piece_slots("2", 4, 3)
        core.share_banks(4, 3)
        m.xh, m.xl = core.sb("x_hi2", [P, KD, 2 * S], F32R), core.sb("x_lo2", [P, KD, 2 * S], F32R)
        m.acc, m.sigma = core.sb("merged", [P, 4, D]), core.sb("sigma", [P, 4, WC])
        m.cv, m.u2 = (m.acc[:, i:i + 2, :].rearrange("p a (b t) -> p (a b) t", t=2 * S) for i in (0, 2))
        m.kkv, m.gv = core.sb("gla_k_att_kv", [P, 4, 512]), core.sb("gla_v", [P, 4, 512])
        m.lrq, m.aq = core.sb("low_gla_q", [P, 4, 288]), core.sb("att_q", [P, 4, 512])
        m.par, m.rows = core.sb("par2", [P, LAYERS, PAR_COLS]), core.sb("rows2", [P, LAYERS, 2 * P])
        m.bias, m.sel = core.sb("bias_parts", [96, LAYERS, WC], BF16), core.sb("bias_sel", [96, N_BIAS, P], BF16)
        m.cg, m.ams = m.aq, core.sb("att_ms", [P, 3, 8])
        m.scale = core.sb("scale", [P, LAYERS, KD, 2])
        m.cos, m.sin = core.sb("cos2", [P, NT, HD]), core.sb("sin2", [P, NT, HD])
        m.tri2, m.halves = core.sb("tri2", [P, 4, P]), core.sb("halves", [P, 2])
        m.gmask = core.sb("gla_mask", [P, 4, P], mybir.dt.uint32)
        m.mean_w = core.sb("mean_w", [P, P])
        m.gtmp = core.ring("gate_tmp", 2, [P, 512])
        temporary = ExitStack()
        part_of = temporary.enter_context(nc.sbuf_tensor("bias_part", [96, LAYERS, WC], BF16))
        small, act, dve, pool = core.small, core.act, core.dve, core.pool
        raw_of, rest_of = m.gv[0:96, 0:LAYERS, :], m.gv[0:96, LAYERS:2 * LAYERS, :]
        z = dve.mark(dve.after().memset(raw_of, 0.0))
        par_in = small.start(4, m.par[:, :, :], io["par2"].rearrange("l p n -> p l n"))
        for i in range(3):
            bias_in = small.start(5, raw_of[32 * i:32 * i + N_BIAS, :, :], io["bias2"].rearrange("l c n -> c l n"), z)
        m.ctx_in = small.start(7, m.acc[:, 2:4, :], io["ctx2"].rearrange("(t p) d -> p t d", p=P))
        for layer in range(LAYERS):
            stream_second(core, layer, io)
        core.load_ahead()
        sel_rows = m.acc[0:96, 0:2, :].rearrange("p a b -> p (a b)")[:, 0:N_BIAS * P]
        sel_in = small.start(6, sel_rows, io["bias_sel"])
        for name, place in (("cos2", m.cos[:, :, :]), ("sin2", m.sin[:, :, :]), ("tri2", m.tri2[:, :, :]),
                            ("halves", m.halves[:, :]), ("gla_mask", m.gmask[:, :, :])):
            m.consts_in = small.start(3, place, io[name])
        m.consts_in = small.start(3, m.rows[:, :, :].rearrange("p l n -> p (l n)"),
                                  io["rows2"].rearrange("l n -> (l n)").partition_broadcast(P))
        def bias_rows(e, l):
            raw, rest, part = raw_of[:, l, :], rest_of[:, l, :], part_of[:, l, :]
            bias = m.bias[:, l, :]
            end = e.mark(e.after(bias_in).tensor_copy(part, raw))
            end = e.mark(e.after(end).tensor_copy(bias[0:32, :], part[0:32]))
            end = e.mark(e.after(end).tensor_tensor(rest, raw, part, ALU.subtract))
            end = e.mark(e.after(end).tensor_copy(part, rest))
            end = e.mark(e.after(end).tensor_copy(bias[32:64, :], part[32:64]))
            end = e.mark(e.after(end).tensor_tensor(raw, rest, part, ALU.subtract))
            return e.mark(e.after(end).tensor_copy(bias[64:96, :], raw[64:96]))
        m.mod = m.mod_cols[:, :].rearrange("p (l a k s) -> p l a k s", l=LAYERS, a=3, k=KD)

        def set_up_first():
            for l in range(LAYERS):
                b_mod = m.par[:, l, PAR_COLS - 3 * KD:PAR_COLS].rearrange("p (a k) -> p a k", a=3)
                mb = dve.mark(dve.after(par_in).tensor_tensor(
                    m.mod[:, l], m.mod[:, l], b_mod.unsqueeze(3).to_broadcast([P, 3, KD, 2]), ALU.add))
                s1 = dve.mark(dve.after(mb).tensor_scalar(m.scale[:, l], m.mod[:, l, 1], 1.0, None, ALU.add))
                m.scale_ready = dve.mark(dve.after(s1).tensor_tensor(
                    m.scale[:, l], m.scale[:, l], m.par[:, l, 0:KD].unsqueeze(2).to_broadcast([P, KD, 2]), ALU.mult))
            m.set_up[0] = [bias_rows(dve, 0)]

        mean_w = pool.mark(pool.after().memset(m.mean_w[:, :], 1.0 / CONV))

        def set_up_rest():
            sel = act.mark(act.after(sel_in).activation(m.sel[:, :, :].rearrange("p a b -> p (a b)"), sel_rows, ACT.Copy))
            m.set_up[0] += [sel, mean_w]
            m.set_up[1] = [bias_rows(pool, 1)]
            pool.after(*m.set_up[1])
        m.set_up_first, m.set_up_rest, m.set_up = set_up_first, set_up_rest, {}
        core.x_ready, core.sigma_read, m.scope_free = {}, [], []
        for layer in range(LAYERS):
            second_layer(core, layer, io, m)
        temporary.close()
        core.sp.after((small.sems[10], small.counts[10]))
        core.ctx = outer


def shared_memory(core, io):
    m = Mem()
    m.ident, m.ones = core.sb("ident", [P, P]), core.sb("ones", [P, P])
    m.half = core.sb("minus_half", [P, 32])
    m.mod_cols = core.sb("mod_cols", [P, LAYERS * MOD_COLS])
    m.x = core.sb("x", [P, NT, D])
    core.ident = m.ident
    core.small.start(0, m.ident[:, :], io["ident"])
    got = core.small.start(0, m.x[:, :, :], io["x"].rearrange("(t p) d -> p t d", p=P))
    core.dve.mark(core.dve.after(got).memset(m.ones[:, :], 1.0))
    core.dve.mark(core.dve.after().memset(m.half[:, :], -0.5))
    return m


def program(nc, io):
    from contextlib import ExitStack
    with ExitStack() as ctx:
        core = Core(nc, ctx)
        core.loaded = []
        m = shared_memory(core, io)
        first_block(core, io, m)
        second_block(core, io, m)


def chunk_pieces(w, cols):
    k = w.shape[0] // P
    part = w[:, cols]
    n = part.shape[1]
    return part.reshape(k // KP, KP, P, n).transpose(0, 2, 1, 3).reshape(-1)


def columns(split, chunk):
    at, start = {}, 0
    for name, n in split:
        at[name] = start
        start += n
    return np.concatenate([np.arange(at[name] + first, at[name] + first + n) for name, first, n in chunk])


def rope_1():
    inv = np.float32(10000.0) ** (-np.arange(0, HD, 2, dtype=np.float32) / np.float32(HD))
    ang = np.arange(S, dtype=np.float32)[:, None] * inv[None, :]
    cos, sin = np.cos(ang), np.sin(ang)
    lay = lambda a: np.ascontiguousarray(a.reshape(NT, P, HD).transpose(1, 0, 2).astype(np.float32))
    return lay(np.concatenate([cos, cos], 1)), lay(np.concatenate([-sin, sin], 1))


def rope_2():
    rows, n_freq = S // 64, HD // 4
    pos_r = np.repeat(np.arange(rows, dtype=np.float32), 64)
    pos_c = np.tile(np.arange(64, dtype=np.float32), rows)
    freqs = np.float32(10000.0) ** (-np.arange(n_freq, dtype=np.float32) / np.float32(n_freq))
    ar, ac = pos_r[:, None] * freqs, pos_c[:, None] * freqs
    cos = np.concatenate([np.cos(ar), np.cos(ar), np.cos(ac), np.cos(ac)], 1)
    sin = np.concatenate([-np.sin(ar), np.sin(ar), -np.sin(ac), np.sin(ac)], 1)
    lay = lambda a: np.ascontiguousarray(a.reshape(NT, P, HD).transpose(1, 0, 2).astype(np.float32))
    return lay(cos), lay(sin)


def lay_out(inp):
    a = {}
    f = lambda n: np.asarray(inp[n])
    a["x"] = f("x").reshape(S, D)
    w, wo = f("w_in"), f("w_out")
    cols = [columns(SPLIT1, c) for c in CHUNKS1]
    a["w1"] = np.stack([np.concatenate([chunk_pieces(w[l], c) for c in cols]) for l in range(LAYERS)])
    a["wo1"] = np.stack([np.concatenate([chunk_pieces(wo[l], slice(c * WC, (c + 1) * WC)) for c in range(2)])
                         for l in range(LAYERS)])
    a["small1"] = np.concatenate([f("b_f"), f("lam_q1"), f("lam_k1"), f("lam_q2"), f("lam_k2"),
                                  f("g_subln"), f("ln_g"), f("ln_b")], axis=1)
    a["cos1"], a["sin1"] = rope_1()
    w, wm, bi = f("w_in_2"), f("w_mod_2"), f("b_in_2")
    cols = [columns(SPLIT2, c) for c in CHUNKS2]
    per = lambda fn: np.stack([fn(l) for l in range(LAYERS)])
    halves = lambda mat, n: np.concatenate([chunk_pieces(mat, slice(c * WC, (c + 1) * WC)) for c in range(n)])
    a["w2"] = per(lambda l: np.concatenate([chunk_pieces(w[l], c) for c in cols]))
    a["wm2"] = per(lambda l: halves(wm[l], 6))
    a["wo2"] = per(lambda l: halves(f("w_out_2")[l], 2))
    for n, key in (("conv", "w_conv_out_2"), ("gla", "w_gla_out_2")):
        a["wy_" + n] = per(lambda l: halves(f(key)[l], 2))
    rows = np.concatenate([np.arange(h * HD, (h + 1) * HD) for h in PAIRED])
    a["wy_att"] = per(lambda l: halves(f("w_attn_out_2")[l][rows], 2))
    col = lambda v: v.reshape(-1, P).T
    dw = f("conv_dw_w_2")
    a["par2"] = per(lambda l: np.concatenate(
        [col(f("norm_g_2")[l]), col(bi[l][cols[0]]), col(bi[l][cols[1]]), col(bi[l][cols[2]]),
         dw[l].T.reshape(4, P, TAPS).transpose(1, 0, 2).reshape(P, 4 * TAPS),
         col(f("conv_dw_b_2")[l]), col(f("conv_ln_g_2")[l]), col(f("conv_ln_b_2")[l]),
         col(f("b_mod_2")[l])], axis=1))
    a["rows2"] = np.concatenate([f("gla_norm_g_2"), f("q_norm_g_2"), f("k_norm_g_2")], axis=1)
    a["bias2"] = np.zeros((LAYERS, N_BIAS, WC), np.float32)
    for l in range(LAYERS):
        for c in range(N_BIAS):
            a["bias2"][l, c, :WIDTH2[c + 3]] = bi[l][cols[c + 3]]
    a["w_gate2"], a["b_gate2"] = f("gla_w_gate_2"), f("gla_b_gate_2").reshape(LAYERS, 2 * QK2)
    a["c2"] = np.stack([f("c_2").reshape(KD, P).T, f("c_ctx_2").reshape(KD, P).T], axis=2)
    a["ctx2"] = f("ctx_2").reshape(S, D)
    a["cos2"], a["sin2"] = rope_2()
    i = np.arange(P)
    t_from, t_to = i[:, None], i[None, :]
    same = t_from // GC == t_to // GC
    a["tri2"] = np.stack([same & (t_from <= t_to), same & (t_from >= t_to),
                          same & (t_from > t_to), same & (t_from < t_to)], axis=1).astype(np.float32)
    a["halves"] = np.stack([i < GC, i >= GC], axis=1).astype(np.float32)
    a["gla_mask"] = np.stack([same & (t_from <= t_to)] * 2 + [same & (t_from >= t_to)] * 2, axis=1).astype(np.uint32)
    sel = np.zeros((96, N_BIAS, P), np.float32)
    for c in range(N_BIAS):
        sel[[c, 32 + c, 64 + c], c, :] = 1.0
    a["bias_sel"] = sel.reshape(96, N_BIAS * P)
    i = np.arange(P)
    a["ident"] = np.eye(P, dtype=np.float32)
    a["causal"] = np.where(i[:, None] >= i[None, :], 0, NEG).astype(np.float32)
    a["tri"] = (i[:, None] <= i[None, :]).astype(np.float32)
    li = [0.8 - 0.6 * np.exp(-0.3 * l) for l in range(LAYERS)]
    a["lam_consts"] = np.tile(np.array([v for x in li for v in (x, 1.0 - x)], np.float32), (P, 1))
    a["sel4"] = np.array([[1, 0], [0, 1], [1, 0], [0, 1]], np.float32)
    return a


def kernel(**inputs):
    import concourse.bacc as bacc
    from concourse.bass_utils import run_bass_kernel_spmd

    arrays = {n: np.ascontiguousarray(v) for n, v in lay_out(inputs).items()}
    nc = bacc.Bacc("TRN2", target_bir_lowering=False, num_devices=1)
    io = {n: nc.dram_tensor("in_" + n, v.shape, mybir.dt.from_np(v.dtype), kind="ExternalInput").ap()
          for n, v in arrays.items()}
    io["y"] = nc.dram_tensor("out_y", (S, D), F32, kind="ExternalOutput").ap()
    program(nc, io)
    r = run_bass_kernel_spmd(nc, [{"in_" + n: v for n, v in arrays.items()}], core_ids=[0])
    return r.results[0]["out_y"].reshape(1, S, D)
```
